# Optimizing a Trainium2 kernel written in Bass

```python
import math
import jax
import jax.numpy as jnp
from jax import lax
import numpy as np

D_MODEL = 1024
BATCH = 1
SEQ = 512
DEPTH = 2

CHUNK = 64
RMS_EPS = 1e-6
S5_WIDTH = 512
S5_GROUP_CH = 16
S5_GROUPS = S5_WIDTH // S5_GROUP_CH
S5_STATE = 64
ML_HEADS = 4
ML_HEAD_DIM = 128
ML_WIDTH = ML_HEADS * ML_HEAD_DIM
ML_CONV = 4
AB_IN = S5_WIDTH + 3 * ML_WIDTH
AB_OUT = S5_WIDTH + ML_WIDTH
SWA_Q_HEADS = 16
SWA_KV_HEADS = 2
SWA_GROUP = SWA_Q_HEADS // SWA_KV_HEADS
SWA_HEAD_DIM = 64
SWA_WINDOW = 128
SWA_WIN_CHUNKS = SWA_WINDOW // CHUNK
SWA_QKV = (SWA_Q_HEADS + 2 * SWA_KV_HEADS) * SWA_HEAD_DIM
N_REL_BUCKETS = 32
REL_MAX_DIST = 128
D_FF = 2816
FFN_CONV = 3
N_EVEN = (DEPTH + 1) // 2
N_ODD = DEPTH // 2

kernel_name = 'hybrid_s5_mlstm_swa_convffn'

def rmsnorm(x, g):
    xf = x.astype(jnp.float32)
    y = xf * lax.rsqrt(jnp.mean(xf * xf, axis=-1, keepdims=True) + RMS_EPS)
    return (y * g.astype(jnp.float32)).astype(x.dtype)

def causal_dwconv(x, w, b):
    width = w.shape[0]
    seq = x.shape[1]
    xp = jnp.pad(x, ((0, 0), (width - 1, 0), (0, 0)))
    return sum(xp[:, j:j + seq] * w[j] for j in range(width)) + b

def _linear_recurrence_combine(earlier, later):
    a_e, x_e = earlier
    a_l, x_l = later
    return a_l * a_e, a_l * x_e + x_l

def s5_group(u, log_dt, a_re, a_im, b_re, b_im, c_re, c_im, d_skip, w_glu):
    bsz, seq, _ = u.shape
    f32 = jnp.float32
    uf = u.astype(f32).reshape(bsz, seq, S5_GROUPS, S5_GROUP_CH)
    lam = lax.complex(jnp.minimum(a_re.astype(f32), -1e-4), a_im.astype(f32))
    dt = jnp.exp(log_dt.astype(f32))[:, None]
    a_bar = jnp.exp(lam * dt)
    b_bar = ((a_bar - 1.0) / lam)[..., None] * lax.complex(b_re.astype(f32), b_im.astype(f32))
    bu = lax.complex(jnp.einsum('blgc,gpc->blgp', uf, b_bar.real),
                     jnp.einsum('blgc,gpc->blgp', uf, b_bar.imag))
    a_seq = jnp.broadcast_to(a_bar, bu.shape)
    _, states = lax.associative_scan(_linear_recurrence_combine, (a_seq, bu), axis=1)
    y = (jnp.einsum('blgp,gcp->blgc', states.real, c_re.astype(f32))
         - jnp.einsum('blgp,gcp->blgc', states.imag, c_im.astype(f32)))
    y = y.reshape(bsz, seq, S5_WIDTH) + d_skip.astype(f32) * u.astype(f32)
    g = jax.nn.gelu(y)
    return (g * jax.nn.sigmoid(g @ w_glu.astype(f32))).astype(u.dtype)

def mlstm_chunkwise(q, k, v, i_pre, f_pre):
    bsz, seq, nh, dh = q.shape
    nc = seq // CHUNK

    def to_chunks(t):
        t = t.astype(jnp.float32).reshape((bsz, nc, CHUNK, nh) + t.shape[3:])
        return jnp.moveaxis(t, 3, 1)

    q, v = to_chunks(q), to_chunks(v)
    k = to_chunks(k) * dh ** -0.5
    log_f = jax.nn.log_sigmoid(to_chunks(f_pre))
    log_i = to_chunks(i_pre)
    b = jnp.cumsum(log_f, axis=-1)
    g = b[..., -1]
    w_end = g[..., None] - b + log_i
    m_loc = w_end.max(-1)
    e_end = jnp.exp(w_end - m_loc[..., None])
    c_loc = jnp.einsum('bhcsk,bhcsv->bhckv', e_end[..., None] * k, v)
    n_loc = jnp.einsum('bhcs,bhcsk->bhck', e_end, k)

    def step(carry, inp):
        c_st, n_st, m_st = carry
        c_l, n_l, m_l, g_c = inp
        m_new = jnp.maximum(g_c + m_st, m_l)
        a_old = jnp.exp(g_c + m_st - m_new)
        a_loc = jnp.exp(m_l - m_new)
        c_new = a_old[..., None, None] * c_st + a_loc[..., None, None] * c_l
        n_new = a_old[..., None] * n_st + a_loc[..., None] * n_l
        return (c_new, n_new, m_new), (c_st, n_st, m_st)

    init = (jnp.zeros((bsz, nh, dh, dh), jnp.float32),
            jnp.zeros((bsz, nh, dh), jnp.float32),
            jnp.zeros((bsz, nh), jnp.float32))
    xs = (jnp.moveaxis(c_loc, 2, 0), jnp.moveaxis(n_loc, 2, 0),
          jnp.moveaxis(m_loc, 2, 0), jnp.moveaxis(g, 2, 0))
    _, (c_prev, n_prev, m_prev) = lax.scan(step, init, xs)
    c_prev = jnp.moveaxis(c_prev, 0, 2)
    n_prev = jnp.moveaxis(n_prev, 0, 2)
    m_prev = jnp.moveaxis(m_prev, 0, 2)

    causal = jnp.tril(jnp.ones((CHUNK, CHUNK), dtype=bool))
    d_log = jnp.where(causal, b[..., :, None] - b[..., None, :] + log_i[..., None, :], -jnp.inf)
    inter_log = b + m_prev[..., None]
    m_t = jnp.maximum(inter_log, d_log.max(-1))
    w_intra = jnp.exp(d_log - m_t[..., None]) * jnp.einsum('bhctd,bhcsd->bhcts', q, k)
    a_inter = jnp.exp(inter_log - m_t)
    num = (jnp.einsum('bhcts,bhcsv->bhctv', w_intra, v)
           + a_inter[..., None] * jnp.einsum('bhctk,bhckv->bhctv', q, c_prev))
    den = w_intra.sum(-1) + a_inter * jnp.einsum('bhctk,bhck->bhct', q, n_prev)
    h = num / jnp.maximum(jnp.abs(den), jnp.exp(-m_t))[..., None]
    return jnp.moveaxis(h, 1, 3).reshape(bsz, seq, nh, dh)

def s5_mlstm_mixer(xn, w_in, s5_log_dt, s5_a_re, s5_a_im, s5_b_re, s5_b_im, s5_c_re, s5_c_im,
                   s5_d, s5_w_glu, ml_conv_w, ml_conv_b, ml_w_q, ml_w_k, ml_w_gates, ml_b_gates,
                   ml_norm_g, w_out):
    bsz, seq, _ = xn.shape
    proj = xn @ w_in
    u, xm, v, o_pre = jnp.split(proj, [S5_WIDTH, S5_WIDTH + ML_WIDTH, S5_WIDTH + 2 * ML_WIDTH], axis=-1)
    y_a = s5_group(u, s5_log_dt, s5_a_re, s5_a_im, s5_b_re, s5_b_im, s5_c_re, s5_c_im, s5_d, s5_w_glu)
    xc = jax.nn.silu(causal_dwconv(xm, ml_conv_w, ml_conv_b)).reshape(bsz, seq, ML_HEADS, ML_HEAD_DIM)
    q = jnp.einsum('bshd,hde->bshe', xc, ml_w_q)
    k = jnp.einsum('bshd,hde->bshe', xc, ml_w_k)
    vh = v.reshape(bsz, seq, ML_HEADS, ML_HEAD_DIM)
    qkv = jnp.concatenate([q, k, vh], axis=-1).reshape(bsz, seq, 3 * ML_WIDTH)
    gates = qkv @ ml_w_gates + ml_b_gates
    h_t = mlstm_chunkwise(q, k, vh, gates[..., :ML_HEADS], gates[..., ML_HEADS:])
    h_t = rmsnorm(h_t, ml_norm_g.reshape(ML_HEADS, ML_HEAD_DIM)).reshape(bsz, seq, ML_WIDTH)
    y_b = jax.nn.sigmoid(o_pre) * h_t.astype(xn.dtype)
    return jnp.concatenate([y_a, y_b], axis=-1) @ w_out

def t5_bucket(rel):
    nb = N_REL_BUCKETS // 2
    max_exact = nb // 2
    n = np.abs(rel)
    scaled = np.log(np.maximum(n, 1) / max_exact) / np.log(REL_MAX_DIST / max_exact) * (nb - max_exact)
    large = np.minimum(max_exact + scaled.astype(np.int32), nb - 1)
    return (rel > 0).astype(np.int32) * nb + np.where(n < max_exact, n, large)

def band_rel_bias(rel_bias):
    q_pos = np.arange(CHUNK)[:, None]
    k_pos = np.arange(SWA_WIN_CHUNKS * CHUNK)[None, :] - (SWA_WIN_CHUNKS - 1) * CHUNK
    bucket = t5_bucket(k_pos - q_pos)
    bias = rel_bias.astype(jnp.float32)[jnp.asarray(bucket, dtype=jnp.int32)]
    return jnp.transpose(bias, (2, 0, 1)).reshape(SWA_KV_HEADS, SWA_GROUP, CHUNK, SWA_WIN_CHUNKS * CHUNK)

def banded(t, n_chunks):
    bsz, seq = t.shape[:2]
    tp = jnp.pad(t, ((0, 0), ((SWA_WIN_CHUNKS - 1) * CHUNK, 0), (0, 0), (0, 0)))
    blocks = [tp[:, j * CHUNK:j * CHUNK + seq].reshape((bsz, n_chunks, CHUNK) + t.shape[2:])
              for j in range(SWA_WIN_CHUNKS)]
    return jnp.concatenate(blocks, axis=2)

def swa_sink_attention(xn, w_qkv, b_qkv, sinks, w_o, bias_band):
    bsz, seq, _ = xn.shape
    nc = seq // CHUNK
    nq = SWA_Q_HEADS * SWA_HEAD_DIM
    nkv = SWA_KV_HEADS * SWA_HEAD_DIM
    qkv = xn @ w_qkv + b_qkv
    q = qkv[..., :nq].reshape(bsz, nc, CHUNK, SWA_KV_HEADS, SWA_GROUP, SWA_HEAD_DIM)
    k = qkv[..., nq:nq + nkv].reshape(bsz, seq, SWA_KV_HEADS, SWA_HEAD_DIM)
    v = qkv[..., nq + nkv:].reshape(bsz, seq, SWA_KV_HEADS, SWA_HEAD_DIM)
    kb, vb = banded(k, nc), banded(v, nc)
    s = jnp.einsum('bcqkgd,bcjkd->bckgqj', q, kb).astype(jnp.float32) * SWA_HEAD_DIM ** -0.5 + bias_band
    key_chunk = (jnp.arange(nc)[:, None]
                 + jnp.repeat(jnp.arange(SWA_WIN_CHUNKS) - (SWA_WIN_CHUNKS - 1), CHUNK)[None, :])
    s = jnp.where((key_chunk >= 0)[None, :, None, None, None, :], s, -jnp.inf)
    sink = jnp.broadcast_to(sinks.astype(jnp.float32).reshape(SWA_KV_HEADS, SWA_GROUP, 1, 1),
                            s.shape[:-1] + (1,))
    p = jax.nn.softmax(jnp.concatenate([s, sink], axis=-1), axis=-1)[..., :-1]
    o = jnp.einsum('bckgqj,bcjkd->bcqkgd', p.astype(vb.dtype), vb).reshape(bsz, seq, nq)
    return o @ w_o

def conv_gated_mlp(xn, w_up, conv_w, conv_b, w_down):
    gate, val = jnp.split(xn @ w_up, 2, axis=-1)
    return (jax.nn.silu(causal_dwconv(gate, conv_w, conv_b)) * val) @ w_down

def setup_inputs(seed: int = 0) -> dict:
    key = jax.random.key(seed)
    ks = iter(jax.random.split(key, 40))

    def nrm(shape, scale):
        return scale * jax.random.normal(next(ks), shape, jnp.float32)

    d = D_MODEL
    ne, no = N_EVEN, N_ODD
    x = nrm((BATCH, SEQ, d), 1.0)
    rel_bias = nrm((N_REL_BUCKETS, SWA_Q_HEADS), 0.5)
    norm_mix_g = 1.0 + nrm((DEPTH, d), 0.02)
    norm_ffn_g = 1.0 + nrm((DEPTH, d), 0.02)
    norm_final_g = 1.0 + nrm((d,), 0.02)
    ffn_w_up = nrm((DEPTH, d, 2 * D_FF), d ** -0.5)
    ffn_conv_w = nrm((DEPTH, FFN_CONV, D_FF), FFN_CONV ** -0.5)
    ffn_conv_b = nrm((DEPTH, D_FF), 0.01)
    ffn_w_down = nrm((DEPTH, D_FF, d), D_FF ** -0.5)
    ab_w_in = nrm((ne, d, AB_IN), d ** -0.5)
    s5_log_dt = jax.random.uniform(next(ks), (ne, S5_GROUPS), jnp.float32,
                                   minval=math.log(1e-3), maxval=math.log(1e-1))
    s5_a_re = -0.5 + nrm((ne, S5_GROUPS, S5_STATE), 0.01)
    s5_a_im = math.pi * jnp.arange(S5_STATE, dtype=jnp.float32) + nrm((ne, S5_GROUPS, S5_STATE), 0.01)
    s5_b_re = nrm((ne, S5_GROUPS, S5_STATE, S5_GROUP_CH), (2 * S5_GROUP_CH) ** -0.5)
    s5_b_im = nrm((ne, S5_GROUPS, S5_STATE, S5_GROUP_CH), (2 * S5_GROUP_CH) ** -0.5)
    s5_c_re = nrm((ne, S5_GROUPS, S5_GROUP_CH, S5_STATE), S5_STATE ** -0.5)
    s5_c_im = nrm((ne, S5_GROUPS, S5_GROUP_CH, S5_STATE), S5_STATE ** -0.5)
    s5_d = nrm((ne, S5_WIDTH), 1.0)
    s5_w_glu = nrm((ne, S5_WIDTH, S5_WIDTH), S5_WIDTH ** -0.5)
    ml_conv_w = nrm((ne, ML_CONV, ML_WIDTH), ML_CONV ** -0.5)
    ml_conv_b = nrm((ne, ML_WIDTH), 0.01)
    ml_w_q = nrm((ne, ML_HEADS, ML_HEAD_DIM, ML_HEAD_DIM), ML_HEAD_DIM ** -0.5)
    ml_w_k = nrm((ne, ML_HEADS, ML_HEAD_DIM, ML_HEAD_DIM), ML_HEAD_DIM ** -0.5)
    ml_w_gates = nrm((ne, 3 * ML_WIDTH, 2 * ML_HEADS), (3 * ML_WIDTH) ** -0.5)
    ml_b_gates = jnp.concatenate(
        [nrm((ne, ML_HEADS), 0.1),
         jnp.linspace(3.0, 6.0, ML_HEADS, dtype=jnp.float32) + nrm((ne, ML_HEADS), 0.01)], axis=-1)
    ml_norm_g = 1.0 + nrm((ne, ML_WIDTH), 0.02)
    ab_w_out = nrm((ne, AB_OUT, d), AB_OUT ** -0.5)
    swa_w_qkv = nrm((no, d, SWA_QKV), d ** -0.5)
    swa_b_qkv = nrm((no, SWA_QKV), 0.01)
    swa_sinks = nrm((no, SWA_Q_HEADS), 0.5)
    swa_w_o = nrm((no, SWA_Q_HEADS * SWA_HEAD_DIM, d), (SWA_Q_HEADS * SWA_HEAD_DIM) ** -0.5)
    return {
        'x': x, 'rel_bias': rel_bias, 'norm_mix_g': norm_mix_g, 'norm_ffn_g': norm_ffn_g,
        'norm_final_g': norm_final_g, 'ffn_w_up': ffn_w_up, 'ffn_conv_w': ffn_conv_w,
        'ffn_conv_b': ffn_conv_b, 'ffn_w_down': ffn_w_down, 'ab_w_in': ab_w_in,
        's5_log_dt': s5_log_dt, 's5_a_re': s5_a_re, 's5_a_im': s5_a_im, 's5_b_re': s5_b_re,
        's5_b_im': s5_b_im, 's5_c_re': s5_c_re, 's5_c_im': s5_c_im, 's5_d': s5_d,
        's5_w_glu': s5_w_glu, 'ml_conv_w': ml_conv_w, 'ml_conv_b': ml_conv_b, 'ml_w_q': ml_w_q,
        'ml_w_k': ml_w_k, 'ml_w_gates': ml_w_gates, 'ml_b_gates': ml_b_gates,
        'ml_norm_g': ml_norm_g, 'ab_w_out': ab_w_out, 'swa_w_qkv': swa_w_qkv,
        'swa_b_qkv': swa_b_qkv, 'swa_sinks': swa_sinks, 'swa_w_o': swa_w_o,
    }

def reference(x, rel_bias, norm_mix_g, norm_ffn_g, norm_final_g, ffn_w_up, ffn_conv_w, ffn_conv_b,
              ffn_w_down, ab_w_in, s5_log_dt, s5_a_re, s5_a_im, s5_b_re, s5_b_im, s5_c_re, s5_c_im,
              s5_d, s5_w_glu, ml_conv_w, ml_conv_b, ml_w_q, ml_w_k, ml_w_gates, ml_b_gates,
              ml_norm_g, ab_w_out, swa_w_qkv, swa_b_qkv, swa_sinks, swa_w_o):
    bias_band = band_rel_bias(rel_bias)
    h = x
    for layer in range(DEPTH):
        xn = rmsnorm(h, norm_mix_g[layer])
        j = layer // 2
        if layer % 2 == 0:
            mix = s5_mlstm_mixer(xn, ab_w_in[j], s5_log_dt[j], s5_a_re[j], s5_a_im[j], s5_b_re[j],
                                 s5_b_im[j], s5_c_re[j], s5_c_im[j], s5_d[j], s5_w_glu[j],
                                 ml_conv_w[j], ml_conv_b[j], ml_w_q[j], ml_w_k[j], ml_w_gates[j],
                                 ml_b_gates[j], ml_norm_g[j], ab_w_out[j])
        else:
            mix = swa_sink_attention(xn, swa_w_qkv[j], swa_b_qkv[j], swa_sinks[j], swa_w_o[j], bias_band)
        h = h + mix.astype(h.dtype)
        ffn = conv_gated_mlp(rmsnorm(h, norm_ffn_g[layer]), ffn_w_up[layer], ffn_conv_w[layer],
                             ffn_conv_b[layer], ffn_w_down[layer])
        h = h + ffn.astype(h.dtype)
    return rmsnorm(h, norm_final_g)


_drawn_inputs = setup_inputs


def setup_inputs(seed=0):
    import zlib

    import numpy as np

    out = dict(_drawn_inputs(seed))
    spreads = {}
    factors = {'norm_mix_g': 2.891,
     'norm_ffn_g': 2.967,
     'norm_final_g': 2.869,
     'ffn_conv_b': 8.0,
     's5_log_dt': 2.699,
     's5_a_re': 8.0,
     's5_a_im': 2.681,
     's5_b_re': 3.685,
     's5_b_im': 3.765,
     's5_c_re': 3.755,
     's5_c_im': 3.779,
     'ml_conv_b': 7.679,
     'ml_norm_g': 6.692,
     'swa_b_qkv': 6.356,
     'swa_sinks': 8.0}
    for name, (base, spread) in spreads.items():
        noise = np.random.default_rng([zlib.crc32(name.encode()), seed]).standard_normal(out[name].shape)
        drawn = base * np.exp(spread * noise) if base else spread * noise
        out[name] = jnp.asarray(drawn.astype(out[name].dtype))
    for name, factor in factors.items():
        out[name] = (out[name] * factor).astype(out[name].dtype)
    return out
```

```python
from contextlib import ExitStack

import numpy as np

import concourse.bass as bass
from concourse import mybir

P = 128
SEQ = 512
DM = 1024
KB = DM // P
D_FF = 2816
FJ = D_FF // P
HEADS = 4
SB = SEQ // P
GROUPS, GCH, STATE = 32, 16, 64
PAIRS = GROUPS // 2
CH = P // GCH
NCH = SEQ // CH
SUP = 8
QH, AHD, WIN = 16, 64, 64
NC = SEQ // WIN
EPS = 1e-6
EXPM_LOG = 10

T_IN, T_QK, T_GLU, T_OUT = 0, 16, 17, 19
T_UP = [27, 114]
T_DN = [T_UP[0] + 2 * FJ, T_UP[1] + 2 * FJ]
T_QKV = T_DN[0] + 3 * KB
NQKV = 11
T_WO = T_QKV + NQKV
T_END = T_DN[1] + 3 * KB
assert T_WO + KB == T_UP[1] and T_END % 2 == 0
O_IN, O_QK, O_GLU, O_OUT = 0, 16, 24, 28
O_UP = [36, 107]
O_DN = [O_UP[0] + 2 * FJ, O_UP[1] + 2 * FJ]
O_QKV = O_DN[0] + KB
O_WO = O_QKV + NQKV
assert O_WO + KB == O_UP[1]
RAWS, RING = 2, 4

COLS = {}


def _col(name, n):
    COLS[name] = (sum(w for _, w in COLS.values()), n)


for _n, _w in (("g_mix0", KB), ("g_ffn0", KB), ("g_mix1", KB), ("g_ffn1", KB), ("g_fin", KB),
               ("fw0", 4 * FJ), ("fw1", 4 * FJ), ("mlw", 4 * HEADS), ("mlb", HEADS), ("mlg", HEADS),
               ("bqkv", NQKV), ("sink", QH // 2), ("bgate", 1), ("ddiag", GROUPS),
               ("ldt", PAIRS), ("are", PAIRS), ("aim", PAIRS), ("wg", 12 * 8)):
    _col(_n, _w)
NCOL = sum(w for _, w in COLS.values())


def used_count(t):
    return t + 1 if t < T_QK else t + 1 - 3


class Steps:

    def __init__(self, sem):
        self.sem, self.n, self.i, self.per = sem, 0, None, 0

    def up(self, ins):
        ins.then_inc(self.sem, 1)
        self.n += 1

    def value(self):
        return self.n if self.i is None else self.i * self.per + self.n

    def enter(self, i, per):
        self.i, self.per, self.base = i, per, self.n

    def leave(self, iters):
        assert self.n - self.base == self.per, (self.n - self.base, self.per)
        self.i, self.n = None, self.base + self.per * iters


def build(nc, wstream, xT, params, bc, consts, band, outT, u_scratch, y_scratch):
    f32, f32r = mybir.dt.float32, mybir.dt.float32r
    ACT, ALU, AX = mybir.ActivationFunctionType, mybir.AluOpType, mybir.AxisListType
    ctx = ExitStack()

    def sem(name):
        return ctx.enter_context(nc.semaphore(name))

    top = [nc.sbuf_base + (-nc.sbuf_base) % 64]

    def at(name, shape, offset, dt=f32):
        return nc.alloc_sbuf_tensor_at(name, shape, dt, offset=offset)

    def size(shape):
        return (int(np.prod(shape[1:])) * 4 + 63) // 64 * 64

    def sb(name, shape, dt=f32):
        o = top[0]
        top[0] += size(shape)
        return at(name, shape, o, dt)

    raw = sb("raw", [P, RAWS, 8 * P])
    whi = sb("whi", [P, RING, 8 * P], f32r)
    wlo = sb("wlo", [P, RING, 8 * P], f32r)
    xn_at = top[0]
    xhi = sb("xhi", [P, KB, SEQ], f32r)
    xlo = sb("xlo", [P, KB, SEQ], f32r)
    con = sb("con", [P, 2, P])
    ident, tri = con[:, 0, :], con[:, 1, :]
    ones = sb("ones", [P, P])
    mean_w = sb("mean_w", [P, P])
    rstd = sb("rstd", [P, SEQ])
    sq = sb("sq", [P, 2, SEQ])
    ssum_at = top[0]
    ssum = sb("ssum", [P, SEQ])
    prm = sb("prm", [P, NCOL + 1])

    def col(name, j=0, parts=P):
        o = COLS[name][0] + j
        return prm[0:parts, o:o + 1]

    def cols(name, parts=P):
        o, n = COLS[name]
        return prm[0:parts, o:o + n]

    base = top[0]
    end = nc.sbuf_usable_end

    def plan(*items, start=base):
        o, out = start, []
        for name, shape, dt in items:
            out.append(at(name, shape, o, dt))
            o += size(shape)
        assert o <= end, (items[0][0], o - end)
        return out

    h_at = end - size([P, KB, SEQ]) - (end - size([P, KB, SEQ])) % 64
    h = at("h", [P, KB, SEQ], h_at)
    ahi, alo, gpad, cbuf, sbuf, vbuf, abuf = plan(
        ("ahi", [P, FJ, SEQ], f32r), ("alo", [P, FJ, SEQ], f32r), ("gpad", [P, 2 + SEQ], f32),
        ("cbuf", [P, SEQ], f32), ("sbuf", [P, SEQ], f32), ("vbuf", [P, SEQ], f32), ("abuf", [P, SEQ], f32))
    assert base + 2 * size([P, FJ, SEQ]) + 5 * 2112 <= h_at
    F2 = [P, PAIRS, P]
    (fre, fim, gre, gim, m1re, m1im, uc, uperm, xchi, xclo, sigo, xs, ksb) = plan(
        ("fre", F2, f32), ("fim", F2, f32), ("gre", F2, f32), ("gim", F2, f32),
        ("m1re", F2, f32), ("m1im", F2, f32), ("uc", [P, GROUPS, NCH], f32), ("uperm", [P, 4, SEQ], f32),
        ("xchi", [P, 4, SEQ], f32r), ("xclo", [P, 4, SEQ], f32r), ("sigo", [P, 4, SEQ], f32),
        ("xs", [P, 2, PAIRS, NCH + 1], f32), ("ksb", [P, GCH, GROUPS], f32))
    o0 = base + 6 * size(F2) + 3 * 8192
    toep = at("toep", [P, CH, GCH, GROUPS], base + 2 * size(F2))
    xin = at("xin", [P, KB, SEQ], base + 4 * size(F2))
    qT = at("qT", [P, HEADS, SEQ], base + 4 * size(F2))
    kT = at("kT", [P, HEADS, SEQ], base + 5 * size(F2))
    vT = at("vT", [P, HEADS, SEQ], base + 6 * size(F2) + 8192)
    vtok = at("vtok", [P, HEADS, SB, P], base + 6 * size(F2) + 16384)
    yaf = at("yaf", [P, 4, SEQ], base + 6 * size(F2) + 16384)
    ysb = at("ysb", [P, GROUPS, NCH], base + 6 * size(F2) + 24576)
    gsig = at("gsig", [P, 4, SEQ], base + 6 * size(F2) + 24576)
    tail = base + 6 * size(F2) + 6 * 8192 + size([P, 2, PAIRS, NCH + 1]) + 2048
    nmb, emb, ebuf, wbuf, hb, h2 = plan(
        ("nmb", [P, SEQ], f32), ("emb", [P, SEQ], f32), ("ebuf", [P, 2, SEQ], f32),
        ("wbuf", [P, 2, SEQ], f32), ("hb", [P, SEQ], f32), ("h2", [P, SEQ], f32), start=tail)
    bcp, xpad, cacc, xcf, ptmp, sm = plan(
        ("bcp", [P, 4, PAIRS * GCH], f32), ("xpad", [P, 3 + SEQ], f32), ("cacc", [P, SEQ], f32),
        ("xcf", [P, SEQ], f32), ("ptmp", [P, 4, 256], f32), ("sm", [P, 40, PAIRS], f32), start=tail)
    s5x_at = tail + 4096 + 2112 + 4096 + 4096 + 2560
    q_re, q_im = plan(("q_re", [P, SUP, PAIRS], f32), ("q_im", [P, SUP, PAIRS], f32),
                      start=s5x_at)
    keep_at = s5x_at + 1024
    acol, = plan(("acol", [P, SB, HEADS], f32), start=keep_at)
    qk2, aj2 = plan(("qk2", [P, 2 * PAIRS, SUP], f32), ("aj2", [P, 2 * PAIRS, SUP], f32), start=ssum_at)
    st1 = at("st1", [P, 2 * PAIRS, 64], xn_at)
    st2 = at("st2", [P, 2 * PAIRS, 64], xn_at + 4 * 4 * SEQ * 2)
    g8 = at("g8", [8, SEQ], xn_at + 6 * 2048)
    lf = at("lf", [HEADS, SEQ], xn_at + 7 * 2048)
    fcum = at("fcum", [HEADS, SEQ], xn_at + 14 * 2048)
    arow = at("arow", [HEADS, SEQ], xn_at + 15 * 2048)
    nmrow = at("nmrow", [HEADS, 2, SEQ], ssum_at - 4096)
    (aq, akd, avT, vwin, bandsb, sbuf2, pbuf, ptb, obuf, st) = plan(
        ("aq", [P, 8, SEQ], f32), ("akd", [P, 2, WIN + SEQ], f32), ("avT", [P, WIN + SEQ], f32),
        ("vwin", [P, NC, P], f32), ("bandsb", [P, 8, P], f32), ("sbuf2", [P, 2, SEQ], f32),
        ("pbuf", [P, 2, SEQ], f32), ("ptb", [P, 2, SEQ], f32), ("obuf", [P, 8, SEQ], f32), ("st", [P, 2, 8, 4], f32))
    assert base + 16384 + 2 * 2304 + 2304 + 4096 + 4096 + 12288 + 16384 + 256 <= h_at
    outb = at("outb", [P, KB, SEQ], base)

    bank = [ctx.enter_context(nc.psum_tensor(f"bank{b}", [P, SEQ], f32)) for b in range(8)]

    raw_in = [sem(f"raw_in{s}") for s in range(RAWS)]
    hi_done, lo_done = sem("hi_done"), sem("lo_done")
    tile_used = sem("tile_used")
    out_freed = sem("out_freed")
    params_in, x_in, band_in = sem("params_in"), sem("x_in"), sem("band_in")
    consts_set = sem("consts_set")
    pads_set = sem("pads_set")
    sq_done, acc_done = sem("sq_done"), sem("acc_done")
    sum_clear = sem("sum_clear")
    mean_done, rstd_done, rms_done = sem("mean_done"), sem("rstd_done"), sem("rms_done")
    h_done = sem("h_done")
    xhi_done, xlo_done = sem("xhi_done"), sem("xlo_done")
    dve_step, act_step, pool_step = sem("dve_step"), sem("act_step"), sem("pool_step")
    conv_done, silu_done, a_done, ahi_done, alo_done = (sem(n) for n in (
        "conv_done", "silu_done", "a_done", "ahi_done", "alo_done"))
    u_saved, u_back = sem("u_saved"), sem("u_back")
    s5_recip, prep_done = sem("s5_recip"), sem("prep_done")
    ybhi_done, oahi_done, oalo_done = sem("ybhi_done"), sem("oahi_done"), sem("oalo_done")
    yahi_done = sem("yahi_done")
    mconv_done, xcf_done, xchi_done, xclo_done = (sem(n) for n in ("mconv_done", "xcf_done", "xchi_done", "xclo_done"))
    o_scaled, sigo_done = sem("o_scaled"), sem("sigo_done")
    dt_done, g_built, f_built, lam_sq = sem("dt_done"), sem("g_built"), sem("f_built"), sem("lam_sq")
    k_ready, k_copied, k_final, toep_clear, toep_built = (sem(n) for n in (
        "k_ready", "k_copied", "k_final", "toep_clear", "toep_built"))
    m1_ready, m1_copied = sem("m1_ready"), sem("m1_copied")
    s5in_ready, s5in_copied, scan_done = sem("s5in_ready"), sem("s5in_copied"), sem("scan_done")
    qk_ready, qk_copied, gates_ready, gates_copied, fsel_ready = (sem(n) for n in (
        "qk_ready", "qk_copied", "gates_ready", "gates_copied", "fsel_ready"))
    absf_done, expf_done, lnf_done, rows_done, sum_rows, emrow_done = (sem(n) for n in (
        "absf_done", "expf_done", "lnf_done", "rows_done", "sum_rows", "emrow_done"))
    acol_ready, acol_copied, vtok_ready, vtok_copied = (sem(n) for n in (
        "acol_ready", "acol_copied", "vtok_ready", "vtok_copied"))
    nmb_ready, nmb_copied, emb_ready, emb_copied = (sem(n) for n in (
        "nmb_ready", "nmb_copied", "emb_ready", "emb_copied"))
    earg_done, e_done, sc_ready, w_done, w_used = (sem(n) for n in (
        "earg_done", "e_done", "sc_ready", "w_done", "w_used"))
    hh_done, hsq_done, hms_ready, hms_read, yb_done = (sem(n) for n in (
        "hh_done", "hsq_done", "hms_ready", "hms_read", "yb_done"))
    y_ready, y_copied, y_saved, y_back, gelu_done = (sem(n) for n in (
        "y_ready", "y_copied", "y_saved", "y_back", "gelu_done"))
    gahi_done, galo_done, glu_ready, glusig_done, ya_done = (sem(n) for n in (
        "gahi_done", "galo_done", "glu_ready", "glusig_done", "ya_done"))
    x_back, den_abs = sem("x_back"), sem("den_abs")
    qkv_done, vwin_ready, vwin_copied = sem("qkv_done"), sem("vwin_ready"), sem("vwin_copied")
    asc_ready, asc_done, aexp_done, anorm_done, apt_ready, apt_copied, ao_ready, ao_copied = (sem(n) for n in (
        "asc_ready", "asc_done", "aexp_done", "anorm_done", "apt_ready", "apt_copied", "ao_ready", "ao_copied"))
    out_done, out_saved = sem("out_done"), sem("out_saved")

    block = ctx.enter_context(nc.Block())

    def wait_tile_used(eng, t):
        if isinstance(t, tuple):
            eng.wait_ge(tile_used, t[1] * t[2] + used_count(t[0]))
        elif t == T_QK:
            eng.wait_ge(qk_ready, 8)
        elif t in (T_GLU, T_GLU + 1):
            eng.wait_ge(glu_ready, 2 * (t - T_GLU + 1))
        else:
            eng.wait_ge(tile_used, used_count(t))

    @block.sync
    def _(sp):
        pairs_of = wstream.rearrange("(r s) p f -> r s p f", s=RAWS)
        sp.dma_start(con[:, :, :], consts).then_inc(params_in, 16)
        sp.dma_start(prm[:, 0:NCOL], params).then_inc(params_in, 16)
        for k in range(4):
            sp.dma_start(xin[:, 2 * k:2 * k + 2, :], xT[:, 2 * k:2 * k + 2, :]).then_inc(x_in, 16)
        sp.dma_start(bcp[:, :, :], bc).then_inc(params_in, 16)
        for t in range(RAWS):
            sp.dma_start(raw[:, t, :], wstream[t]).then_inc(raw_in[t], 16)

        def load(t, s, need):
            sp.wait_ge(lo_done, need)
            sp.dma_start(raw[:, s, :], wstream[t]).then_inc(raw_in[s], 16)

        def loads(t0, t1):
            with sp.Fori(t0 // 2, t1 // 2) as r:
                need0, need1 = sp.snap(r * 2 - 1), sp.snap(r * 2)
                sp.wait_ge(lo_done, need0)
                sp.dma_start(raw[:, 0, :], pairs_of[r, 0]).then_inc(raw_in[0], 16)
                sp.wait_ge(lo_done, need1)
                sp.dma_start(raw[:, 1, :], pairs_of[r, 1]).then_inc(raw_in[1], 16)

        loads(2, 10)
        sp.wait_ge(out_freed, 4)
        sp.dma_start(u_scratch.rearrange("m p s c -> p m (s c)"), uperm[:, :, :]).then_inc(u_saved, 16)
        sp.wait_ge(u_saved, 16)
        for s in range(CH):
            src = u_scratch.rearrange("m (g i) s c -> i (m g) s c", i=GCH)[:, :, CH - 1 - s, :]
            sp.dma_start(uc[s * GCH:(s + 1) * GCH, :, :], src).then_inc(u_back, 16)
        loads(10, T_QK)
        load(T_QK, 0, T_QK - 1)
        for t in range(T_QK + 1, T_OUT + 3):
            load(t, t % RAWS, t - 1)
        sp.wait_ge(k_final, 1)
        sp.wait_ge(toep_clear, 1)
        for t in range(CH):
            sp.dma_start(toep[(CH - 1 - t) * GCH:P, t, :, :],
                         ksb[0:(t + 1) * GCH, :, :]).then_inc(toep_built, 16)
        load(T_OUT + 3, 0, T_OUT + 2)
        sp.wait_ge(y_copied, 4)
        sp.dma_start(y_scratch.rearrange("s i g c -> (s i) (g c)"),
                     ysb[:, :, :].rearrange("p g c -> p (g c)")).then_inc(y_saved, 16)
        sp.wait_ge(y_saved, 16)
        for m in range(4):
            for g in range(8):
                src = y_scratch.rearrange("s i g c -> i g s c")[:, 8 * m + g, :, :]
                dst = uperm[g * GCH:(g + 1) * GCH, m, :].rearrange("p (s c) -> p s c", s=CH)
                sp.dma_start(dst, src).then_inc(y_back, 16)
        sp.wait_ge(yb_done, HEADS)
        sp.wait_ge(galo_done, 4)
        sp.dma_start(h[:, :, :], xT).then_inc(x_back, 16)
        load(T_OUT + 4, 1, T_OUT + 3)
        loads(T_OUT + 5, T_QKV + 3)
        sp.wait_ge(tile_used, used_count(T_DN[0] + 3 * KB - 1))
        sp.dma_start(bandsb[:, :, :], band).then_inc(band_in, 16)
        loads(T_QKV + 3, T_END)
        for m in range(KB):
            sp.wait_ge(out_done, m + 1)
            sp.dma_start(outT[:, m, :], outb[:, m, :]).then_inc(out_saved, 16)
        sp.wait_ge(out_saved, 16 * KB)

    @block.gpsimd
    def _(pool):
        steps = Steps(pool_step)
        G = nc.gpsimd

        def do(ins):
            steps.up(ins)

        def settle():
            pool.wait_ge(pool_step, steps.value())

        G.memset(ones[:, :], 1.0)
        G.memset(prm[:, NCOL:NCOL + 1], EPS)
        G.memset(mean_w[:, :], 1.0 / DM).then_inc(consts_set, 1)
        G.memset(xpad[:, 0:3], 0.0)
        G.memset(xs[:, :, :, 0:1], 0.0).then_inc(pads_set, 1)

        def sum_squares(first):
            for m in range(KB):
                add_square(KB * first + m, m)

        def add_square(n, m):
            pool.wait_ge(sq_done, n + 1)
            if m == 0:
                if n:
                    pool.wait_ge(mean_done, n // KB)
                G.tensor_copy(ssum[:, :], sq[:, m % 2, :]).then_inc(acc_done, 1)
            else:
                pool.wait_ge(acc_done, n)
                G.tensor_tensor(ssum[:, :], ssum[:, :], sq[:, m % 2, :], ALU.add).then_inc(acc_done, 1)

        sum_squares(0)

        pool.wait_ge(params_in, 48)
        S = [sm[:, j, :] for j in range(40)]
        lr, zr, zi, wr, wi, pr, pi, mr, mi, den, cr, ci = S[:12]
        T = S[12:16]
        li = cols("aim")

        def tt(o, a, b, op):
            do(G.tensor_tensor(o, a, b, op))

        def ts(o, a, s1, op0, s2=None, op1=ALU.bypass):
            if s2 is None:
                do(G.tensor_scalar(o, a, s1, None, op0))
            else:
                do(G.tensor_scalar(o, a, s1, s2, op0, op1))

        def cmul(orr, oi, ar, ai, br, bi, t):
            tt(t[0], ar, br, ALU.mult)
            tt(t[1], ai, bi, ALU.mult)
            tt(t[2], ar, bi, ALU.mult)
            tt(t[3], ai, br, ALU.mult)
            settle()
            tt(orr, t[0], t[1], ALU.subtract)
            tt(oi, t[2], t[3], ALU.add)
            settle()

        ts(lr, cols("are"), -1e-4, ALU.min)
        pool.wait_ge(dt_done, 1)
        settle()
        dt = S[39]
        tt(zr, lr, dt, ALU.mult)
        tt(zi, li, dt, ALU.mult)
        settle()
        ts(wr, zr, 2.0 ** -EXPM_LOG, ALU.mult)
        ts(wi, zi, 2.0 ** -EXPM_LOG, ALU.mult)
        settle()
        ts(pr, wr, 1.0 / 6, ALU.mult, 1.0, ALU.add)
        ts(pi, wi, 1.0 / 6, ALU.mult)
        settle()
        for n in (5, 4, 3, 2):
            cmul(cr, ci, wr, wi, pr, pi, T)
            ts(pr, cr, 1.0 / n, ALU.mult, 1.0, ALU.add)
            ts(pi, ci, 1.0 / n, ALU.mult)
            settle()
        cmul(mr, mi, wr, wi, pr, pi, T)
        for _ in range(EXPM_LOG):
            ts(cr, mr, 2.0, ALU.add)
            settle()
            cmul(pr, pi, mr, mi, cr, mi, T)
            ts(mr, pr, 1.0, ALU.mult)
            ts(mi, pi, 1.0, ALU.mult)
            settle()
        tt(T[0], lr, lr, ALU.mult)
        tt(T[1], li, li, ALU.mult)
        ts(wi, li, -1.0, ALU.mult)
        settle()
        G.tensor_tensor(den, T[0], T[1], ALU.add).then_inc(lam_sq, 1)
        pool.wait_ge(lam_sq, 1)
        cmul(cr, ci, mr, mi, lr, wi, T)
        pool.wait_ge(s5_recip, 1)
        tt(pr, cr, den, ALU.mult)
        tt(pi, ci, den, ALU.mult)
        ts(q_re[:, 0, :], mr, 1.0, ALU.add)
        ts(q_im[:, 0, :], mi, 1.0, ALU.mult)
        settle()

        def bro(ap, n):
            return ap.unsqueeze(1).to_broadcast([P, n, PAIRS])

        Tp = [ptmp[:, j, 0:4 * PAIRS].rearrange("p (a b) -> p a b", b=PAIRS) for j in range(4)]
        for n in (1, 2, 4):
            cmul(q_re[:, n:2 * n, :], q_im[:, n:2 * n, :], q_re[:, 0:n, :], q_im[:, 0:n, :],
                 bro(q_re[:, n - 1, :], n), bro(q_im[:, n - 1, :], n), [t[:, 0:n, :] for t in Tp])

        T3 = [ptmp[:, j, :].rearrange("p (a b) -> p a b", b=GCH) for j in range(4)]
        B = [bcp[:, j, :].rearrange("p (a b) -> p a b", b=GCH) for j in range(4)]

        def wide(ap):
            return ap.unsqueeze(2).to_broadcast([P, PAIRS, GCH])

        def step_view(tensor, s):
            return tensor[:, :, s * GCH:(s + 1) * GCH]

        cmul(step_view(gre, 0), step_view(gim, 0), B[0], B[1], wide(pr), wide(pi), T3)
        for s in range(1, CH):
            cmul(step_view(gre, s), step_view(gim, s), step_view(gre, 0), step_view(gim, 0),
                 wide(q_re[:, s - 1, :]), wide(q_im[:, s - 1, :]), T3)
        tt(T3[0], B[3], B[3], ALU.add)
        settle()
        G.tensor_tensor(B[3], B[3], T3[0], ALU.subtract).then_inc(g_built, 1)
        pool.wait_ge(g_built, 1)
        for s in range(CH):
            pw, pv = wide(q_re[:, s, :]), wide(q_im[:, s, :])
            tt(T3[0], B[2], pw, ALU.mult)
            tt(T3[1], B[3], pv, ALU.mult)
            tt(T3[2], B[3], pw, ALU.mult)
            tt(T3[3], B[2], pv, ALU.mult)
            settle()
            tt(step_view(fre, s), T3[0], T3[1], ALU.add)
            tt(step_view(fim, s), T3[2], T3[3], ALU.subtract)
            settle()
        pool.wait_ge(mean_done, 1)
        r2 = qk2[:, :, :].rearrange("p (r j) k -> p r j k", r=2)
        i2 = aj2[:, :, :].rearrange("p (r j) k -> p r j k", r=2)
        Ts = [ptmp[:, j, 0:4 * PAIRS].rearrange("p (b a) -> p b a", b=PAIRS) for j in range(4)]
        ts(r2[:, 0, :, 0], q_re[:, 7, :], 1.0, ALU.mult)
        ts(i2[:, 1, :, 0], q_im[:, 7, :], 1.0, ALU.mult)
        settle()
        for n in (1, 2, 4):
            bb = [x.to_broadcast([P, PAIRS, n]) for x in (r2[:, 0, :, n - 1:n], i2[:, 1, :, n - 1:n])]
            cmul(r2[:, 0, :, n:2 * n], i2[:, 1, :, n:2 * n], r2[:, 0, :, 0:n], i2[:, 1, :, 0:n],
                 bb[0], bb[1], [t[:, :, 0:n] for t in Ts])
        ts(r2[:, 1, :, :], r2[:, 0, :, :], 1.0, ALU.mult)
        G.tensor_scalar(i2[:, 0, :, :], i2[:, 1, :, :], -1.0, None, ALU.mult).then_inc(prep_done, 1)
        pool.wait_ge(prep_done, 1)
        settle()
        pool.wait_ge(s5in_copied, 2)
        X = [xs[:, r, :, 1:NCH + 1].rearrange("p j (s i) -> p j s i", i=SUP) for r in range(2)]
        XX = xs[:, :, :, 1:NCH + 1].rearrange("p r j (s i) -> p (r j) s i", i=SUP)

        def axpy(dst, co, prev, a, b, shape):
            tt(a, co[0].to_broadcast(shape), prev[0], ALU.mult)
            half = [shape[0], PAIRS] + list(shape[2:])
            tt(b[:, 0:PAIRS], co[1][:, 0:PAIRS].to_broadcast(half), prev[1][1], ALU.mult)
            tt(b[:, PAIRS:], co[1][:, PAIRS:].to_broadcast(half), prev[1][0], ALU.mult)
            settle()
            tt(a, a, b, ALU.add)
            settle()
            tt(dst, dst, a, ALU.add)
            settle()

        a8, b8 = st1[:, :, 0:SUP], st2[:, :, 0:SUP]
        for i in range(1, SUP):
            axpy(XX[:, :, :, i], (qk2[:, :, 0:1], aj2[:, :, 0:1]),
                 (XX[:, :, :, i - 1], (X[0][:, :, :, i - 1], X[1][:, :, :, i - 1])), a8, b8,
                 [P, 2 * PAIRS, SUP])
        a1, b1 = st1[:, :, 0:1], st2[:, :, 0:1]
        for s in range(1, SUP):
            axpy(XX[:, :, s, SUP - 1:SUP], (qk2[:, :, SUP - 1:SUP], aj2[:, :, SUP - 1:SUP]),
                 (XX[:, :, s - 1, SUP - 1:SUP], (X[0][:, :, s - 1, SUP - 1:SUP], X[1][:, :, s - 1, SUP - 1:SUP])),
                 a1, b1, [P, 2 * PAIRS, 1])
        a7, b7 = st1[:, :, 0:SUP - 1], st2[:, :, 0:SUP - 1]
        for i in range(SUP - 1):
            axpy(XX[:, :, 1:, i], (qk2[:, :, i:i + 1], aj2[:, :, i:i + 1]),
                 (XX[:, :, 0:SUP - 1, SUP - 1], (X[0][:, :, 0:SUP - 1, SUP - 1], X[1][:, :, 0:SUP - 1, SUP - 1])),
                 a7, b7, [P, 2 * PAIRS, SUP - 1])
        G.memset(xs[:, 0, :, 0:1], 0.0).then_inc(scan_done, 1)

        sum_squares(1)
        for n in (2, 3, 4):
            sum_squares(n)


    @block.scalar
    def _(act):
        steps = Steps(act_step)
        A = nc.scalar.activation

        def split_hi(t, i=0, per=0):
            act.wait_ge(raw_in[t % RAWS], i * (8 * per) + 16 * (t // RAWS + 1))
            if t >= RING:
                wait_tile_used(act, (t - RING, i, per) if per else t - RING)
            A(whi[:, t % RING, :], raw[:, t % RAWS, :], ACT.Copy).then_inc(hi_done, 1)

        def square(src, n, slot, i=0, per=0):
            if n >= 2:
                act.wait_ge(acc_done, i * per + n - 1)
            A(sq[:, slot, :], src, ACT.Square).then_inc(sq_done, 1)

        def root_mean_square(n):
            act.wait_ge(mean_done, n + 1)
            if n:
                act.wait_ge(out_freed, (0, O_IN + 16, O_DN[0], O_WO, O_DN[1])[n])
            A(rstd[:, :], bank[7][:, :], ACT.Sqrt, bias=prm[:, NCOL:NCOL + 1]).then_inc(rms_done, 1)

        def operand_hi(src, g):
            for m in range(KB):
                A(xhi[:, m, :], src[:, m, :], ACT.Copy, scale=col(g, m)).then_inc(xhi_done, 1)

        act.wait_ge(params_in, 48)
        A(sm[:, 39, :], cols("ldt"), ACT.Exp).then_inc(dt_done, 1)
        act.wait_ge(x_in, 64)
        operand_hi(xin, "g_mix0")
        for t in range(RING):
            split_hi(t)
        for m in range(KB):
            square(xin[:, m, :], m, m % 2)
        act.wait_ge(consts_set, 1)
        root_mean_square(0)

        for t in range(16):
            split_hi(t + RING) if t + RING <= T_OUT else None
            if 4 <= t < 8:
                m = t - 4
                act.wait_ge(mconv_done, m + 1)
                if m:
                    act.wait_ge(xclo_done, m)
                A(xcf[:, :], cacc[:, :], ACT.Silu).then_inc(xcf_done, 1)
                act.wait_ge(xcf_done, m + 1)
                A(xchi[:, m, :], xcf[:, :], ACT.Copy).then_inc(xchi_done, 1)
            if t >= 12:
                m = t - 12
                act.wait_ge(out_freed, t + 1)
                A(sigo[:, m, :], sigo[:, m, :], ACT.Sigmoid).then_inc(sigo_done, 1)
        for b in range(8):
            act.wait_ge(m1_ready, b + 1)
            dst = (m1re if b < 4 else m1im)[:, 4 * (b % 4):4 * (b % 4) + 4, :]
            A(dst, bank[5 + b % 2][:, :].rearrange("p (j q) -> p j q", q=P), ACT.Copy).then_inc(m1_copied, 1)
        for r in range(2):
            act.wait_ge(s5in_ready, r + 1)
            for k in range(2):
                ins = A(xs[:, r, 8 * k:8 * k + 8, 1:NCH + 1],
                        bank[4 + 2 * r + k][:, :].rearrange("p (j c) -> p j c", c=NCH), ACT.Copy)
            ins.then_inc(s5in_copied, 1)
        split_hi(T_QK + RING)
        for hd in range(HEADS):
            act.wait_ge(vtok_ready, hd + 1)
            A(vtok[:, hd, :, :], bank[6 + hd % 2][:, :].rearrange("p (s v) -> p s v", v=P),
              ACT.Copy).then_inc(vtok_copied, 1)
        act.wait_ge(fsel_ready, 1)
        A(lf[:, :], bank[5][0:HEADS, :], ACT.Abs).then_inc(absf_done, 1)
        act.wait_ge(absf_done, 1)
        A(lf[:, :], lf[:, :], ACT.Exp, scale=-1.0).then_inc(expf_done, 1)
        act.wait_ge(expf_done, 1)
        A(lf[:, :], lf[:, :], ACT.Ln, bias=1.0).then_inc(lnf_done, 1)
        act.wait_ge(sum_rows, 1)
        A(nmrow[:, 1, :], nmrow[:, 1, :], ACT.Exp, scale=-1.0).then_inc(emrow_done, 1)
        for hd in range(HEADS):
            act.wait_ge(nmb_ready, hd + 1)
            if hd:
                act.wait_ge(earg_done, SB * hd)
            A(nmb[:, :], bank[7][:, :], ACT.Copy).then_inc(nmb_copied, 1)
            for s in range(SB):
                n = SEQ - P * s
                act.wait_ge(earg_done, SB * hd + s + 1)
                A(ebuf[:, s % 2, 0:n], ebuf[:, s % 2, 0:n], ACT.Exp).then_inc(e_done, 1)
            act.wait_ge(w_used, SB * (hd + 1))
            A(h2[:, :], bank[7][:, :], ACT.Abs).then_inc(den_abs, 1)
            act.wait_ge(hh_done, hd + 1)
            A(h2[:, :], hb[:, :], ACT.Square).then_inc(hsq_done, 1)
            act.wait_ge(hms_ready, hd + 1)
            A(h2[:, :], bank[0][:, :], ACT.Sqrt, bias=prm[:, NCOL:NCOL + 1], scale=float(DM // P)).then_inc(hms_read, 1)
            act.wait_ge(o_scaled, hd + 1)
            A(xhi[:, 4 + hd, :], hb[:, :], ACT.Copy).then_inc(ybhi_done, 1)
        for n, q in enumerate((1, 2, 3, 0)):
            act.wait_ge(y_ready, n + 1)
            A(ysb[:, 16 * (q // 2) + q % 2:16 * (q // 2) + 16:2, :],
              bank[q][:, :].rearrange("p (g c) -> p g c", c=NCH), ACT.Copy).then_inc(y_copied, 1)
        act.wait_ge(y_back, 16 * 32)
        for m in range(4):
            A(uperm[:, m, :], uperm[:, m, :], ACT.Gelu_apprx_tanh).then_inc(gelu_done, 1)
        for m in range(4):
            act.wait_ge(gelu_done, m + 1)
            A(xhi[:, m, :], uperm[:, m, :], ACT.Copy).then_inc(gahi_done, 1)
        for m in range(4):
            act.wait_ge(glu_ready, m + 1)
            A(gsig[:, m, :], bank[m][:, :], ACT.Sigmoid).then_inc(glusig_done, 1)
        split_hi(T_GLU + RING)
        split_hi(T_GLU + 1 + RING)
        for m in range(4):
            act.wait_ge(out_freed, O_GLU + m + 1)
            A(xhi[:, m, :], yaf[:, m, :], ACT.Copy).then_inc(yahi_done, 1)

        def residual_squares(t0, o0, n):
            for m in range(KB):
                split_hi(t0 + m + RING)
                act.wait_ge(out_freed, o0 + m + 1)
                square(h[:, m, :], KB * n + m, m % 2)

        def mlp(l):
            t0, d0 = T_UP[l], T_DN[l]
            with act.Fori(0, FJ // 2) as i:
                for jj in range(2):
                    j = FJ * l + jj
                    split_hi(t0 + 2 * jj + RING, i, 4)
                    act.wait_ge(conv_done, i * 2 + (j + 1))
                    A(sbuf[:, :], cbuf[:, :], ACT.Silu).then_inc(silu_done, 1)
                    split_hi(t0 + 2 * jj + 1 + RING, i, 4)
                    act.wait_ge(a_done, i * 2 + (j + 1))
                    A(ahi[:, i * 2 + jj, :], abuf[:, :], ACT.Copy).then_inc(ahi_done, 1)
            n = 1 + 2 * l + 1

            def down(i, last):
                for s in range(12):
                    if not (last and s >= 8):
                        split_hi(d0 + s + RING, i, 12)
                    if s % 3 == 2:
                        act.wait_ge(out_freed, i * 4 + (O_DN[l] + s // 3 + 1))
                        square(h[:, i * 4 + s // 3, :], KB * n + s // 3, (s // 3) % 2, i, 4)

            if l == 0:
                with act.Fori(0, 2) as i:
                    down(i, False)
            else:
                down(0, False)
                down(1, True)

        residual_squares(T_OUT, O_OUT, 1)
        operand_hi(h, "g_ffn0")
        root_mean_square(1)
        mlp(0)
        operand_hi(h, "g_mix1")
        root_mean_square(2)
        for m in range(NQKV):
            split_hi(T_QKV + m + RING)
        for b in range(2):
            act.wait_ge(vwin_ready, b + 1)
            A(vwin[:, 4 * b:4 * b + 4, :], bank[4 + b][:, :].rearrange("p (c v) -> p c v", v=P),
              ACT.Copy).then_inc(vwin_copied, 1)
        for w in range(2 * NC + 2):
            if w < 2 * NC:
                act.wait_ge(asc_done, w + 1)
                if w >= 2:
                    act.wait_ge(apt_ready, w - 1)
                A(st[:, w % 2, 4, :], st[:, w % 2, 1, :], ACT.Exp)
                A(pbuf[:, w % 2, :], sbuf2[:, w % 2, :], ACT.Exp).then_inc(aexp_done, 1)
            if 1 <= w <= 2 * NC:
                v = w - 1
                act.wait_ge(apt_ready, v + 1)
                if v >= 2:
                    act.wait_ge(ao_ready, v - 1)
                A(ptb[:, v % 2, :], bank[6][:, :], ACT.Copy).then_inc(apt_copied, 1)
            if w >= 2:
                v = w - 2
                c, kv = v // 2, v % 2
                act.wait_ge(ao_ready, v + 1)
                A(obuf[:, 4 * kv:4 * kv + 4, WIN * c:WIN * (c + 1)],
                  bank[7][:, 0:4 * WIN].rearrange("p (j q) -> p j q", q=WIN), ACT.Copy).then_inc(ao_copied, 1)
        act.wait_ge(ao_copied, 2 * NC)
        for m in range(KB):
            A(xhi[:, m, :], obuf[:, m, :], ACT.Copy).then_inc(oahi_done, 1)
        residual_squares(T_WO, O_WO, 3)
        operand_hi(h, "g_ffn1")
        root_mean_square(3)
        mlp(1)
        root_mean_square(4)

    @block.vector
    def _(dve):
        steps = Steps(dve_step)
        V = nc.vector

        def settle():
            dve.wait_ge(dve_step, steps.value())

        def split_lo(t, i=0, per=0):
            dve.wait_ge(hi_done, i * per + (t + 1))
            V.tensor_tensor(wlo[:, t % RING, :], raw[:, t % RAWS, :], whi[:, t % RING, :].bitcast(f32),
                            ALU.subtract).then_inc(lo_done, 1)

        def operand_lo(src, g, n, k):
            for m in range(KB):
                dve.wait_ge(xhi_done, KB * k + m + 1)
                V.scalar_tensor_tensor(out=xlo[:, m, :], in0=src[:, m, :], scalar=col(g, m),
                                       in1=xhi[:, m, :].bitcast(f32), op0=ALU.mult,
                                       op1=ALU.subtract).then_inc(xlo_done, 1)
            row_factor(n)

        def row_factor(n):
            dve.wait_ge(rms_done, n + 1)
            V.reciprocal(rstd[:, :], rstd[:, :]).then_inc(rstd_done, 1)
            dve.wait_ge(rstd_done, n + 1)

        dve.wait_ge(params_in, 48)
        dve.wait_ge(x_in, 64)
        for m in range(KB):
            dve.wait_ge(xhi_done, m + 1)
            V.scalar_tensor_tensor(out=xlo[:, m, :], in0=xin[:, m, :], scalar=col("g_mix0", m),
                                   in1=xhi[:, m, :].bitcast(f32), op0=ALU.mult,
                                   op1=ALU.subtract).then_inc(xlo_done, 1)
        for t in range(RING):
            split_lo(t)
        row_factor(0)
        dve.wait_ge(pads_set, 1)
        for t in range(16):
            wait_tile_used(dve, t)
            if t + RING <= T_OUT:
                split_lo(t + RING)
            src = bank[t % 4]
            m = t % 4
            if t < 4:
                V.tensor_tensor(uperm[:, m, :].rearrange("p (s c) -> p c s", s=CH),
                                src[:, :].rearrange("p (c s) -> p c s", s=CH),
                                rstd[:, :].rearrange("p (c s) -> p c s", s=CH), ALU.mult).then_inc(out_freed, 1)
            elif t < 8:
                V.tensor_tensor(xpad[:, 3:], src[:, :], rstd[:, :], ALU.mult).then_inc(out_freed, 1)
                dve.wait_ge(out_freed, t + 1)
                if m:
                    dve.wait_ge(xcf_done, m)
                steps.up(V.tensor_scalar(cacc[:, :], xpad[:, 3:], col("mlw", 4 * m + 3), col("mlb", m),
                                         ALU.mult, ALU.add))
                for w in (2, 1, 0):
                    settle()
                    ins = V.scalar_tensor_tensor(out=cacc[:, :], in0=xpad[:, w:w + SEQ],
                                                 scalar=col("mlw", 4 * m + w), in1=cacc[:, :],
                                                 op0=ALU.mult, op1=ALU.add)
                    if w:
                        steps.up(ins)
                ins.then_inc(mconv_done, 1)
                dve.wait_ge(xchi_done, m + 1)
                V.tensor_tensor(xclo[:, m, :], xcf[:, :], xchi[:, m, :].bitcast(f32),
                                ALU.subtract).then_inc(xclo_done, 1)
            elif t < 12:
                if m == 0:
                    dve.wait_ge(u_saved, 16)
                V.tensor_tensor(vT[:, m, :], src[:, :], rstd[:, :], ALU.mult).then_inc(out_freed, 1)
            else:
                V.tensor_tensor(sigo[:, m, :], src[:, :], rstd[:, :], ALU.mult).then_inc(out_freed, 1)
            if t == 5:
                dve.wait_ge(lam_sq, 1)
                V.reciprocal(sm[:, 9, :], sm[:, 9, :]).then_inc(s5_recip, 1)
        dve.wait_ge(k_ready, 1)
        by_pair = ksb[:, :, :].rearrange("p i (j f) -> p f i j", f=2)
        for f in range(2):
            V.tensor_copy(by_pair[:, f], bank[(4, 7)[f]][:, 0:PAIRS * GCH].rearrange("p (j i) -> p i j", i=GCH)
                          ).then_inc(k_copied, 1)
        skip = cacc[0:GCH, :].rearrange("p (i g) -> p i g", i=GCH)
        steps.up(V.tensor_tensor(skip, ident[0:GCH, 0:GCH].unsqueeze(2).to_broadcast([GCH, GCH, GROUPS]),
                                 cols("ddiag", GCH).unsqueeze(1).to_broadcast([GCH, GCH, GROUPS]), ALU.mult))
        dve.wait_ge(k_copied, 2)
        settle()
        V.tensor_tensor(ksb[0:GCH, :, :], ksb[0:GCH, :, :], skip, ALU.add).then_inc(k_final, 1)
        dve.wait_ge(m1_ready, 8)
        V.memset(toep[:, :, :, :], 0.0).then_inc(toep_clear, 1)
        for b in range(8):
            dve.wait_ge(qk_ready, b + 1)
            V.tensor_copy((qT if b < 4 else kT)[:, b % 4, :], bank[b % 4][:, :]).then_inc(out_freed, 1)
        split_lo(T_QK + RING)
        dve.wait_ge(gates_ready, 1)
        V.tensor_scalar(g8[:, :], bank[4][0:8, :], col("bgate", 0, 8), None, ALU.add).then_inc(gates_copied, 1)
        dve.wait_ge(lnf_done, 1)
        steps.up(V.scalar_tensor_tensor(out=lf[:, :], in0=bank[5][0:HEADS, :], scalar=0.0, in1=lf[:, :],
                                        op0=ALU.min, op1=ALU.subtract))
        settle()
        steps.up(V.tensor_tensor_scan(fcum[:, :], ones[0:HEADS, 0:1].to_broadcast([HEADS, SEQ]), lf[:, :], 0.0,
                                      ALU.mult, ALU.add))
        settle()
        steps.up(V.tensor_tensor(arow[:, :], g8[0:HEADS, :], fcum[:, :], ALU.subtract))
        settle()
        steps.up(V.tensor_tensor_scan(lf[:, :], arow[:, :], arow[:, :], 0.0, ALU.max, ALU.max))
        settle()
        V.tensor_tensor(nmrow[:, 1, :], lf[:, :], fcum[:, :], ALU.add).then_inc(sum_rows, 1)
        V.tensor_scalar(nmrow[:, 0, :], lf[:, :], -1.0, None, ALU.mult).then_inc(rows_done, 1)
        dve.wait_ge(acol_ready, 1)
        V.tensor_copy(acol[:, :, :], bank[4][:, 0:SB * HEADS].rearrange("p (s h) -> p s h", h=HEADS)
                      ).then_inc(acol_copied, 1)
        dve.wait_ge(prep_done, 1)
        dve.wait_ge(acol_copied, 1)
        for hd in range(HEADS):
            dve.wait_ge(emb_ready, hd + 1)
            V.tensor_copy(emb[:, :], bank[6][:, :]).then_inc(emb_copied, 1)
            dve.wait_ge(nmb_copied, hd + 1)

            def exp_argument(s):
                n = SEQ - P * s
                if s >= 2 or hd:
                    dve.wait_ge(w_done, SB * hd + s - 1)
                V.tensor_scalar(ebuf[:, s % 2, 0:n], nmb[:, P * s:], acol[:, s, hd:hd + 1], 0.0,
                                ALU.add, ALU.min).then_inc(earg_done, 1)

            exp_argument(0)
            exp_argument(1)
            for s in range(SB):
                k = SB * hd + s
                n = SEQ - P * s
                dve.wait_ge(sc_ready, k + 1)
                dve.wait_ge(e_done, k + 1)
                if k >= 2:
                    dve.wait_ge(w_used, k - 1)
                steps.up(V.scalar_tensor_tensor(out=wbuf[:, k % 2, 0:n], in0=bank[4 + k % 2][:, 0:n],
                                                scalar=float(P) ** -0.5, in1=ebuf[:, s % 2, 0:n],
                                                op0=ALU.mult, op1=ALU.mult))
                settle()
                V.tensor_tensor(wbuf[:, k % 2, 0:P], wbuf[:, k % 2, 0:P], tri, ALU.mult).then_inc(w_done, 1)
                if s + 2 < SB:
                    exp_argument(s + 2)
            dve.wait_ge(w_used, SB * (hd + 1))
            dve.wait_ge(emb_copied, hd + 1)
            dve.wait_ge(den_abs, hd + 1)
            steps.up(V.tensor_tensor(h2[:, :], h2[:, :], emb[:, :], ALU.max))
            settle()
            steps.up(V.reciprocal(h2[:, :], h2[:, :]))
            settle()
            V.tensor_tensor(hb[:, :], bank[6][:, :], h2[:, :], ALU.mult).then_inc(hh_done, 1)
            dve.wait_ge(hms_ready, hd + 1)
            dve.wait_ge(hms_read, hd + 1)
            steps.up(V.reciprocal(h2[:, :], h2[:, :]))
            settle()
            dve.wait_ge(hh_done, hd + 1)
            steps.up(V.tensor_tensor(hb[:, :], hb[:, :], h2[:, :], ALU.mult))
            settle()
            dve.wait_ge(sigo_done, HEADS)
            V.scalar_tensor_tensor(out=hb[:, :], in0=hb[:, :], scalar=col("mlg", hd), in1=sigo[:, hd, :],
                                   op0=ALU.mult, op1=ALU.mult).then_inc(o_scaled, 1)
            dve.wait_ge(ybhi_done, hd + 1)
            V.tensor_tensor(xlo[:, 4 + hd, :], hb[:, :], xhi[:, 4 + hd, :].bitcast(f32),
                            ALU.subtract).then_inc(yb_done, 1)
        for m in range(4):
            dve.wait_ge(gahi_done, m + 1)
            V.tensor_tensor(xlo[:, m, :], uperm[:, m, :], xhi[:, m, :].bitcast(f32),
                            ALU.subtract).then_inc(galo_done, 1)
        for m in range(4):
            dve.wait_ge(glusig_done, m + 1)
            V.tensor_tensor(yaf[:, m, :].rearrange("p (c s) -> p c s", s=CH),
                            uperm[:, m, :].rearrange("p (s c) -> p c s", s=CH),
                            gsig[:, m, :].rearrange("p (s c) -> p c s", s=CH), ALU.mult).then_inc(out_freed, 1)
        split_lo(T_GLU + RING)
        split_lo(T_GLU + 1 + RING)
        for m in range(4):
            dve.wait_ge(yahi_done, m + 1)
            V.tensor_tensor(xlo[:, m, :], yaf[:, m, :], xhi[:, m, :].bitcast(f32),
                            ALU.subtract).then_inc(ya_done, 1)

        def residual(t0, o0):
            for m in range(KB):
                wait_tile_used(dve, t0 + m)
                split_lo(t0 + m + RING)
                V.tensor_tensor(h[:, m, :], h[:, m, :], bank[(o0 + m) % 4][:, :], ALU.add).then_inc(out_freed, 1)
            dve.wait_ge(out_freed, o0 + KB)

        def mlp(l):
            t0, d0, fw = T_UP[l], T_DN[l], "fw%d" % l
            V.memset(gpad[:, 0:2], 0.0)
            with dve.Fori(0, FJ // 2) as i:
                steps.enter(i, 4)
                for jj in range(2):
                    j = FJ * l + jj

                    def tap(k):
                        o = COLS[fw][0] + FJ * k + jj
                        return prm[:, bass.ds(i * 2 + o, 1)]

                    wait_tile_used(dve, (t0 + 2 * jj, i, 4))
                    split_lo(t0 + 2 * jj + RING, i, 4)
                    V.tensor_tensor(gpad[:, 2:], bank[(O_UP[l] + 2 * jj) % 4][:, :], rstd[:, :],
                                    ALU.mult).then_inc(out_freed, 1)
                    dve.wait_ge(out_freed, i * 4 + (O_UP[l] + 2 * jj + 1))
                    if j:
                        dve.wait_ge(silu_done, i * 2 + j)
                    steps.up(V.tensor_scalar(cbuf[:, :], gpad[:, 2:], tap(2), tap(3), ALU.mult, ALU.add))
                    settle()
                    steps.up(V.scalar_tensor_tensor(out=cbuf[:, :], in0=gpad[:, 1:1 + SEQ], scalar=tap(1),
                                                    in1=cbuf[:, :], op0=ALU.mult, op1=ALU.add))
                    settle()
                    V.scalar_tensor_tensor(out=cbuf[:, :], in0=gpad[:, 0:SEQ], scalar=tap(0),
                                           in1=cbuf[:, :], op0=ALU.mult, op1=ALU.add).then_inc(conv_done, 1)
                    wait_tile_used(dve, (t0 + 2 * jj + 1, i, 4))
                    split_lo(t0 + 2 * jj + 1 + RING, i, 4)
                    V.tensor_tensor(vbuf[:, :], bank[(O_UP[l] + 2 * jj + 1) % 4][:, :], rstd[:, :],
                                    ALU.mult).then_inc(out_freed, 1)
                    dve.wait_ge(out_freed, i * 4 + (O_UP[l] + 2 * jj + 2))
                    dve.wait_ge(silu_done, i * 2 + (j + 1))
                    V.tensor_tensor(abuf[:, :], vbuf[:, :], sbuf[:, :], ALU.mult).then_inc(a_done, 1)
                    dve.wait_ge(ahi_done, i * 2 + (j + 1))
                    V.tensor_tensor(alo[:, i * 2 + jj, :], abuf[:, :], ahi[:, i * 2 + jj, :].bitcast(f32),
                                    ALU.subtract).then_inc(alo_done, 1)
            steps.leave(FJ // 2)

            def down(i, last):
                for s in range(12):
                    wait_tile_used(dve, (d0 + s, i, 12))
                    if not (last and s >= 8):
                        split_lo(d0 + s + RING, i, 12)
                    if s % 3 == 2:
                        m = s // 3
                        V.tensor_tensor(h[:, i * 4 + m, :], h[:, i * 4 + m, :], bank[(O_DN[l] + m) % 4][:, :],
                                        ALU.add).then_inc(out_freed, 1)

            if l == 0:
                with dve.Fori(0, 2) as i:
                    down(i, False)
            else:
                down(0, False)
                down(1, True)
            dve.wait_ge(out_freed, O_DN[l] + KB)

        dve.wait_ge(x_back, 16)
        residual(T_OUT, O_OUT)
        operand_lo(h, "g_ffn0", 1, 1)
        mlp(0)
        operand_lo(h, "g_mix1", 2, 2)
        V.memset(akd[:, :, 0:WIN], 0.0)
        steps.up(V.memset(avT[:, 0:WIN], 0.0))
        for m in range(NQKV):
            wait_tile_used(dve, T_QKV + m)
            split_lo(T_QKV + m + RING)
            dst = aq[:, m, :] if m < 8 else akd[:, m - 8, WIN:] if m < 10 else avT[:, WIN:]
            V.tensor_tensor(dst, bank[(O_QKV + m) % 4][:, :], rstd[:, :], ALU.mult).then_inc(out_freed, 1)
            dve.wait_ge(out_freed, O_QKV + m + 1)
            V.tensor_scalar(dst, dst, col("bqkv", m), None, ALU.add).then_inc(qkv_done, 1)
        dve.wait_ge(band_in, 16)
        S4 = [P, 4, P]

        def scores(w):
            c, kv = w // 2, w % 2
            s4 = sbuf2[:, w % 2, :].rearrange("p (j k) -> p j k", k=P)
            mx, sk = st[:, w % 2, 0, :], st[:, w % 2, 1, :]
            dve.wait_ge(asc_ready, w + 1)
            if w >= 2:
                dve.wait_ge(aexp_done, w - 1)
            steps.up(V.scalar_tensor_tensor(
                out=s4, in0=bank[4 + w % 2][:, :].rearrange("p (j k) -> p j k", k=P), scalar=float(AHD) ** -0.5,
                in1=bandsb[:, 4 * kv:4 * kv + 4, :], op0=ALU.mult, op1=ALU.add))
            settle()
            if c == 0:
                steps.up(V.memset(s4[:, :, 0:WIN], -1e30))
                settle()
            steps.up(V.tensor_reduce(mx, s4, AX.X, ALU.max))
            settle()
            steps.up(V.tensor_tensor(mx, mx, cols("sink")[:, 4 * kv:4 * kv + 4], ALU.max))
            settle()
            V.tensor_tensor(sk, cols("sink")[:, 4 * kv:4 * kv + 4], mx, ALU.subtract)
            V.tensor_tensor(s4, s4, mx.unsqueeze(2).to_broadcast(S4), ALU.subtract).then_inc(asc_done, 1)

        def normalise(w):
            p4 = pbuf[:, w % 2, :].rearrange("p (j k) -> p j k", k=P)
            su = st[:, w % 2, 2, :]
            dve.wait_ge(aexp_done, w + 1)
            steps.up(V.tensor_reduce(su, p4, AX.X, ALU.add))
            settle()
            steps.up(V.tensor_tensor(su, su, st[:, w % 2, 4, :], ALU.add))
            settle()
            steps.up(V.reciprocal(su, su))
            settle()
            V.tensor_tensor(p4, p4, su.unsqueeze(2).to_broadcast(S4), ALU.mult).then_inc(anorm_done, 1)

        for w in range(2 * NC + 1):
            if w < 2 * NC:
                scores(w)
            if w:
                normalise(w - 1)
        for m in range(KB):
            dve.wait_ge(oahi_done, m + 1)
            V.tensor_tensor(xlo[:, m, :], obuf[:, m, :], xhi[:, m, :].bitcast(f32),
                            ALU.subtract).then_inc(oalo_done, 1)
        residual(T_WO, O_WO)
        operand_lo(h, "g_ffn1", 3, 3)
        mlp(1)
        row_factor(4)
        for m in range(KB):
            V.scalar_tensor_tensor(out=outb[:, m, :], in0=h[:, m, :], scalar=col("g_fin", m), in1=rstd[:, :],
                                   op0=ALU.mult, op1=ALU.mult).then_inc(out_done, 1)

    @block.tensor
    def _(pe):
        MM = nc.tensor.matmul

        def block3(dst, slot, b, rhi, rlo, start, stop):
            wh, wl = whi[:, slot, b * P:(b + 1) * P], wlo[:, slot, b * P:(b + 1) * P]
            MM(dst, wh, rhi, start=start, stop=False)
            MM(dst, wh, rlo, start=False, stop=False)
            return MM(dst, wl, rhi, start=False, stop=stop)

        def product(t, o, i=0, per=0):
            pe.wait_ge(lo_done, i * per + (t + 1))
            if o >= 4:
                pe.wait_ge(out_freed, i * per + (o - 3))
            for b in range(KB):
                ins = block3(bank[o % 4][:, :], t % RING, b, xhi[:, b, :], xlo[:, b, :], b == 0, b == KB - 1)
            ins.then_inc(tile_used, 1)

        def mean(n):
            pe.wait_ge(acc_done, KB * (n + 1))
            MM(bank[7][:, :], mean_w[:, :], ssum[:, :], start=True, stop=True).then_inc(mean_done, 1)

        def transpose(dst, src, k):
            return nc.tensor.transpose(dst, src, ident[0:k, 0:k])

        pe.wait_ge(params_in, 48)
        pe.wait_ge(consts_set, 1)
        pe.wait_ge(xlo_done, KB)
        product(0, 0)
        mean(0)
        for t in range(1, 16):
            product(t, t)
        pe.wait_ge(g_built, 1)
        for g in range(GROUPS):
            r = slice(STATE * (g % 2), STATE * (g % 2) + STATE)
            j = g // 2
            dst = bank[(4, 7)[g % 2]][:, j * GCH:(j + 1) * GCH]
            MM(dst, gre[r, j, :], bcp[r, 2, j * GCH:(j + 1) * GCH], start=True, stop=False)
            ins = MM(dst, gim[r, j, :], bcp[r, 3, j * GCH:(j + 1) * GCH], start=False, stop=True)
        ins.then_inc(k_ready, 1)
        for b in range(8):
            if b >= 2:
                pe.wait_ge(m1_copied, b - 1)
            for k in range(4):
                ins = transpose(bank[5 + b % 2][:, k * P:(k + 1) * P],
                                (gre if b < 4 else gim)[:, 4 * (b % 4) + k, :], P)
            ins.then_inc(m1_ready, 1)
        pe.wait_ge(m1_copied, 8)
        pe.wait_ge(k_copied, 2)
        pe.wait_ge(u_back, 16 * CH)
        pe.wait_ge(rstd_done, 1)
        for r, m1 in enumerate((m1re, m1im)):
            for g in range(GROUPS):
                p0, j = STATE * (g % 2), g // 2
                ins = MM(bank[4 + 2 * r + j // 8][p0:p0 + STATE, (j % 8) * NCH:(j % 8 + 1) * NCH],
                         m1[:, j, p0:p0 + STATE], uc[:, g, :], start=True, stop=True)
            ins.then_inc(s5in_ready, 1)
        pe.wait_ge(lo_done, T_QK + 1)
        pe.wait_ge(xclo_done, HEADS)
        for b in range(8):
            pe.wait_ge(out_freed, O_QK + b - 3)
            block3(bank[b % 4][:, :], T_QK % RING, b, xchi[:, b % 4, :], xclo[:, b % 4, :], True,
                   True).then_inc(qk_ready, 1)
        pe.wait_ge(s5in_copied, 2)
        for hd in range(HEADS):
            if hd >= 2:
                pe.wait_ge(vtok_copied, hd - 1)
            for s in range(SB):
                ins = transpose(bank[6 + hd % 2][:, s * P:(s + 1) * P], vT[:, hd, s * P:(s + 1) * P], P)
            ins.then_inc(vtok_ready, 1)
        pe.wait_ge(out_freed, O_QK + 8)
        for k in range(12):
            ins = MM(bank[4][0:8, :], cols("wg")[:, 8 * k:8 * k + 8], (qT, kT, vT)[k % 3][:, k // 3, :],
                     start=k == 0, stop=k == 11)
        ins.then_inc(gates_ready, 1)
        pe.wait_ge(gates_copied, 1)
        MM(bank[5][0:HEADS, :], ident[0:8, HEADS:8], g8[:, :], start=True, stop=True).then_inc(fsel_ready, 1)
        pe.wait_ge(rows_done, 1)
        for s in range(SB):
            ins = transpose(bank[4][:, s * HEADS:(s + 1) * HEADS], arow[:, s * P:(s + 1) * P], HEADS)
        ins.then_inc(acol_ready, 1)
        pe.wait_ge(vtok_copied, HEADS)
        pe.wait_ge(emrow_done, 1)
        pe.wait_ge(acol_copied, 1)

        def head_scores(k):
            hd, s = k // SB, k % SB
            if k >= 2:
                pe.wait_ge(w_done, k - 1)
            MM(bank[4 + k % 2][:, 0:SEQ - P * s], kT[:, hd, s * P:(s + 1) * P], qT[:, hd, s * P:],
               start=True, stop=True).then_inc(sc_ready, 1)

        for hd in range(HEADS):
            if hd:
                pe.wait_ge(hh_done, hd)
            pick = ident[0:HEADS, hd:hd + 1].to_broadcast([HEADS, P])
            MM(bank[7][:, :], pick, nmrow[:, 0, :], start=True, stop=True).then_inc(nmb_ready, 1)
            MM(bank[6][:, :], pick, nmrow[:, 1, :], start=True, stop=True).then_inc(emb_ready, 1)
            if hd:
                pe.wait_ge(hsq_done, hd)
                if hd >= 2:
                    pe.wait_ge(hms_read, hd - 1)
                MM(bank[0][:, :], mean_w[:, :], h2[:, :], start=True, stop=True).then_inc(hms_ready, 1)
            head_scores(SB * hd)
            for s in range(SB):
                k = SB * hd + s
                if s + 1 < SB:
                    head_scores(k + 1)
                pe.wait_ge(w_done, k + 1)
                if s == 0:
                    pe.wait_ge(nmb_copied, hd + 1)
                    pe.wait_ge(emb_copied, hd + 1)
                w = wbuf[:, k % 2, 0:SEQ - P * s]
                MM(bank[6][:, P * s:], vtok[:, hd, s, :], w, start=s == 0, stop=s == SB - 1)
                MM(bank[7][:, P * s:], ones[:, :], w, start=s == 0, stop=s == SB - 1).then_inc(w_used, 1)
        pe.wait_ge(hsq_done, HEADS)
        pe.wait_ge(hms_read, HEADS - 1)
        MM(bank[0][:, :], mean_w[:, :], h2[:, :], start=True, stop=True).then_inc(hms_ready, 1)
        pe.wait_ge(toep_built, 16 * CH)
        pe.wait_ge(scan_done, 1)
        for q in (1, 2, 3, 0):
            if q == 0:
                pe.wait_ge(hms_read, HEADS)
            for j in range(8 * (q // 2), 8 * (q // 2) + 8):
                g = 2 * j + q % 2
                r = slice(STATE * (g % 2), STATE * (g % 2) + STATE)
                dst = bank[q][:, (j % 8) * NCH:(j % 8 + 1) * NCH]
                MM(dst, toep[:, :, :, g].rearrange("p s i -> p (s i)"), uc[:, g, :], start=True, stop=False)
                MM(dst, fre[r, j, :], xs[r, 0, j, 0:NCH], start=False, stop=False)
                ins = MM(dst, fim[r, j, :], xs[r, 1, j, 0:NCH], start=False, stop=True)
            ins.then_inc(y_ready, 1)
        pe.wait_ge(galo_done, 4)
        for m in range(4):
            t = T_GLU + m // 2
            pe.wait_ge(lo_done, t + 1)
            for b in range(4):
                ins = block3(bank[m][:, :], t % RING, 4 * (m % 2) + b, xhi[:, b, :], xlo[:, b, :], b == 0, b == 3)
            ins.then_inc(glu_ready, 1)
        pe.wait_ge(ya_done, 4)
        pe.wait_ge(yb_done, HEADS)
        for m in range(KB):
            product(T_OUT + m, O_OUT + m)

        def mlp(l):
            mean(1 + 2 * l)
            pe.wait_ge(xlo_done, KB * (2 + 2 * l))
            with pe.Fori(0, FJ // 2) as i:
                for s in range(4):
                    product(T_UP[l] + s, O_UP[l] + s, i, 4)
            with pe.Fori(0, 2) as i:
                for m in range(4):
                    pe.wait_ge(out_freed, i * 4 + (O_DN[l] + m - 3))
                    for part in range(3):
                        t = T_DN[l] + 3 * m + part
                        pe.wait_ge(lo_done, i * 12 + (t + 1))
                        ks = (range(0, 8), range(8, 15), range(15, FJ))[part]
                        for k in ks:
                            if k == 0 or k == FJ - 2:
                                pe.wait_ge(alo_done, FJ * (l + 1) - (2 if k == 0 else 0))
                            ins = block3(bank[(O_DN[l] + m) % 4][:, :], t % RING, k - ks[0], ahi[:, k, :],
                                         alo[:, k, :], k == 0, k == FJ - 1)
                        ins.then_inc(tile_used, 1)

        mlp(0)
        mean(2)
        pe.wait_ge(xlo_done, 3 * KB)
        for m in range(NQKV):
            product(T_QKV + m, O_QKV + m)
        pe.wait_ge(qkv_done, NQKV)
        for b in range(2):
            for k in range(4):
                c = 4 * b + k
                ins = transpose(bank[4 + b][:, k * P:(k + 1) * P], avT[:, c * WIN:c * WIN + P], P)
            ins.then_inc(vwin_ready, 1)
        pe.wait_ge(vwin_copied, 2)
        for w in range(2 * NC + 2):
            if w < 2 * NC:
                c, kv = w // 2, w % 2
                if w >= 2:
                    pe.wait_ge(asc_done, w - 1)
                for j in range(4):
                    for hf in range(2):
                        r = slice(AHD * hf, AHD * hf + AHD)
                        ins = MM(bank[4 + w % 2][r, j * P:(j + 1) * P],
                                 aq[r, 4 * kv + j, WIN * c:WIN * (c + 1)], akd[r, kv, WIN * c:WIN * c + P],
                                 start=True, stop=True)
                ins.then_inc(asc_ready, 1)
            if 1 <= w <= 2 * NC:
                v = w - 1
                pe.wait_ge(anorm_done, v + 1)
                if v:
                    pe.wait_ge(apt_copied, v)
                for j in range(4):
                    ins = transpose(bank[6][:, j * P:(j + 1) * P], pbuf[:, v % 2, j * P:(j + 1) * P], P)
                ins.then_inc(apt_ready, 1)
            if w >= 2:
                v = w - 2
                c, kv = v // 2, v % 2
                pe.wait_ge(apt_copied, v + 1)
                if v:
                    pe.wait_ge(ao_copied, v)
                p4 = ptb[:, v % 2, :].rearrange("p (j f q) -> p j f q", f=2, q=WIN)
                for hf in range(2):
                    ins = MM(bank[7][AHD * hf:AHD * hf + AHD, 0:4 * WIN], vwin[:, c, AHD * kv:AHD * kv + AHD],
                             p4[:, :, hf, :], start=True, stop=True)
                ins.then_inc(ao_ready, 1)
        pe.wait_ge(oalo_done, KB)
        for m in range(KB):
            product(T_WO + m, O_WO + m)
        mlp(1)
        mean(4)

    ctx.close()


def _tile(w):
    k = w.shape[0] // P
    return w.reshape(k, P, P).transpose(1, 0, 2).reshape(P, k * P)


def _tiles(w):
    return [_tile(w[:, c:c + P]) for c in range(0, w.shape[1], P)]


def _columns(v):
    return v.reshape(-1, P).T


def _bucket():
    rel = (np.arange(2 * WIN)[None, :] - WIN) - np.arange(WIN)[:, None]
    n = np.abs(rel)
    scaled = np.log(np.maximum(n, 1) / 8) / np.log(128 / 8) * 8
    large = np.minimum(8 + scaled.astype(np.int32), 15)
    return (rel > 0).astype(np.int32) * 16 + np.where(n < 8, n, large)


def kernel(**inputs):
    import concourse.bacc as bacc
    from concourse.bass_utils import run_bass_kernel_spmd

    a = {k: np.asarray(v) for k, v in inputs.items()}
    f32 = np.float32
    stream = _tiles(a["ab_w_in"][0])
    blocks = [a["ml_w_q"][0][h] for h in range(HEADS)] + [a["ml_w_k"][0][h] for h in range(HEADS)]
    stream.append(np.concatenate(blocks, axis=1))
    glu = _tiles(a["s5_w_glu"][0])
    stream += [np.concatenate(glu[2 * k:2 * k + 2], axis=1) for k in range(2)]
    stream += _tiles(a["ab_w_out"][0])

    def mlp(l):
        up = _tiles(a["ffn_w_up"][l])
        out = []
        for j in range(FJ):
            out += [up[j], up[FJ + j]]
        for w in _tiles(a["ffn_w_down"][l]):
            for k0, k1 in ((0, 8), (8, 15), (15, FJ)):
                part = w[:, k0 * P:k1 * P]
                out.append(np.concatenate([part, np.zeros((P, (8 - k1 + k0) * P), f32)], axis=1))
        return out

    stream += mlp(0)
    wqkv = a["swa_w_qkv"][0]
    bqkv = a["swa_b_qkv"][0]
    nq = QH * AHD
    order = np.concatenate([np.arange(nq), nq + np.tile(np.arange(AHD), 2), nq + AHD + np.tile(np.arange(AHD), 2),
                            nq + 2 * AHD + np.arange(2 * AHD)])
    stream += _tiles(wqkv[:, order])
    stream += _tiles(a["swa_w_o"][0])
    stream += mlp(1)
    assert len(stream) == T_END
    wstream = np.ascontiguousarray(np.stack(stream))

    def pairs(v):
        v = v.reshape((PAIRS, P) + v.shape[2:])
        return np.moveaxis(v, 0, 1)

    prm = np.zeros((P, NCOL), f32)

    def put(name, v):
        o, n = COLS[name]
        assert v.shape[1] == n, name
        prm[:v.shape[0], o:o + n] = v

    put("g_mix0", _columns(a["norm_mix_g"][0]))
    put("g_mix1", _columns(a["norm_mix_g"][1]))
    put("g_ffn0", _columns(a["norm_ffn_g"][0]))
    put("g_ffn1", _columns(a["norm_ffn_g"][1]))
    put("g_fin", _columns(a["norm_final_g"]))
    for l in range(2):
        put("fw%d" % l, np.concatenate([_columns(a["ffn_conv_w"][l][k]) for k in range(3)]
                                       + [_columns(a["ffn_conv_b"][l])], axis=1))
    put("mlw", np.stack([_columns(a["ml_conv_w"][0][k]) for k in range(4)], axis=2).reshape(P, 4 * HEADS))
    put("mlb", _columns(a["ml_conv_b"][0]))
    put("mlg", _columns(a["ml_norm_g"][0]))
    put("bqkv", _columns(bqkv[order]))
    put("sink", np.repeat(a["swa_sinks"][0].reshape(QH // 2, 2).T, WIN, axis=0))
    put("bgate", a["ml_b_gates"][0].reshape(8, 1))
    put("ddiag", a["s5_d"][0].reshape(GROUPS, GCH).T)
    put("ldt", pairs(np.repeat(a["s5_log_dt"][0][:, None], STATE, axis=1)))
    put("are", pairs(a["s5_a_re"][0]))
    put("aim", pairs(a["s5_a_im"][0]))
    put("wg", a["ml_w_gates"][0].reshape(12, P, 8).transpose(1, 0, 2).reshape(P, 96))
    bc = np.stack([pairs(a["s5_b_re"][0]), pairs(a["s5_b_im"][0]),
                   pairs(a["s5_c_re"][0].transpose(0, 2, 1)), pairs(a["s5_c_im"][0].transpose(0, 2, 1))], axis=1)
    bc = np.ascontiguousarray(bc.reshape(P, 4, PAIRS * GCH))
    consts = np.stack([np.eye(P, dtype=f32), np.triu(np.ones((P, P), f32))], axis=1)
    band = a["rel_bias"][_bucket()]
    band = band.transpose(2, 0, 1).reshape(QH // 2, 2 * WIN, 2 * WIN).transpose(1, 0, 2)
    xT = a["x"][0].T.reshape(KB, P, SEQ).transpose(1, 0, 2)

    nc = bacc.Bacc("TRN2", target_bir_lowering=False, num_devices=1)
    dt = mybir.dt.float32
    arrays = {"wstream": wstream, "xT": xT, "params": prm, "bc": bc, "consts": consts, "band": band}
    arrays = {k: np.ascontiguousarray(v) for k, v in arrays.items()}
    aps = {k: nc.dram_tensor(k, v.shape, dt, kind="ExternalInput").ap() for k, v in arrays.items()}
    outT = nc.dram_tensor("outT", (P, KB, SEQ), dt, kind="ExternalOutput").ap()
    u_scratch = nc.dram_tensor("u_scratch", (4, P, CH, NCH), dt, kind="Internal").ap()
    y_scratch = nc.dram_tensor("y_scratch", (CH, GCH, GROUPS, NCH), dt, kind="Internal").ap()
    build(nc, **aps, outT=outT, u_scratch=u_scratch, y_scratch=y_scratch)
    r = run_bass_kernel_spmd(nc, [arrays], core_ids=[0])
    out = r.results[0]["outT"]
    return np.ascontiguousarray(out.transpose(2, 1, 0).reshape(1, SEQ, DM))
```

```python
from contextlib import ExitStack

import numpy as np

import concourse.bass as bass
from concourse import mybir

P = 128
SEQ = 512
DM = 1024
KB = DM // P
D_FF = 2816
FJ = D_FF // P
HEADS = 4
SB = SEQ // P
GROUPS, GCH, STATE = 32, 16, 64
PAIRS = GROUPS // 2
CH = P // GCH
NCH = SEQ // CH
SUP = 8
QH, AHD, WIN = 16, 64, 64
NC = SEQ // WIN
KW = 2 * WIN + 1
EPS = 1e-6
DEN_SCALE = EPS * P / DM
NUM_BANK = (6, 0, 6, 6)
Y_AFTER = ((), (), (0, 1), (2, 3))
EXPM_LOG = 10

T_IN, T_QK, T_GLU, T_OUT = 0, 16, 17, 19
T_UP = [27, 114]
T_DN = [T_UP[0] + 2 * FJ, T_UP[1] + 2 * FJ]
T_QKV = T_DN[0] + 3 * KB
NQKV = 11
T_WO = T_QKV + NQKV
T_END = T_DN[1] + 3 * KB
assert T_WO + KB == T_UP[1] and T_END % 2 == 0
O_IN, O_QK, O_GLU, O_OUT = 0, 16, 24, 28
O_UP = [36, 107]
O_DN = [O_UP[0] + 2 * FJ, O_UP[1] + 2 * FJ]
O_QKV = O_DN[0] + KB
O_WO = O_QKV + NQKV
assert O_WO + KB == O_UP[1]
RAWS, RING = 2, 4

COLS = {}


def _col(name, n):
    COLS[name] = (sum(w for _, w in COLS.values()), n)


for _n, _w in (("g_mix0", KB), ("g_ffn0", KB), ("g_mix1", KB), ("g_ffn1", KB), ("g_fin", KB),
               ("fw0", 4 * FJ), ("fw1", 4 * FJ), ("mlw", 4 * HEADS), ("mlb", HEADS), ("mlg", HEADS),
               ("bqkv", NQKV), ("sink", QH // 2), ("bgate", 1), ("ddiag", GROUPS),
               ("ldt", PAIRS), ("are", PAIRS), ("aim", PAIRS), ("wg", 12 * 8)):
    _col(_n, _w)
NCOL = sum(w for _, w in COLS.values())


def used_count(t):
    return t + 1 if t < T_QK else t + 1 - 3


class Steps:

    def __init__(self, sem):
        self.sem, self.n, self.i, self.per = sem, 0, None, 0

    def up(self, ins):
        ins.then_inc(self.sem, 1)
        self.n += 1

    def value(self):
        return self.n if self.i is None else self.i * self.per + self.n

    def enter(self, i, per):
        self.i, self.per, self.base = i, per, self.n

    def leave(self, iters):
        assert self.n - self.base == self.per, (self.n - self.base, self.per)
        self.i, self.n = None, self.base + self.per * iters


def build(nc, wstream, xT, params, bc, consts, band, outT, u_scratch, y_scratch):
    f32, f32r = mybir.dt.float32, mybir.dt.float32r
    ACT, ALU, AX = mybir.ActivationFunctionType, mybir.AluOpType, mybir.AxisListType
    ctx = ExitStack()

    def sem(name):
        return ctx.enter_context(nc.semaphore(name))

    top = [nc.sbuf_base + (-nc.sbuf_base) % 64]

    def at(name, shape, offset, dt=f32):
        return nc.alloc_sbuf_tensor_at(name, shape, dt, offset=offset)

    def size(shape):
        return (int(np.prod(shape[1:])) * 4 + 63) // 64 * 64

    def sb(name, shape, dt=f32):
        o = top[0]
        top[0] += size(shape)
        return at(name, shape, o, dt)

    raw = sb("raw", [P, RAWS, 8 * P])
    whi = sb("whi", [P, RING, 8 * P], f32r)
    wlo = sb("wlo", [P, RING, 8 * P], f32r)
    xn_at = top[0]
    xhi = sb("xhi", [P, KB, SEQ], f32r)
    xlo = sb("xlo", [P, KB, SEQ], f32r)
    con = sb("con", [P, 2, P])
    ident, tri = con[:, 0, :], con[:, 1, :]
    ones = sb("ones", [P, P])
    mean_w = sb("mean_w", [P, P])
    rstd = sb("rstd", [P, SEQ])
    sq = sb("sq", [P, 2, SEQ])
    ssum_at = top[0]
    ssum = sb("ssum", [P, SEQ])
    prm = sb("prm", [P, NCOL + 1])

    def col(name, j=0, parts=P):
        o = COLS[name][0] + j
        return prm[0:parts, o:o + 1]

    def cols(name, parts=P):
        o, n = COLS[name]
        return prm[0:parts, o:o + n]

    base = top[0]
    end = nc.sbuf_usable_end

    def plan(*items, start=base):
        o, out = start, []
        for name, shape, dt in items:
            out.append(at(name, shape, o, dt))
            o += size(shape)
        assert o <= end, (items[0][0], o - end)
        return out

    h_at = end - size([P, KB, SEQ]) - (end - size([P, KB, SEQ])) % 64
    h = at("h", [P, KB, SEQ], h_at)
    ahi, alo, gpad, cbuf, sbuf, vbuf, abuf = plan(
        ("ahi", [P, FJ, SEQ], f32r), ("alo", [P, FJ, SEQ], f32r), ("gpad", [P, 2 + SEQ], f32),
        ("cbuf", [P, SEQ], f32), ("sbuf", [P, SEQ], f32), ("vbuf", [P, SEQ], f32), ("abuf", [P, SEQ], f32))
    assert base + 2 * size([P, FJ, SEQ]) + 5 * 2112 <= h_at
    F2 = [P, PAIRS, P]
    (fre, fim, gre, gim, m1re, m1im, uc, uperm, xchi, xclo, sigo, xs, ksb) = plan(
        ("fre", F2, f32), ("fim", F2, f32), ("gre", F2, f32), ("gim", F2, f32),
        ("m1re", F2, f32), ("m1im", F2, f32), ("uc", [P, GROUPS, NCH], f32), ("uperm", [P, 4, SEQ], f32),
        ("xchi", [P, 4, SEQ], f32r), ("xclo", [P, 4, SEQ], f32r), ("sigo", [P, 4, SEQ], f32),
        ("xs", [P, 2, PAIRS, NCH + 1], f32), ("ksb", [P, GCH, GROUPS], f32))
    o0 = base + 6 * size(F2) + 3 * 8192
    toep = at("toep", [P, CH, GCH, GROUPS], base + 2 * size(F2))
    xin = at("xin", [P, KB, SEQ], base + 4 * size(F2))
    qT = at("qT", [P, HEADS, SEQ], base + 4 * size(F2))
    kT = at("kT", [P, HEADS, SEQ], base + 5 * size(F2))
    vT = at("vT", [P, HEADS, SEQ], base + 6 * size(F2) + 8192)
    vtok = at("vtok", [P, HEADS, SB, P], base + 6 * size(F2) + 16384)
    yaf = at("yaf", [P, 4, SEQ], base + 6 * size(F2) + 16384)
    ysb = at("ysb", [P, GROUPS, NCH], base + 6 * size(F2) + 24576)
    gsig = at("gsig", [P, 4, SEQ], base + 6 * size(F2) + 24576)
    tail = base + 6 * size(F2) + 6 * 8192 + size([P, 2, PAIRS, NCH + 1]) + 2048
    ebuf, wbuf, hb = plan(
        ("ebuf", [P, SB, SEQ], f32), ("wbuf", [P, 2, SEQ], f32), ("hb", [P, 2, SEQ], f32), start=tail)
    bcp, xpad, cacc, xcf, ptmp, sm = plan(
        ("bcp", [P, 4, PAIRS * GCH], f32), ("xpad", [P, 3 + SEQ], f32), ("cacc", [P, SEQ], f32),
        ("xcf", [P, SEQ], f32), ("ptmp", [P, 4, 256], f32), ("sm", [P, 40, PAIRS], f32), start=tail)
    s5x_at = tail + 4096 + 2112 + 4096 + 4096 + 2560
    q_re, q_im = plan(("q_re", [P, SUP, PAIRS], f32), ("q_im", [P, SUP, PAIRS], f32),
                      start=s5x_at)
    keep_at = s5x_at + 1024
    acol, = plan(("acol", [P, SB, HEADS], f32), start=keep_at)
    qk2, aj2 = plan(("qk2", [P, 2 * PAIRS, SUP], f32), ("aj2", [P, 2 * PAIRS, SUP], f32), start=ssum_at)
    st1 = at("st1", [P, 2 * PAIRS, SUP], xn_at)
    st2 = at("st2", [P, 2 * PAIRS, SUP], xn_at + 8 * 2048)
    hsq = at("hsq", [P, SEQ], xn_at + 2048)
    dsq = at("dsq", [P, 2, SEQ], xn_at + 2 * 2048)
    g8 = at("g8", [8, SEQ], xn_at + 6 * 2048)
    lf = at("lf", [HEADS, SEQ], xn_at + 7 * 2048)
    fcum = at("fcum", [HEADS, SEQ], xn_at + 14 * 2048)
    arow = at("arow", [HEADS, SEQ], xn_at + 15 * 2048)
    nmrow = at("nmrow", [HEADS, 2, SEQ], ssum_at - 4096)
    (aq, akd, avT, vwin, bandsb, sbuf2, pbuf, ptb, obuf, st) = plan(
        ("aq", [P, 8, SEQ], f32), ("akd", [P, 2, WIN + SEQ], f32), ("avT", [P, WIN + SEQ], f32),
        ("vwin", [P, NC, P], f32), ("bandsb", [P, 8, P], f32), ("sbuf2", [P, 2, 4, KW], f32),
        ("pbuf", [P, 4, 4, KW], f32), ("ptb", [P, 2, SEQ], f32), ("obuf", [P, 8, SEQ], f32),
        ("st", [P, 4, 3, 4], f32))
    assert st is not None and base + 16384 + 2 * 2304 + 2304 + 2 * 4096 + 8 * 4096 + 16384 <= h_at
    outb = at("outb", [P, KB, SEQ], base)

    bank = [ctx.enter_context(nc.psum_tensor(f"bank{b}", [P, SEQ], f32)) for b in range(8)]

    raw_in = [sem(f"raw_in{s}") for s in range(RAWS)]
    hi_done, lo_done = sem("hi_done"), sem("lo_done")
    tile_used = sem("tile_used")
    out_freed = sem("out_freed")
    params_in, x_in, band_in = sem("params_in"), sem("x_in"), sem("band_in")
    consts_set = sem("consts_set")
    pads_set = sem("pads_set")
    sq_done, acc_done = sem("sq_done"), sem("acc_done")
    sum_clear = sem("sum_clear")
    mean_done, rstd_done, rms_done = sem("mean_done"), sem("rstd_done"), sem("rms_done")
    h_done = sem("h_done")
    xhi_done, xlo_done = sem("xhi_done"), sem("xlo_done")
    dve_step, act_step, pool_step = sem("dve_step"), sem("act_step"), sem("pool_step")
    conv_done, silu_done, a_done, ahi_done, alo_done = (sem(n) for n in (
        "conv_done", "silu_done", "a_done", "ahi_done", "alo_done"))
    u_saved, u_back = sem("u_saved"), sem("u_back")
    s5_recip, prep_done = sem("s5_recip"), sem("prep_done")
    ybhi_done, oahi_done, oalo_done = sem("ybhi_done"), sem("oahi_done"), sem("oalo_done")
    yahi_done = sem("yahi_done")
    mconv_done, xcf_done, xchi_done, xclo_done = (sem(n) for n in ("mconv_done", "xcf_done", "xchi_done", "xclo_done"))
    o_scaled, sigo_done = sem("o_scaled"), sem("sigo_done")
    dt_done, g_built, f_built, lam_sq = sem("dt_done"), sem("g_built"), sem("f_built"), sem("lam_sq")
    k_ready, k_copied, k_final, toep_clear, toep_built = (sem(n) for n in (
        "k_ready", "k_copied", "k_final", "toep_clear", "toep_built"))
    m1_ready, m1_copied = sem("m1_ready"), sem("m1_copied")
    s5in_ready, s5in_copied, scan_done = sem("s5in_ready"), sem("s5in_copied"), sem("scan_done")
    qk_ready, qk_copied, gates_ready, gates_copied, fsel_ready = (sem(n) for n in (
        "qk_ready", "qk_copied", "gates_ready", "gates_copied", "fsel_ready"))
    absf_done, expf_done, lnf_done, rows_done, sum_rows, emrow_done = (sem(n) for n in (
        "absf_done", "expf_done", "lnf_done", "rows_done", "sum_rows", "emrow_done"))
    acol_ready, acol_copied, vtok_ready, vtok_copied = (sem(n) for n in (
        "acol_ready", "acol_copied", "vtok_ready", "vtok_copied"))
    nmb_ready, emb_ready, e_done, sc_ready, w_done, w_used = (sem(n) for n in (
        "nmb_ready", "emb_ready", "e_done", "sc_ready", "w_done", "w_used"))
    hsq_done, dsq_done, num_gated, floor_done, hms_ready, hms_added, hfac_done, yb_done = (sem(n) for n in (
        "hsq_done", "dsq_done", "num_gated", "floor_done", "hms_ready", "hms_added", "hfac_done", "yb_done"))
    y_ready, y_copied, y_saved, y_back, gelu_done = (sem(n) for n in (
        "y_ready", "y_copied", "y_saved", "y_back", "gelu_done"))
    gahi_done, galo_done, glu_ready, glusig_done, ya_done = (sem(n) for n in (
        "gahi_done", "galo_done", "glu_ready", "glusig_done", "ya_done"))
    x_back = sem("x_back")
    qkv_done, vwin_ready, vwin_copied = sem("qkv_done"), sem("vwin_ready"), sem("vwin_copied")
    asc_ready, asc_read, asc_done, aexp_done, anorm_done, apt_ready, apt_copied, ao_ready, ao_copied = (sem(n) for n in (
        "asc_ready", "asc_read", "asc_done", "aexp_done", "anorm_done", "apt_ready", "apt_copied", "ao_ready", "ao_copied"))
    asum_inv = sem("asum_inv")
    out_done, out_saved = sem("out_done"), sem("out_saved")

    block = ctx.enter_context(nc.Block())

    def wait_tile_used(eng, t):
        if isinstance(t, tuple):
            eng.wait_ge(tile_used, t[1] * t[2] + used_count(t[0]))
        elif t == T_QK:
            eng.wait_ge(qk_ready, 8)
        elif t in (T_GLU, T_GLU + 1):
            eng.wait_ge(glu_ready, 2 * (t - T_GLU + 1))
        else:
            eng.wait_ge(tile_used, used_count(t))

    @block.sync
    def _(sp):
        pairs_of = wstream.rearrange("(r s) p f -> r s p f", s=RAWS)
        sp.dma_start(con[:, :, :], consts).then_inc(params_in, 16)
        sp.dma_start(prm[:, 0:NCOL], params).then_inc(params_in, 16)
        for k in range(4):
            sp.dma_start(xin[:, 2 * k:2 * k + 2, :], xT[:, 2 * k:2 * k + 2, :]).then_inc(x_in, 16)
        sp.dma_start(bcp[:, :, :], bc).then_inc(params_in, 16)
        for t in range(RAWS):
            sp.dma_start(raw[:, t, :], wstream[t]).then_inc(raw_in[t], 16)

        def load(t, s, need):
            sp.wait_ge(lo_done, need)
            sp.dma_start(raw[:, s, :], wstream[t]).then_inc(raw_in[s], 16)

        def loads(t0, t1):
            with sp.Fori(t0 // 2, t1 // 2) as r:
                need0, need1 = sp.snap(r * 2 - 1), sp.snap(r * 2)
                sp.wait_ge(lo_done, need0)
                sp.dma_start(raw[:, 0, :], pairs_of[r, 0]).then_inc(raw_in[0], 16)
                sp.wait_ge(lo_done, need1)
                sp.dma_start(raw[:, 1, :], pairs_of[r, 1]).then_inc(raw_in[1], 16)

        loads(2, 10)
        sp.wait_ge(out_freed, 4)
        sp.dma_start(u_scratch.rearrange("m p s c -> p m (s c)"), uperm[:, :, :]).then_inc(u_saved, 16)
        sp.wait_ge(u_saved, 16)
        for s in range(CH):
            src = u_scratch.rearrange("m (g i) s c -> i (m g) s c", i=GCH)[:, :, CH - 1 - s, :]
            sp.dma_start(uc[s * GCH:(s + 1) * GCH, :, :], src).then_inc(u_back, 16)
        loads(10, T_QK)
        load(T_QK, 0, T_QK - 1)
        for t in range(T_QK + 1, T_OUT + 3):
            load(t, t % RAWS, t - 1)
        sp.wait_ge(k_final, 1)
        sp.wait_ge(toep_clear, 1)
        for t in range(CH):
            sp.dma_start(toep[(CH - 1 - t) * GCH:P, t, :, :],
                         ksb[0:(t + 1) * GCH, :, :]).then_inc(toep_built, 16)
        load(T_OUT + 3, 0, T_OUT + 2)
        for half in range(2):
            sp.wait_ge(y_copied, 2 * half + 2)
            for s in range(CH):
                sp.dma_start(y_scratch.rearrange("g i s c -> s i g c")[s, :, 16 * half:16 * half + 16, :],
                             ysb[s * GCH:(s + 1) * GCH, 16 * half:16 * half + 16, :]).then_inc(y_saved, 16)
            sp.wait_ge(y_saved, 16 * CH * (half + 1))
            for m in (2 * half, 2 * half + 1):
                sp.dma_start(uperm[:, m, :], y_scratch.rearrange("(m g) i s c -> m (g i) (s c)", g=8)[m]
                             ).then_inc(y_back, 16)
        sp.wait_ge(yb_done, HEADS)
        sp.wait_ge(galo_done, 4)
        sp.dma_start(h[:, :, :], xT).then_inc(x_back, 16)
        load(T_OUT + 4, 1, T_OUT + 3)
        loads(T_OUT + 5, T_QKV + 3)
        sp.wait_ge(tile_used, used_count(T_DN[0] + 3 * KB - 1))
        sp.dma_start(bandsb[:, :, :], band).then_inc(band_in, 16)
        loads(T_QKV + 3, T_END)
        for m in range(KB):
            sp.wait_ge(out_done, m + 1)
            sp.dma_start(outT[:, m, :], outb[:, m, :]).then_inc(out_saved, 16)
        sp.wait_ge(out_saved, 16 * KB)

    @block.gpsimd
    def _(pool):
        steps = Steps(pool_step)
        G = nc.gpsimd

        def do(ins):
            steps.up(ins)

        def settle():
            pool.wait_ge(pool_step, steps.value())

        G.memset(ones[:, :], 1.0)
        G.memset(prm[:, NCOL:NCOL + 1], EPS)
        G.memset(mean_w[:, :], 1.0 / DM).then_inc(consts_set, 1)
        G.memset(xpad[:, 0:3], 0.0)
        G.memset(xs[:, :, :, 0:1], 0.0).then_inc(pads_set, 1)

        def sum_squares(first):
            for m in range(KB):
                add_square(KB * first + m, m)

        def add_square(n, m):
            pool.wait_ge(sq_done, n + 1)
            if m == 0:
                pool.wait_ge(mean_done, n // KB)
                G.tensor_copy(ssum[:, :], sq[:, m % 2, :]).then_inc(acc_done, 1)
            else:
                pool.wait_ge(acc_done, n)
                G.tensor_tensor(ssum[:, :], ssum[:, :], sq[:, m % 2, :], ALU.add).then_inc(acc_done, 1)

        pool.wait_ge(params_in, 48)
        S = [sm[:, j, :] for j in range(40)]
        lr, zr, zi, wr, wi, pr, pi, mr, mi, den, cr, ci = S[:12]
        T = S[12:16]
        li = cols("aim")

        def tt(o, a, b, op):
            do(G.tensor_tensor(o, a, b, op))

        def ts(o, a, s1, op0, s2=None, op1=ALU.bypass):
            if s2 is None:
                do(G.tensor_scalar(o, a, s1, None, op0))
            else:
                do(G.tensor_scalar(o, a, s1, s2, op0, op1))

        def cmul(orr, oi, ar, ai, br, bi, t):
            tt(t[0], ar, br, ALU.mult)
            tt(t[1], ai, bi, ALU.mult)
            tt(t[2], ar, bi, ALU.mult)
            tt(t[3], ai, br, ALU.mult)
            settle()
            tt(orr, t[0], t[1], ALU.subtract)
            tt(oi, t[2], t[3], ALU.add)
            settle()

        ts(lr, cols("are"), -1e-4, ALU.min)
        pool.wait_ge(dt_done, 1)
        settle()
        dt = S[39]
        tt(zr, lr, dt, ALU.mult)
        tt(zi, li, dt, ALU.mult)
        settle()
        ts(wr, zr, 2.0 ** -EXPM_LOG, ALU.mult)
        ts(wi, zi, 2.0 ** -EXPM_LOG, ALU.mult)
        settle()
        ts(pr, wr, 1.0 / 6, ALU.mult, 1.0, ALU.add)
        ts(pi, wi, 1.0 / 6, ALU.mult)
        settle()
        for n in (5, 4, 3, 2):
            cmul(cr, ci, wr, wi, pr, pi, T)
            ts(pr, cr, 1.0 / n, ALU.mult, 1.0, ALU.add)
            ts(pi, ci, 1.0 / n, ALU.mult)
            settle()
        cmul(mr, mi, wr, wi, pr, pi, T)
        for _ in range(EXPM_LOG):
            ts(cr, mr, 2.0, ALU.add)
            settle()
            cmul(pr, pi, mr, mi, cr, mi, T)
            ts(mr, pr, 1.0, ALU.mult)
            ts(mi, pi, 1.0, ALU.mult)
            settle()
        tt(T[0], lr, lr, ALU.mult)
        tt(T[1], li, li, ALU.mult)
        ts(wi, li, -1.0, ALU.mult)
        settle()
        G.tensor_tensor(den, T[0], T[1], ALU.add).then_inc(lam_sq, 1)
        pool.wait_ge(lam_sq, 1)
        cmul(cr, ci, mr, mi, lr, wi, T)
        pool.wait_ge(s5_recip, 1)
        tt(pr, cr, den, ALU.mult)
        tt(pi, ci, den, ALU.mult)
        ts(q_re[:, 0, :], mr, 1.0, ALU.add)
        ts(q_im[:, 0, :], mi, 1.0, ALU.mult)
        settle()

        def bro(ap, n):
            return ap.unsqueeze(1).to_broadcast([P, n, PAIRS])

        Tp = [ptmp[:, j, 0:4 * PAIRS].rearrange("p (a b) -> p a b", b=PAIRS) for j in range(4)]
        for n in (1, 2, 4):
            cmul(q_re[:, n:2 * n, :], q_im[:, n:2 * n, :], q_re[:, 0:n, :], q_im[:, 0:n, :],
                 bro(q_re[:, n - 1, :], n), bro(q_im[:, n - 1, :], n), [t[:, 0:n, :] for t in Tp])

        T3 = [ptmp[:, j, :].rearrange("p (a b) -> p a b", b=GCH) for j in range(4)]
        B = [bcp[:, j, :].rearrange("p (a b) -> p a b", b=GCH) for j in range(4)]

        def wide(ap):
            return ap.unsqueeze(2).to_broadcast([P, PAIRS, GCH])

        def step_view(tensor, s):
            return tensor[:, :, s * GCH:(s + 1) * GCH]

        cmul(step_view(gre, 0), step_view(gim, 0), B[0], B[1], wide(pr), wide(pi), T3)
        for s in range(1, CH):
            cmul(step_view(gre, s), step_view(gim, s), step_view(gre, 0), step_view(gim, 0),
                 wide(q_re[:, s - 1, :]), wide(q_im[:, s - 1, :]), T3)
        tt(T3[0], B[3], B[3], ALU.add)
        settle()
        G.tensor_tensor(B[3], B[3], T3[0], ALU.subtract).then_inc(g_built, 1)
        pool.wait_ge(g_built, 1)
        for s in range(CH):
            pw, pv = wide(q_re[:, s, :]), wide(q_im[:, s, :])
            tt(T3[0], B[2], pw, ALU.mult)
            tt(T3[1], B[3], pv, ALU.mult)
            tt(T3[2], B[3], pw, ALU.mult)
            tt(T3[3], B[2], pv, ALU.mult)
            settle()
            tt(step_view(fre, s), T3[0], T3[1], ALU.add)
            tt(step_view(fim, s), T3[2], T3[3], ALU.subtract)
            settle()
        pool.wait_ge(mean_done, 1)
        r2 = qk2[:, :, :].rearrange("p (r j) k -> p r j k", r=2)
        i2 = aj2[:, :, :].rearrange("p (r j) k -> p r j k", r=2)
        Ts = [ptmp[:, j, 0:4 * PAIRS].rearrange("p (b a) -> p b a", b=PAIRS) for j in range(4)]
        ts(r2[:, 0, :, 0], q_re[:, 7, :], 1.0, ALU.mult)
        ts(i2[:, 1, :, 0], q_im[:, 7, :], 1.0, ALU.mult)
        settle()
        for n in (1, 2, 4):
            bb = [x.to_broadcast([P, PAIRS, n]) for x in (r2[:, 0, :, n - 1:n], i2[:, 1, :, n - 1:n])]
            cmul(r2[:, 0, :, n:2 * n], i2[:, 1, :, n:2 * n], r2[:, 0, :, 0:n], i2[:, 1, :, 0:n],
                 bb[0], bb[1], [t[:, :, 0:n] for t in Ts])
        ts(r2[:, 1, :, :], r2[:, 0, :, :], 1.0, ALU.mult)
        G.tensor_scalar(i2[:, 0, :, :], i2[:, 1, :, :], -1.0, None, ALU.mult).then_inc(prep_done, 1)
        pool.wait_ge(prep_done, 1)
        settle()
        pool.wait_ge(s5in_copied, 2)
        X = [xs[:, r, :, 1:NCH + 1].rearrange("p j (s i) -> p j s i", i=SUP) for r in range(2)]
        XX = xs[:, :, :, 1:NCH + 1].rearrange("p r j (s i) -> p (r j) s i", i=SUP)

        def axpy(dst, co, prev, a, b, shape):
            tt(a, co[0].to_broadcast(shape), prev[0], ALU.mult)
            half = [shape[0], PAIRS] + list(shape[2:])
            tt(b[:, 0:PAIRS], co[1][:, 0:PAIRS].to_broadcast(half), prev[1][1], ALU.mult)
            tt(b[:, PAIRS:], co[1][:, PAIRS:].to_broadcast(half), prev[1][0], ALU.mult)
            settle()
            tt(a, a, b, ALU.add)
            settle()
            tt(dst, dst, a, ALU.add)
            settle()

        a8, b8 = st1[:, :, 0:SUP], st2[:, :, 0:SUP]
        for i in range(1, SUP):
            axpy(XX[:, :, :, i], (qk2[:, :, 0:1], aj2[:, :, 0:1]),
                 (XX[:, :, :, i - 1], (X[0][:, :, :, i - 1], X[1][:, :, :, i - 1])), a8, b8,
                 [P, 2 * PAIRS, SUP])
        a1, b1 = st1[:, :, 0:1], st2[:, :, 0:1]
        for s in range(1, SUP):
            axpy(XX[:, :, s, SUP - 1:SUP], (qk2[:, :, SUP - 1:SUP], aj2[:, :, SUP - 1:SUP]),
                 (XX[:, :, s - 1, SUP - 1:SUP], (X[0][:, :, s - 1, SUP - 1:SUP], X[1][:, :, s - 1, SUP - 1:SUP])),
                 a1, b1, [P, 2 * PAIRS, 1])
        a7, b7 = st1[:, :, 0:SUP - 1], st2[:, :, 0:SUP - 1]
        for i in range(SUP - 1):
            axpy(XX[:, :, 1:, i], (qk2[:, :, i:i + 1], aj2[:, :, i:i + 1]),
                 (XX[:, :, 0:SUP - 1, SUP - 1], (X[0][:, :, 0:SUP - 1, SUP - 1], X[1][:, :, 0:SUP - 1, SUP - 1])),
                 a7, b7, [P, 2 * PAIRS, SUP - 1])
        G.memset(xs[:, 0, :, 0:1], 0.0).then_inc(scan_done, 1)

        sum_squares(1)
        sum_squares(2)
        for w in range(2 * NC):
            p4 = pbuf[:, w % 4, :, 0:KW - 1]
            pool.wait_ge(asum_inv, w + 1)
            G.tensor_tensor(p4, p4, st[:, w % 4, 2, :].unsqueeze(2).to_broadcast([P, 4, P]),
                            ALU.mult).then_inc(anorm_done, 1)
        sum_squares(3)
        sum_squares(4)

    @block.scalar
    def _(act):
        steps = Steps(act_step)
        A = nc.scalar.activation

        def split_hi(t, i=0, per=0):
            act.wait_ge(raw_in[t % RAWS], i * (8 * per) + 16 * (t // RAWS + 1))
            if t >= RING:
                wait_tile_used(act, (t - RING, i, per) if per else t - RING)
            A(whi[:, t % RING, :], raw[:, t % RAWS, :], ACT.Copy).then_inc(hi_done, 1)

        def square(src, n, slot, i=0, per=0):
            if n >= 2:
                act.wait_ge(acc_done, i * per + n - 1)
            A(sq[:, slot, :], src, ACT.Square).then_inc(sq_done, 1)

        def root_mean_square(n):
            act.wait_ge(mean_done, n + 1)
            if n:
                act.wait_ge(out_freed, (0, O_IN + 16, O_DN[0], O_WO, O_DN[1])[n])
            A(rstd[:, :], bank[7][:, :], ACT.Sqrt, bias=prm[:, NCOL:NCOL + 1]).then_inc(rms_done, 1)

        def operand_hi(src, g):
            for m in range(KB):
                A(xhi[:, m, :], src[:, m, :], ACT.Copy, scale=col(g, m)).then_inc(xhi_done, 1)

        act.wait_ge(params_in, 48)
        A(sm[:, 39, :], cols("ldt"), ACT.Exp).then_inc(dt_done, 1)
        act.wait_ge(x_in, 64)
        operand_hi(xin, "g_mix0")
        for t in range(RING):
            split_hi(t)
        for m in range(KB):
            square(xin[:, m, :], m, m % 2)
        act.wait_ge(consts_set, 1)
        root_mean_square(0)

        for t in range(16):
            split_hi(t + RING) if t + RING <= T_OUT else None
            if 4 <= t < 8:
                m = t - 4
                act.wait_ge(mconv_done, m + 1)
                if m:
                    act.wait_ge(xclo_done, m)
                A(xcf[:, :], cacc[:, :], ACT.Silu).then_inc(xcf_done, 1)
                act.wait_ge(xcf_done, m + 1)
                A(xchi[:, m, :], xcf[:, :], ACT.Copy).then_inc(xchi_done, 1)
            if t >= 12:
                m = t - 12
                act.wait_ge(out_freed, t + 1)
                A(sigo[:, m, :], sigo[:, m, :], ACT.Sigmoid).then_inc(sigo_done, 1)
        for b in range(8):
            act.wait_ge(m1_ready, b + 1)
            dst = (m1re if b < 4 else m1im)[:, 4 * (b % 4):4 * (b % 4) + 4, :]
            A(dst, bank[5 + b % 2][:, :].rearrange("p (j q) -> p j q", q=P), ACT.Copy).then_inc(m1_copied, 1)
        for r in range(2):
            act.wait_ge(s5in_ready, r + 1)
            for k in range(2):
                ins = A(xs[:, r, 8 * k:8 * k + 8, 1:NCH + 1],
                        bank[4 + 2 * r + k][:, :].rearrange("p (j c) -> p j c", c=NCH), ACT.Copy)
            ins.then_inc(s5in_copied, 1)
        split_hi(T_QK + RING)
        for hd in range(HEADS):
            act.wait_ge(vtok_ready, hd + 1)
            A(vtok[:, hd, :, :], bank[6 + hd % 2][:, :].rearrange("p (s v) -> p s v", v=P),
              ACT.Copy).then_inc(vtok_copied, 1)
        act.wait_ge(fsel_ready, 1)
        A(lf[:, :], bank[5][0:HEADS, :], ACT.Abs).then_inc(absf_done, 1)
        act.wait_ge(absf_done, 1)
        A(lf[:, :], lf[:, :], ACT.Exp, scale=-1.0).then_inc(expf_done, 1)
        act.wait_ge(expf_done, 1)
        A(lf[:, :], lf[:, :], ACT.Ln, bias=1.0).then_inc(lnf_done, 1)
        act.wait_ge(sum_rows, 1)
        A(nmrow[:, 1, :], nmrow[:, 1, :], ACT.Exp, scale=-2.0).then_inc(emrow_done, 1)
        act.wait_ge(prep_done, 1)
        act.wait_ge(k_final, 1)

        def decay(hd, s):
            act.wait_ge(nmb_ready, hd + 1)
            if hd:
                act.wait_ge(w_done, SB * (hd - 1) + s + 1)
            A(ebuf[:, s, P * s:], bank[2][:, P * s:], ACT.Exp, bias=acol[:, s, hd:hd + 1]).then_inc(e_done, 1)

        def head_squares(hd):
            act.wait_ge(w_used, SB * (hd + 1))
            if hd:
                act.wait_ge(hms_ready, hd)
            A(hsq[:, :], bank[NUM_BANK[hd]][:, :], ACT.Square).then_inc(hsq_done, 1)
            if hd >= 2:
                act.wait_ge(yb_done, hd - 1)
            A(dsq[:, hd % 2, :], bank[NUM_BANK[hd] + 1][:, :], ACT.Square, scale=DEN_SCALE ** 0.5).then_inc(dsq_done, 1)

        def head_factor(hd):
            act.wait_ge(hms_added, hd + 1)
            steps.up(A(dsq[:, hd % 2, :], dsq[:, hd % 2, :], ACT.Ln, scale=float(DM // P)))
            act.wait_ge(act_step, steps.value())
            A(dsq[:, hd % 2, :], dsq[:, hd % 2, :], ACT.Exp, scale=-0.5).then_inc(hfac_done, 1)

        def head_hi(hd):
            act.wait_ge(o_scaled, hd + 1)
            A(xhi[:, 4 + hd, :], hb[:, hd % 2, :], ACT.Copy).then_inc(ybhi_done, 1)

        def s5_output(q):
            act.wait_ge(y_ready, q + 1)
            A(ysb[:, 16 * (q // 2) + q % 2:16 * (q // 2) + 16:2, :],
              bank[q % 2][:, :].rearrange("p (g c) -> p g c", c=NCH), ACT.Copy).then_inc(y_copied, 1)

        act.wait_ge(acol_copied, 1)
        for s in range(SB):
            decay(0, s)
        for hd in range(HEADS):
            if hd + 1 < HEADS:
                decay(hd + 1, 0)
                decay(hd + 1, 1)
            head_squares(hd)
            for q in Y_AFTER[hd]:
                s5_output(q)
            if hd + 1 < HEADS:
                decay(hd + 1, 2)
                decay(hd + 1, 3)
            head_factor(hd)
            head_hi(hd)
        act.wait_ge(y_back, 16 * 4)
        for m in range(4):
            A(uperm[:, m, :], uperm[:, m, :], ACT.Gelu_apprx_tanh).then_inc(gelu_done, 1)
        for m in range(4):
            act.wait_ge(gelu_done, m + 1)
            A(xhi[:, m, :], uperm[:, m, :], ACT.Copy).then_inc(gahi_done, 1)
        for m in range(4):
            act.wait_ge(glu_ready, m + 1)
            A(gsig[:, m, :], bank[m][:, :], ACT.Sigmoid).then_inc(glusig_done, 1)
        split_hi(T_GLU + RING)
        split_hi(T_GLU + 1 + RING)
        for m in range(4):
            act.wait_ge(out_freed, O_GLU + m + 1)
            A(xhi[:, m, :], yaf[:, m, :], ACT.Copy).then_inc(yahi_done, 1)

        def residual_squares(t0, o0, n):
            for m in range(KB):
                split_hi(t0 + m + RING)
                act.wait_ge(out_freed, o0 + m + 1)
                square(h[:, m, :], KB * n + m, m % 2)

        def mlp(l):
            t0, d0 = T_UP[l], T_DN[l]
            with act.Fori(0, FJ // 2) as i:
                for jj in range(2):
                    j = FJ * l + jj
                    split_hi(t0 + 2 * jj + RING, i, 4)
                    act.wait_ge(conv_done, i * 2 + (j + 1))
                    A(sbuf[:, :], cbuf[:, :], ACT.Silu).then_inc(silu_done, 1)
                    split_hi(t0 + 2 * jj + 1 + RING, i, 4)
                    act.wait_ge(a_done, i * 2 + (j + 1))
                    A(ahi[:, i * 2 + jj, :], abuf[:, :], ACT.Copy).then_inc(ahi_done, 1)
            n = 1 + 2 * l + 1

            def down(i, last):
                for s in range(12):
                    if not (last and s >= 8):
                        split_hi(d0 + s + RING, i, 12)
                    if s % 3 == 2:
                        act.wait_ge(out_freed, i * 4 + (O_DN[l] + s // 3 + 1))
                        square(h[:, i * 4 + s // 3, :], KB * n + s // 3, (s // 3) % 2, i, 4)

            if l == 0:
                with act.Fori(0, 2) as i:
                    down(i, False)
            else:
                down(0, False)
                down(1, True)

        residual_squares(T_OUT, O_OUT, 1)
        operand_hi(h, "g_ffn0")
        root_mean_square(1)
        mlp(0)
        operand_hi(h, "g_mix1")
        root_mean_square(2)
        for m in range(NQKV):
            split_hi(T_QKV + m + RING)
        for b in range(2):
            act.wait_ge(vwin_ready, b + 1)
            A(vwin[:, 4 * b:4 * b + 4, :], bank[4 + b][:, :].rearrange("p (c v) -> p c v", v=P),
              ACT.Copy).then_inc(vwin_copied, 1)
        for w in range(2 * NC + 3):
            if w < 2 * NC:
                act.wait_ge(asc_done, w + 1)
                if w >= 4:
                    act.wait_ge(apt_ready, w - 3)
                for j in range(4):
                    ins = A(pbuf[:, w % 4, j, :], sbuf2[:, w % 2, j, :], ACT.Exp, bias=st[:, w % 4, 0, j:j + 1],
                            accum_out=st[:, w % 4, 1, j:j + 1])
                ins.then_inc(aexp_done, 1)
            if 2 <= w <= 2 * NC + 1:
                v = w - 2
                act.wait_ge(apt_ready, v + 1)
                if v >= 2:
                    act.wait_ge(ao_ready, v - 1)
                A(ptb[:, v % 2, :], bank[(6, 0)[v % 2]][:, :], ACT.Copy).then_inc(apt_copied, 1)
            if w >= 3:
                v = w - 3
                c, kv = v // 2, v % 2
                act.wait_ge(ao_ready, v + 1)
                A(obuf[:, 4 * kv:4 * kv + 4, WIN * c:WIN * (c + 1)],
                  bank[(7, 1)[v % 2]][:, 0:4 * WIN].rearrange("p (j q) -> p j q", q=WIN),
                  ACT.Copy).then_inc(ao_copied, 1)
        act.wait_ge(ao_copied, 2 * NC)
        for m in range(KB):
            A(xhi[:, m, :], obuf[:, m, :], ACT.Copy).then_inc(oahi_done, 1)
        residual_squares(T_WO, O_WO, 3)
        operand_hi(h, "g_ffn1")
        root_mean_square(3)
        mlp(1)
        root_mean_square(4)

    @block.vector
    def _(dve):
        steps = Steps(dve_step)
        V = nc.vector

        def settle():
            dve.wait_ge(dve_step, steps.value())

        def split_lo(t, i=0, per=0):
            dve.wait_ge(hi_done, i * per + (t + 1))
            V.tensor_tensor(wlo[:, t % RING, :], raw[:, t % RAWS, :], whi[:, t % RING, :].bitcast(f32),
                            ALU.subtract).then_inc(lo_done, 1)

        def operand_lo(src, g, n, k):
            for m in range(KB):
                dve.wait_ge(xhi_done, KB * k + m + 1)
                V.scalar_tensor_tensor(out=xlo[:, m, :], in0=src[:, m, :], scalar=col(g, m),
                                       in1=xhi[:, m, :].bitcast(f32), op0=ALU.mult,
                                       op1=ALU.subtract).then_inc(xlo_done, 1)
            row_factor(n)

        def row_factor(n):
            dve.wait_ge(rms_done, n + 1)
            V.reciprocal(rstd[:, :], rstd[:, :]).then_inc(rstd_done, 1)
            dve.wait_ge(rstd_done, n + 1)

        dve.wait_ge(params_in, 48)
        dve.wait_ge(x_in, 64)
        for m in range(KB):
            dve.wait_ge(xhi_done, m + 1)
            V.scalar_tensor_tensor(out=xlo[:, m, :], in0=xin[:, m, :], scalar=col("g_mix0", m),
                                   in1=xhi[:, m, :].bitcast(f32), op0=ALU.mult,
                                   op1=ALU.subtract).then_inc(xlo_done, 1)
        for t in range(RING):
            split_lo(t)
        for m in range(KB):
            dve.wait_ge(sq_done, m + 1)
            if m:
                dve.wait_ge(acc_done, m)
                V.tensor_tensor(ssum[:, :], ssum[:, :], sq[:, m % 2, :], ALU.add).then_inc(acc_done, 1)
            else:
                V.tensor_copy(ssum[:, :], sq[:, 0, :]).then_inc(acc_done, 1)
        row_factor(0)
        dve.wait_ge(pads_set, 1)
        for t in range(16):
            wait_tile_used(dve, t)
            if t + RING <= T_OUT:
                split_lo(t + RING)
            src = bank[t % 4]
            m = t % 4
            if t < 4:
                V.tensor_tensor(uperm[:, m, :].rearrange("p (s c) -> p c s", s=CH),
                                src[:, :].rearrange("p (c s) -> p c s", s=CH),
                                rstd[:, :].rearrange("p (c s) -> p c s", s=CH), ALU.mult).then_inc(out_freed, 1)
            elif t < 8:
                V.tensor_tensor(xpad[:, 3:], src[:, :], rstd[:, :], ALU.mult).then_inc(out_freed, 1)
                dve.wait_ge(out_freed, t + 1)
                if m:
                    dve.wait_ge(xcf_done, m)
                steps.up(V.tensor_scalar(cacc[:, :], xpad[:, 3:], col("mlw", 4 * m + 3), col("mlb", m),
                                         ALU.mult, ALU.add))
                for w in (2, 1, 0):
                    settle()
                    ins = V.scalar_tensor_tensor(out=cacc[:, :], in0=xpad[:, w:w + SEQ],
                                                 scalar=col("mlw", 4 * m + w), in1=cacc[:, :],
                                                 op0=ALU.mult, op1=ALU.add)
                    if w:
                        steps.up(ins)
                ins.then_inc(mconv_done, 1)
                dve.wait_ge(xchi_done, m + 1)
                V.tensor_tensor(xclo[:, m, :], xcf[:, :], xchi[:, m, :].bitcast(f32),
                                ALU.subtract).then_inc(xclo_done, 1)
            elif t < 12:
                if m == 0:
                    dve.wait_ge(u_saved, 16)
                V.tensor_tensor(vT[:, m, :], src[:, :], rstd[:, :], ALU.mult).then_inc(out_freed, 1)
            else:
                V.tensor_tensor(sigo[:, m, :], src[:, :], rstd[:, :], ALU.mult).then_inc(out_freed, 1)
            if t == 5:
                dve.wait_ge(lam_sq, 1)
                V.reciprocal(sm[:, 9, :], sm[:, 9, :]).then_inc(s5_recip, 1)
        for b in range(8):
            dve.wait_ge(qk_ready, b + 1)
            V.tensor_copy((qT if b < 4 else kT)[:, b % 4, :], bank[b % 4][:, :]).then_inc(out_freed, 1)
        split_lo(T_QK + RING)
        dve.wait_ge(gates_ready, 1)
        V.tensor_scalar(g8[:, :], bank[4][0:8, :], col("bgate", 0, 8), None, ALU.add).then_inc(gates_copied, 1)
        dve.wait_ge(lnf_done, 1)
        steps.up(V.scalar_tensor_tensor(out=lf[:, :], in0=bank[5][0:HEADS, :], scalar=0.0, in1=lf[:, :],
                                        op0=ALU.min, op1=ALU.subtract))
        settle()
        steps.up(V.tensor_tensor_scan(fcum[:, :], ones[0:HEADS, 0:1].to_broadcast([HEADS, SEQ]), lf[:, :], 0.0,
                                      ALU.mult, ALU.add))
        settle()
        steps.up(V.tensor_tensor(arow[:, :], g8[0:HEADS, :], fcum[:, :], ALU.subtract))
        settle()
        steps.up(V.tensor_tensor_scan(lf[:, :], arow[:, :], arow[:, :], 0.0, ALU.max, ALU.max))
        settle()
        V.tensor_tensor(nmrow[:, 1, :], lf[:, :], fcum[:, :], ALU.add).then_inc(sum_rows, 1)
        V.tensor_scalar(nmrow[:, 0, :], lf[:, :], -1.0, None, ALU.mult).then_inc(rows_done, 1)
        dve.wait_ge(acol_ready, 1)
        V.tensor_copy(acol[:, :, :], bank[4][:, 0:SB * HEADS].rearrange("p (s h) -> p s h", h=HEADS)
                      ).then_inc(acol_copied, 1)
        dve.wait_ge(k_ready, 1)
        by_pair = ksb[:, :, :].rearrange("p i (j f) -> p f i j", f=2)
        for f in range(2):
            V.tensor_copy(by_pair[:, f], bank[(6, 7)[f]][:, 0:PAIRS * GCH].rearrange("p (j i) -> p i j", i=GCH)
                          ).then_inc(k_copied, 1)
        dve.wait_ge(xcf_done, HEADS)
        skip = cacc[0:GCH, :].rearrange("p (i g) -> p i g", i=GCH)
        steps.up(V.tensor_tensor(skip, ident[0:GCH, 0:GCH].unsqueeze(2).to_broadcast([GCH, GCH, GROUPS]),
                                 cols("ddiag", GCH).unsqueeze(1).to_broadcast([GCH, GCH, GROUPS]), ALU.mult))
        dve.wait_ge(k_copied, 2)
        settle()
        V.tensor_tensor(ksb[0:GCH, :, :], ksb[0:GCH, :, :], skip, ALU.add).then_inc(k_final, 1)

        def weights(k):
            hd, s = k // SB, k % SB
            dve.wait_ge(e_done, k + 1)
            diag = ebuf[:, s, P * s:P * (s + 1)]
            steps.up(V.scalar_tensor_tensor(out=diag, in0=diag, scalar=1.0, in1=tri, op0=ALU.min, op1=ALU.mult))
            settle()
            dve.wait_ge(sc_ready, k + 1)
            if k >= 2:
                dve.wait_ge(w_used, k - 1)
            V.scalar_tensor_tensor(out=wbuf[:, k % 2, 0:SEQ - P * s], in0=bank[4 + k % 2][:, 0:SEQ - P * s],
                                   scalar=float(P) ** -0.5, in1=ebuf[:, s, P * s:],
                                   op0=ALU.mult, op1=ALU.mult).then_inc(w_done, 1)

        def head_gate(hd):
            dve.wait_ge(hsq_done, hd + 1)
            V.tensor_tensor(hb[:, hd % 2, :], bank[NUM_BANK[hd]][:, :], sigo[:, hd, :], ALU.mult).then_inc(num_gated, 1)
            dve.wait_ge(emb_ready, hd + 1)
            dve.wait_ge(dsq_done, hd + 1)
            V.scalar_tensor_tensor(out=dsq[:, hd % 2, :], in0=bank[3][:, :], scalar=DEN_SCALE,
                                   in1=dsq[:, hd % 2, :], op0=ALU.mult, op1=ALU.max).then_inc(floor_done, 1)

        def head_sum(hd):
            dve.wait_ge(hms_ready, hd + 1)
            dve.wait_ge(floor_done, hd + 1)
            V.tensor_tensor(dsq[:, hd % 2, :], dsq[:, hd % 2, :], bank[3][:, :], ALU.add).then_inc(hms_added, 1)

        def head_scale(hd):
            dve.wait_ge(num_gated, hd + 1)
            dve.wait_ge(hfac_done, hd + 1)
            V.tensor_tensor(hb[:, hd % 2, :], hb[:, hd % 2, :], dsq[:, hd % 2, :], ALU.mult).then_inc(o_scaled, 1)

        def head_lo(hd):
            dve.wait_ge(ybhi_done, hd + 1)
            V.tensor_tensor(xlo[:, 4 + hd, :], hb[:, hd % 2, :], xhi[:, 4 + hd, :].bitcast(f32),
                            ALU.subtract).then_inc(yb_done, 1)

        for m in range(HEADS):
            dve.wait_ge(sigo_done, m + 1)
            steps.up(V.tensor_scalar(sigo[:, m, :], sigo[:, m, :], col("mlg", m), None, ALU.mult))
        settle()
        weights(0)
        for hd in range(HEADS):
            weights(SB * hd + 1)
            if hd == 0:
                V.memset(toep[:, :, :, :], 0.0).then_inc(toep_clear, 1)
            weights(SB * hd + 2)
            if hd:
                head_sum(hd - 1)
            weights(SB * hd + 3)
            if hd:
                head_scale(hd - 1)
            if hd + 1 < HEADS:
                weights(SB * (hd + 1))
            if hd:
                head_lo(hd - 1)
            head_gate(hd)
        head_sum(HEADS - 1)
        head_scale(HEADS - 1)
        head_lo(HEADS - 1)
        for m in range(4):
            dve.wait_ge(gahi_done, m + 1)
            V.tensor_tensor(xlo[:, m, :], uperm[:, m, :], xhi[:, m, :].bitcast(f32),
                            ALU.subtract).then_inc(galo_done, 1)
        for m in range(4):
            dve.wait_ge(glusig_done, m + 1)
            V.tensor_tensor(yaf[:, m, :].rearrange("p (c s) -> p c s", s=CH),
                            uperm[:, m, :].rearrange("p (s c) -> p c s", s=CH),
                            gsig[:, m, :].rearrange("p (s c) -> p c s", s=CH), ALU.mult).then_inc(out_freed, 1)
        split_lo(T_GLU + RING)
        split_lo(T_GLU + 1 + RING)
        for m in range(4):
            dve.wait_ge(yahi_done, m + 1)
            V.tensor_tensor(xlo[:, m, :], yaf[:, m, :], xhi[:, m, :].bitcast(f32),
                            ALU.subtract).then_inc(ya_done, 1)

        def residual(t0, o0):
            for m in range(KB):
                wait_tile_used(dve, t0 + m)
                split_lo(t0 + m + RING)
                V.tensor_tensor(h[:, m, :], h[:, m, :], bank[(o0 + m) % 4][:, :], ALU.add).then_inc(out_freed, 1)
            dve.wait_ge(out_freed, o0 + KB)

        def mlp(l):
            t0, d0, fw = T_UP[l], T_DN[l], "fw%d" % l
            V.memset(gpad[:, 0:2], 0.0)
            with dve.Fori(0, FJ // 2) as i:
                steps.enter(i, 4)
                for jj in range(2):
                    j = FJ * l + jj

                    def tap(k):
                        o = COLS[fw][0] + FJ * k + jj
                        return prm[:, bass.ds(i * 2 + o, 1)]

                    wait_tile_used(dve, (t0 + 2 * jj, i, 4))
                    split_lo(t0 + 2 * jj + RING, i, 4)
                    V.tensor_tensor(gpad[:, 2:], bank[(O_UP[l] + 2 * jj) % 4][:, :], rstd[:, :],
                                    ALU.mult).then_inc(out_freed, 1)
                    dve.wait_ge(out_freed, i * 4 + (O_UP[l] + 2 * jj + 1))
                    if j:
                        dve.wait_ge(silu_done, i * 2 + j)
                    steps.up(V.tensor_scalar(cbuf[:, :], gpad[:, 2:], tap(2), tap(3), ALU.mult, ALU.add))
                    settle()
                    steps.up(V.scalar_tensor_tensor(out=cbuf[:, :], in0=gpad[:, 1:1 + SEQ], scalar=tap(1),
                                                    in1=cbuf[:, :], op0=ALU.mult, op1=ALU.add))
                    settle()
                    V.scalar_tensor_tensor(out=cbuf[:, :], in0=gpad[:, 0:SEQ], scalar=tap(0),
                                           in1=cbuf[:, :], op0=ALU.mult, op1=ALU.add).then_inc(conv_done, 1)
                    wait_tile_used(dve, (t0 + 2 * jj + 1, i, 4))
                    split_lo(t0 + 2 * jj + 1 + RING, i, 4)
                    V.tensor_tensor(vbuf[:, :], bank[(O_UP[l] + 2 * jj + 1) % 4][:, :], rstd[:, :],
                                    ALU.mult).then_inc(out_freed, 1)
                    dve.wait_ge(out_freed, i * 4 + (O_UP[l] + 2 * jj + 2))
                    dve.wait_ge(silu_done, i * 2 + (j + 1))
                    V.tensor_tensor(abuf[:, :], vbuf[:, :], sbuf[:, :], ALU.mult).then_inc(a_done, 1)
                    dve.wait_ge(ahi_done, i * 2 + (j + 1))
                    V.tensor_tensor(alo[:, i * 2 + jj, :], abuf[:, :], ahi[:, i * 2 + jj, :].bitcast(f32),
                                    ALU.subtract).then_inc(alo_done, 1)
            steps.leave(FJ // 2)

            def down(i, last):
                for s in range(12):
                    wait_tile_used(dve, (d0 + s, i, 12))
                    if not (last and s >= 8):
                        split_lo(d0 + s + RING, i, 12)
                    if s % 3 == 2:
                        m = s // 3
                        V.tensor_tensor(h[:, i * 4 + m, :], h[:, i * 4 + m, :], bank[(O_DN[l] + m) % 4][:, :],
                                        ALU.add).then_inc(out_freed, 1)

            if l == 0:
                with dve.Fori(0, 2) as i:
                    down(i, False)
            else:
                down(0, False)
                down(1, True)
            dve.wait_ge(out_freed, O_DN[l] + KB)

        dve.wait_ge(x_back, 16)
        residual(T_OUT, O_OUT)
        operand_lo(h, "g_ffn0", 1, 1)
        mlp(0)
        operand_lo(h, "g_mix1", 2, 2)
        V.memset(akd[:, :, 0:WIN], 0.0)
        steps.up(V.memset(avT[:, 0:WIN], 0.0))
        for m in range(NQKV):
            wait_tile_used(dve, T_QKV + m)
            split_lo(T_QKV + m + RING)
            dst = aq[:, m, :] if m < 8 else akd[:, m - 8, WIN:] if m < 10 else avT[:, WIN:]
            V.tensor_tensor(dst, bank[(O_QKV + m) % 4][:, :], rstd[:, :], ALU.mult).then_inc(out_freed, 1)
            dve.wait_ge(out_freed, O_QKV + m + 1)
            V.tensor_scalar(dst, dst, col("bqkv", m), None, ALU.add).then_inc(qkv_done, 1)
        dve.wait_ge(band_in, 16)
        for kv in range(2):
            steps.up(V.tensor_copy(sbuf2[:, kv, :, KW - 1], cols("sink")[:, 4 * kv:4 * kv + 4]))

        def scores(w):
            c, kv = w // 2, w % 2
            s4 = sbuf2[:, w % 2, :, 0:KW - 1]
            nmx = st[:, w % 4, 0, :]
            dve.wait_ge(asc_ready, w + 1)
            if w >= 2:
                dve.wait_ge(aexp_done, w - 1)
            V.scalar_tensor_tensor(
                out=s4, in0=bank[4 + w % 2][:, :].rearrange("p (j k) -> p j k", k=P), scalar=float(AHD) ** -0.5,
                in1=bandsb[:, 4 * kv:4 * kv + 4, :], op0=ALU.mult, op1=ALU.add).then_inc(asc_read, 1)
            dve.wait_ge(asc_read, w + 1)
            if c == 0:
                steps.up(V.memset(s4[:, :, 0:WIN], -1e30))
                settle()
            if w == 0:
                settle()
            steps.up(V.tensor_reduce(nmx, sbuf2[:, w % 2, :, :], AX.X, ALU.max))
            settle()
            V.tensor_scalar(nmx, nmx, -1.0, None, ALU.mult).then_inc(asc_done, 1)

        def invert(w):
            dve.wait_ge(aexp_done, w + 1)
            V.reciprocal(st[:, w % 4, 2, :], st[:, w % 4, 1, :]).then_inc(asum_inv, 1)

        for w in range(2 * NC + 1):
            if w < 2 * NC:
                scores(w)
            if w:
                invert(w - 1)
        for m in range(KB):
            dve.wait_ge(oahi_done, m + 1)
            V.tensor_tensor(xlo[:, m, :], obuf[:, m, :], xhi[:, m, :].bitcast(f32),
                            ALU.subtract).then_inc(oalo_done, 1)
        residual(T_WO, O_WO)
        operand_lo(h, "g_ffn1", 3, 3)
        mlp(1)
        row_factor(4)
        for m in range(KB):
            V.scalar_tensor_tensor(out=outb[:, m, :], in0=h[:, m, :], scalar=col("g_fin", m), in1=rstd[:, :],
                                   op0=ALU.mult, op1=ALU.mult).then_inc(out_done, 1)

    @block.tensor
    def _(pe):
        MM = nc.tensor.matmul

        def block3(dst, slot, b, rhi, rlo, start, stop):
            wh, wl = whi[:, slot, b * P:(b + 1) * P], wlo[:, slot, b * P:(b + 1) * P]
            MM(dst, wh, rhi, start=start, stop=False)
            MM(dst, wh, rlo, start=False, stop=False)
            return MM(dst, wl, rhi, start=False, stop=stop)

        def product(t, o, i=0, per=0):
            pe.wait_ge(lo_done, i * per + (t + 1))
            if o >= 4:
                pe.wait_ge(out_freed, i * per + (o - 3))
            for b in range(KB):
                ins = block3(bank[o % 4][:, :], t % RING, b, xhi[:, b, :], xlo[:, b, :], b == 0, b == KB - 1)
            ins.then_inc(tile_used, 1)

        def mean(n):
            pe.wait_ge(acc_done, KB * (n + 1))
            MM(bank[7][:, :], mean_w[:, :], ssum[:, :], start=True, stop=True).then_inc(mean_done, 1)

        def transpose(dst, src, k):
            return nc.tensor.transpose(dst, src, ident[0:k, 0:k])

        pe.wait_ge(params_in, 48)
        pe.wait_ge(consts_set, 1)
        pe.wait_ge(xlo_done, KB)
        for t in range(16):
            product(t, t)
            if t == 2:
                mean(0)
        pe.wait_ge(g_built, 1)
        for b in range(8):
            if b >= 2:
                pe.wait_ge(m1_copied, b - 1)
            for k in range(4):
                ins = transpose(bank[5 + b % 2][:, k * P:(k + 1) * P],
                                (gre if b < 4 else gim)[:, 4 * (b % 4) + k, :], P)
            ins.then_inc(m1_ready, 1)
        pe.wait_ge(m1_copied, 8)
        pe.wait_ge(u_back, 16 * CH)
        pe.wait_ge(rstd_done, 1)
        for r, m1 in enumerate((m1re, m1im)):
            for g in list(range(0, GROUPS, 2)) + list(range(1, GROUPS, 2)):
                p0, j = STATE * (g % 2), g // 2
                ins = MM(bank[4 + 2 * r + j // 8][p0:p0 + STATE, (j % 8) * NCH:(j % 8 + 1) * NCH],
                         m1[:, j, p0:p0 + STATE], uc[:, g, :], start=True, stop=True)
            ins.then_inc(s5in_ready, 1)
        pe.wait_ge(lo_done, T_QK + 1)
        pe.wait_ge(xclo_done, HEADS)
        for b in range(8):
            pe.wait_ge(out_freed, O_QK + b - 3)
            block3(bank[b % 4][:, :], T_QK % RING, b, xchi[:, b % 4, :], xclo[:, b % 4, :], True,
                   True).then_inc(qk_ready, 1)
        pe.wait_ge(s5in_copied, 2)
        for hd in range(HEADS):
            if hd >= 2:
                pe.wait_ge(vtok_copied, hd - 1)
            for s in range(SB):
                ins = transpose(bank[6 + hd % 2][:, s * P:(s + 1) * P], vT[:, hd, s * P:(s + 1) * P], P)
            ins.then_inc(vtok_ready, 1)
        pe.wait_ge(out_freed, O_QK + 8)
        for k in range(12):
            ins = MM(bank[4][0:8, :], cols("wg")[:, 8 * k:8 * k + 8], (qT, kT, vT)[k % 3][:, k // 3, :],
                     start=k == 0, stop=k == 11)
        ins.then_inc(gates_ready, 1)
        pe.wait_ge(gates_copied, 1)
        MM(bank[5][0:HEADS, :], ident[0:8, HEADS:8], g8[:, :], start=True, stop=True).then_inc(fsel_ready, 1)
        pe.wait_ge(vtok_copied, HEADS)
        for f in range(2):
            r = slice(STATE * f, STATE * f + STATE)
            for j in range(PAIRS):
                dst = bank[(6, 7)[f]][:, j * GCH:(j + 1) * GCH]
                MM(dst, gre[r, j, :], bcp[r, 2, j * GCH:(j + 1) * GCH], start=True, stop=False)
                ins = MM(dst, gim[r, j, :], bcp[r, 3, j * GCH:(j + 1) * GCH], start=False, stop=True)
        ins.then_inc(k_ready, 1)
        pe.wait_ge(rows_done, 1)
        for s in range(SB):
            ins = transpose(bank[4][:, s * HEADS:(s + 1) * HEADS], arow[:, s * P:(s + 1) * P], HEADS)
        ins.then_inc(acol_ready, 1)

        def broadcast_row(hd, row):
            pick = ident[0:HEADS, hd:hd + 1].to_broadcast([HEADS, P])
            if row == 0:
                pe.wait_ge(e_done, SB * hd) if hd else None
            else:
                pe.wait_ge(hms_added, hd) if hd else None
            MM(bank[2 + row][:, :], pick, nmrow[:, row, :], start=True, stop=True).then_inc(
                (nmb_ready, emb_ready)[row], 1)

        def head_scores(k):
            hd, s = k // SB, k % SB
            if k >= 2:
                pe.wait_ge(w_done, k - 1)
            MM(bank[4 + k % 2][:, 0:SEQ - P * s], kT[:, hd, s * P:(s + 1) * P], qT[:, hd, s * P:],
               start=True, stop=True).then_inc(sc_ready, 1)

        def mean_square(hd):
            pe.wait_ge(hsq_done, hd + 1)
            pe.wait_ge(floor_done, hd + 1)
            MM(bank[3][:, :], mean_w[:, :], hsq[:, :], start=True, stop=True).then_inc(hms_ready, 1)

        def s5_output(q):
            pe.wait_ge(toep_built, 16 * CH)
            if q >= 2:
                pe.wait_ge(y_copied, q - 1)
            pairs = range(8 * (q // 2), 8 * (q // 2) + 8)
            r = slice(STATE * (q % 2), STATE * (q % 2) + STATE)
            dst = {j: bank[q % 2][:, (j % 8) * NCH:(j % 8 + 1) * NCH] for j in pairs}
            for j in pairs:
                g = 2 * j + q % 2
                MM(dst[j], toep[:, :, :, g].rearrange("p s i -> p (s i)"), uc[:, g, :], start=j == pairs[0], stop=False)
            pe.wait_ge(scan_done, 1)
            for j in pairs:
                MM(dst[j], fre[r, j, :], xs[r, 0, j, 0:NCH], start=False, stop=False)
                ins = MM(dst[j], fim[r, j, :], xs[r, 1, j, 0:NCH], start=False, stop=j == pairs[-1])
            ins.then_inc(y_ready, 1)

        broadcast_row(0, 0)
        pe.wait_ge(k_copied, 2)
        head_scores(0)
        head_scores(1)
        pe.wait_ge(emrow_done, 1)
        for hd in range(HEADS):
            for s in range(SB):
                k = SB * hd + s
                before = (0, 0, 1, 3)[hd]
                if s == 0 and before:
                    pe.wait_ge(num_gated, before)
                    pe.wait_ge(dsq_done, before)
                pe.wait_ge(w_done, k + 1)
                w = wbuf[:, k % 2, 0:SEQ - P * s]
                MM(bank[NUM_BANK[hd]][:, P * s:], vtok[:, hd, s, :], w, start=s == 0, stop=s == SB - 1)
                MM(bank[NUM_BANK[hd] + 1][:, P * s:], ones[:, :], w, start=s == 0, stop=s == SB - 1).then_inc(w_used, 1)
                if k + 2 < SB * HEADS:
                    head_scores(k + 2)
                if s == 0 and hd:
                    mean_square(hd - 1)
                if s == 2:
                    if hd + 1 < HEADS:
                        broadcast_row(hd + 1, 0)
                    broadcast_row(hd, 1)
            for q in Y_AFTER[hd]:
                s5_output(q)
        mean_square(HEADS - 1)
        pe.wait_ge(galo_done, 4)
        for m in range(4):
            t = T_GLU + m // 2
            pe.wait_ge(lo_done, t + 1)
            for b in range(4):
                ins = block3(bank[m][:, :], t % RING, 4 * (m % 2) + b, xhi[:, b, :], xlo[:, b, :], b == 0, b == 3)
            ins.then_inc(glu_ready, 1)
        pe.wait_ge(ya_done, 4)
        pe.wait_ge(yb_done, HEADS)
        for m in range(KB):
            product(T_OUT + m, O_OUT + m)

        def mlp(l):
            mean(1 + 2 * l)
            pe.wait_ge(xlo_done, KB * (2 + 2 * l))
            with pe.Fori(0, FJ // 2) as i:
                for s in range(4):
                    product(T_UP[l] + s, O_UP[l] + s, i, 4)
            with pe.Fori(0, 2) as i:
                for m in range(4):
                    pe.wait_ge(out_freed, i * 4 + (O_DN[l] + m - 3))
                    for part in range(3):
                        t = T_DN[l] + 3 * m + part
                        pe.wait_ge(lo_done, i * 12 + (t + 1))
                        ks = (range(0, 8), range(8, 15), range(15, FJ))[part]
                        for k in ks:
                            if k == 0 or k == FJ - 2:
                                pe.wait_ge(alo_done, FJ * (l + 1) - (2 if k == 0 else 0))
                            ins = block3(bank[(O_DN[l] + m) % 4][:, :], t % RING, k - ks[0], ahi[:, k, :],
                                         alo[:, k, :], k == 0, k == FJ - 1)
                        ins.then_inc(tile_used, 1)

        mlp(0)
        mean(2)
        pe.wait_ge(xlo_done, 3 * KB)
        for m in range(NQKV):
            product(T_QKV + m, O_QKV + m)
        pe.wait_ge(qkv_done, NQKV)
        for b in range(2):
            for k in range(4):
                c = 4 * b + k
                ins = transpose(bank[4 + b][:, k * P:(k + 1) * P], avT[:, c * WIN:c * WIN + P], P)
            ins.then_inc(vwin_ready, 1)
        pe.wait_ge(vwin_copied, 2)
        for w in range(2 * NC + 3):
            if w < 2 * NC:
                c, kv = w // 2, w % 2
                if w >= 2:
                    pe.wait_ge(asc_read, w - 1)
                for hf in range(2):
                    for j in range(4):
                        r = slice(AHD * hf, AHD * hf + AHD)
                        ins = MM(bank[4 + w % 2][r, j * P:(j + 1) * P],
                                 aq[r, 4 * kv + j, WIN * c:WIN * (c + 1)], akd[r, kv, WIN * c:WIN * c + P],
                                 start=True, stop=True)
                ins.then_inc(asc_ready, 1)
            if 2 <= w <= 2 * NC + 1:
                v = w - 2
                pe.wait_ge(anorm_done, v + 1)
                if v >= 2:
                    pe.wait_ge(apt_copied, v - 1)
                for j in range(4):
                    ins = transpose(bank[(6, 0)[v % 2]][:, j * P:(j + 1) * P], pbuf[:, v % 4, j, 0:P], P)
                ins.then_inc(apt_ready, 1)
            if w >= 3:
                v = w - 3
                c, kv = v // 2, v % 2
                pe.wait_ge(apt_copied, v + 1)
                if v >= 2:
                    pe.wait_ge(ao_copied, v - 1)
                p4 = ptb[:, v % 2, :].rearrange("p (j f q) -> p j f q", f=2, q=WIN)
                for hf in range(2):
                    ins = MM(bank[(7, 1)[v % 2]][AHD * hf:AHD * hf + AHD, 0:4 * WIN],
                             vwin[:, c, AHD * kv:AHD * kv + AHD], p4[:, :, hf, :], start=True, stop=True)
                ins.then_inc(ao_ready, 1)
        pe.wait_ge(oalo_done, KB)
        for m in range(KB):
            product(T_WO + m, O_WO + m)
        mlp(1)
        mean(4)

    ctx.close()


def _tile(w):
    k = w.shape[0] // P
    return w.reshape(k, P, P).transpose(1, 0, 2).reshape(P, k * P)


def _tiles(w):
    return [_tile(w[:, c:c + P]) for c in range(0, w.shape[1], P)]


def _columns(v):
    return v.reshape(-1, P).T


def _bucket():
    rel = (np.arange(2 * WIN)[None, :] - WIN) - np.arange(WIN)[:, None]
    n = np.abs(rel)
    scaled = np.log(np.maximum(n, 1) / 8) / np.log(128 / 8) * 8
    large = np.minimum(8 + scaled.astype(np.int32), 15)
    return (rel > 0).astype(np.int32) * 16 + np.where(n < 8, n, large)


def kernel(**inputs):
    import concourse.bacc as bacc
    from concourse.bass_utils import run_bass_kernel_spmd

    a = {k: np.asarray(v) for k, v in inputs.items()}
    f32 = np.float32
    stream = _tiles(a["ab_w_in"][0])
    blocks = [a["ml_w_q"][0][h] for h in range(HEADS)] + [a["ml_w_k"][0][h] for h in range(HEADS)]
    stream.append(np.concatenate(blocks, axis=1))
    glu = _tiles(a["s5_w_glu"][0])
    stream += [np.concatenate(glu[2 * k:2 * k + 2], axis=1) for k in range(2)]
    stream += _tiles(a["ab_w_out"][0])

    def mlp(l):
        up = _tiles(a["ffn_w_up"][l])
        out = []
        for j in range(FJ):
            out += [up[j], up[FJ + j]]
        for w in _tiles(a["ffn_w_down"][l]):
            for k0, k1 in ((0, 8), (8, 15), (15, FJ)):
                part = w[:, k0 * P:k1 * P]
                out.append(np.concatenate([part, np.zeros((P, (8 - k1 + k0) * P), f32)], axis=1))
        return out

    stream += mlp(0)
    wqkv = a["swa_w_qkv"][0]
    bqkv = a["swa_b_qkv"][0]
    nq = QH * AHD
    order = np.concatenate([np.arange(nq), nq + np.tile(np.arange(AHD), 2), nq + AHD + np.tile(np.arange(AHD), 2),
                            nq + 2 * AHD + np.arange(2 * AHD)])
    stream += _tiles(wqkv[:, order])
    stream += _tiles(a["swa_w_o"][0])
    stream += mlp(1)
    assert len(stream) == T_END
    wstream = np.ascontiguousarray(np.stack(stream))

    def pairs(v):
        v = v.reshape((PAIRS, P) + v.shape[2:])
        return np.moveaxis(v, 0, 1)

    prm = np.zeros((P, NCOL), f32)

    def put(name, v):
        o, n = COLS[name]
        assert v.shape[1] == n, name
        prm[:v.shape[0], o:o + n] = v

    put("g_mix0", _columns(a["norm_mix_g"][0]))
    put("g_mix1", _columns(a["norm_mix_g"][1]))
    put("g_ffn0", _columns(a["norm_ffn_g"][0]))
    put("g_ffn1", _columns(a["norm_ffn_g"][1]))
    put("g_fin", _columns(a["norm_final_g"]))
    for l in range(2):
        put("fw%d" % l, np.concatenate([_columns(a["ffn_conv_w"][l][k]) for k in range(3)]
                                       + [_columns(a["ffn_conv_b"][l])], axis=1))
    put("mlw", np.stack([_columns(a["ml_conv_w"][0][k]) for k in range(4)], axis=2).reshape(P, 4 * HEADS))
    put("mlb", _columns(a["ml_conv_b"][0]))
    put("mlg", _columns(a["ml_norm_g"][0]))
    put("bqkv", _columns(bqkv[order]))
    put("sink", np.repeat(a["swa_sinks"][0].reshape(QH // 2, 2).T, WIN, axis=0))
    put("bgate", a["ml_b_gates"][0].reshape(8, 1))
    put("ddiag", a["s5_d"][0].reshape(GROUPS, GCH).T)
    put("ldt", pairs(np.repeat(a["s5_log_dt"][0][:, None], STATE, axis=1)))
    put("are", pairs(a["s5_a_re"][0]))
    put("aim", pairs(a["s5_a_im"][0]))
    put("wg", a["ml_w_gates"][0].reshape(12, P, 8).transpose(1, 0, 2).reshape(P, 96))
    bc = np.stack([pairs(a["s5_b_re"][0]), pairs(a["s5_b_im"][0]),
                   pairs(a["s5_c_re"][0].transpose(0, 2, 1)), pairs(a["s5_c_im"][0].transpose(0, 2, 1))], axis=1)
    bc = np.ascontiguousarray(bc.reshape(P, 4, PAIRS * GCH))
    consts = np.stack([np.eye(P, dtype=f32), np.triu(np.ones((P, P), f32))], axis=1)
    band = a["rel_bias"][_bucket()]
    band = band.transpose(2, 0, 1).reshape(QH // 2, 2 * WIN, 2 * WIN).transpose(1, 0, 2)
    xT = a["x"][0].T.reshape(KB, P, SEQ).transpose(1, 0, 2)

    nc = bacc.Bacc("TRN2", target_bir_lowering=False, num_devices=1)
    dt = mybir.dt.float32
    arrays = {"wstream": wstream, "xT": xT, "params": prm, "bc": bc, "consts": consts, "band": band}
    arrays = {k: np.ascontiguousarray(v) for k, v in arrays.items()}
    aps = {k: nc.dram_tensor(k, v.shape, dt, kind="ExternalInput").ap() for k, v in arrays.items()}
    outT = nc.dram_tensor("outT", (P, KB, SEQ), dt, kind="ExternalOutput").ap()
    u_scratch = nc.dram_tensor("u_scratch", (4, P, CH, NCH), dt, kind="Internal").ap()
    y_scratch = nc.dram_tensor("y_scratch", (GROUPS, GCH, CH, NCH), dt, kind="Internal").ap()
    build(nc, **aps, outT=outT, u_scratch=u_scratch, y_scratch=y_scratch)
    r = run_bass_kernel_spmd(nc, [arrays], core_ids=[0])
    out = r.results[0]["outT"]
    return np.ascontiguousarray(out.transpose(2, 1, 0).reshape(1, SEQ, DM))
```

```python
from contextlib import ExitStack

import numpy as np

import concourse.bass as bass
from concourse import mybir

P = 128
SEQ = 512
DM = 1024
KB = DM // P
D_FF = 2816
FJ = D_FF // P
HEADS = 4
SB = SEQ // P
GROUPS, GCH, STATE = 32, 16, 64
PAIRS = GROUPS // 2
CH = P // GCH
NCH = SEQ // CH
SUP = 8
QH, AHD, WIN = 16, 64, 64
NC = SEQ // WIN
KW = 2 * WIN + 1
EPS = 1e-6
DEN_SCALE = EPS * P / DM
NUM_BANK = (6, 0, 6, 6)
Y_AFTER = ((), (), (0, 1), (2, 3))
EXPM_LOG = 10

T_IN, T_QK = 0, 16
T_YB = 17
T_GLU = 19
T_YA = 21
T_OUT = 23
T_UP = [27, 113]
T_DN = [T_UP[0] + 2 * FJ, T_UP[1] + 2 * FJ]
T_QKV = T_DN[0] + 3 * KB
NQKV = 10
T_WO = T_QKV + NQKV
T_END = T_DN[1] + 3 * KB
assert T_WO + KB == T_UP[1] and T_END % 2 == 1
O_IN, O_QK, O_GLU, O_OUT = 0, 16, 24, 28
O_UP = [36, 106]
O_DN = [O_UP[0] + 2 * FJ, O_UP[1] + 2 * FJ]
O_QKV = O_DN[0] + KB
O_WO = O_QKV + NQKV
assert O_WO + KB == O_UP[1]
RAWS, RING = 2, 4

COLS = {}


def _col(name, n):
    COLS[name] = (sum(w for _, w in COLS.values()), n)


for _n, _w in (("g_mix0", KB), ("g_ffn0", KB), ("g_mix1", KB), ("g_ffn1", KB), ("g_fin", KB),
               ("fw0", 4 * FJ), ("fw1", 4 * FJ), ("mlw", 4 * HEADS), ("mlb", HEADS), ("mlg", HEADS),
               ("bqkv", NQKV), ("sink", QH // 2), ("bgate", 1), ("ddiag", GROUPS),
               ("ldt", PAIRS), ("are", PAIRS), ("aim", PAIRS), ("wg", 12 * 8)):
    _col(_n, _w)
NCOL = sum(w for _, w in COLS.values())


OUT_TILES = [T_YA, T_YA, T_YA + 1, T_YA + 1] + [T_OUT + k for k in range(4)]
OUT_SPLITS = [None, T_YA + RING, None, T_YA + 1 + RING] + [T_OUT + k + RING for k in range(4)]
WO_TILES = [T_WO + m for m in range(KB)]
WO_SPLITS = [T_WO + m + RING for m in range(KB)]


def used_count(t):
    return t + 1 if t < T_QK else t if t < T_GLU else t - 2


class Steps:

    def __init__(self, sem):
        self.sem, self.n, self.i, self.per = sem, 0, None, 0

    def up(self, ins):
        ins.then_inc(self.sem, 1)
        self.n += 1

    def value(self):
        return self.n if self.i is None else self.i * self.per + self.n

    def enter(self, i, per):
        self.i, self.per, self.base = i, per, self.n

    def leave(self, iters):
        assert self.n - self.base == self.per, (self.n - self.base, self.per)
        self.i, self.n = None, self.base + self.per * iters


def build(nc, wstream, xT, params, bc, consts, band, outT, u_scratch, y_scratch):
    f32, f32r = mybir.dt.float32, mybir.dt.float32r
    ACT, ALU, AX = mybir.ActivationFunctionType, mybir.AluOpType, mybir.AxisListType
    ctx = ExitStack()

    def sem(name):
        return ctx.enter_context(nc.semaphore(name))

    top = [nc.sbuf_base + (-nc.sbuf_base) % 64]

    def at(name, shape, offset, dt=f32):
        return nc.alloc_sbuf_tensor_at(name, shape, dt, offset=offset)

    def size(shape):
        return (int(np.prod(shape[1:])) * 4 + 63) // 64 * 64

    def sb(name, shape, dt=f32):
        o = top[0]
        top[0] += size(shape)
        return at(name, shape, o, dt)

    raw = sb("raw", [P, RAWS, 8 * P])
    whi = sb("whi", [P, RING, 8 * P], f32r)
    wlo = sb("wlo", [P, RING, 8 * P], f32r)
    xn_at = top[0]
    xhi = sb("xhi", [P, KB, SEQ], f32r)
    xlo = sb("xlo", [P, KB, SEQ], f32r)
    con = sb("con", [P, 2, P])
    ident, tri = con[:, 0, :], con[:, 1, :]
    ones = sb("ones", [P, P])
    mean_w = sb("mean_w", [P, P])
    rstd = sb("rstd", [P, SEQ])
    sq = sb("sq", [P, 2, SEQ])
    ssum_at = top[0]
    ssum = sb("ssum", [P, SEQ])
    warm = sb("warm", [P, 1])
    prm = sb("prm", [P, NCOL + 1])

    def col(name, j=0, parts=P):
        o = COLS[name][0] + j
        return prm[0:parts, o:o + 1]

    def cols(name, parts=P):
        o, n = COLS[name]
        return prm[0:parts, o:o + n]

    base = top[0]
    end = nc.sbuf_usable_end

    def plan(*items, start=base):
        o, out = start, []
        for name, shape, dt in items:
            out.append(at(name, shape, o, dt))
            o += size(shape)
        assert o <= end, (items[0][0], o - end)
        return out

    h_at = end - size([P, KB, SEQ]) - (end - size([P, KB, SEQ])) % 64
    h = at("h", [P, KB, SEQ], h_at)
    ahi, alo, gpad, cbuf, sbuf, vbuf, abuf = plan(
        ("ahi", [P, FJ, SEQ], f32r), ("alo", [P, FJ, SEQ], f32r), ("gpad", [P, 2 + SEQ], f32),
        ("cbuf", [P, SEQ], f32), ("sbuf", [P, SEQ], f32), ("vbuf", [P, SEQ], f32), ("abuf", [P, SEQ], f32))
    assert base + 2 * size([P, FJ, SEQ]) + 5 * 2112 <= h_at
    F2 = [P, PAIRS, P]
    (fre, fim, gre, gim, m1re, m1im, uc, uperm, xchi, xclo, sigo, xs, ksb) = plan(
        ("fre", F2, f32), ("fim", F2, f32), ("gre", F2, f32), ("gim", F2, f32),
        ("m1re", F2, f32), ("m1im", F2, f32), ("uc", [P, GROUPS, NCH], f32), ("uperm", [P, 4, SEQ], f32),
        ("xchi", [P, 4, SEQ], f32r), ("xclo", [P, 4, SEQ], f32r), ("sigo", [P, 4, SEQ], f32),
        ("xs", [P, 2, PAIRS, NCH + 1], f32), ("ksb", [P, GCH, GROUPS], f32))
    o0 = base + 6 * size(F2) + 3 * 8192
    toep = at("toep", [P, CH, GCH, GROUPS], base + 2 * size(F2))
    xin = at("xin", [P, KB, SEQ], base + 4 * size(F2))
    qT = at("qT", [P, HEADS, SEQ], base + 4 * size(F2))
    kT = at("kT", [P, HEADS, SEQ], base + 5 * size(F2))
    vT = at("vT", [P, HEADS, SEQ], base + 6 * size(F2) + 8192)
    vtok = at("vtok", [P, HEADS, SB, P], base + 6 * size(F2) + 16384)
    yaf = at("yaf", [P, 4, SEQ], base + 6 * size(F2) + 16384)
    ysb = at("ysb", [P, GROUPS, NCH], base + 6 * size(F2) + 24576)
    gsig = at("gsig", [P, 4, SEQ], base + 6 * size(F2) + 24576)
    tail = base + 6 * size(F2) + 6 * 8192 + size([P, 2, PAIRS, NCH + 1]) + 2048
    ebuf, wbuf, hb = plan(
        ("ebuf", [P, SB, SEQ], f32), ("wbuf", [P, 2, SEQ], f32), ("hb", [P, 2, SEQ], f32), start=tail)
    bcp, xpad, cacc, xcf, ptmp, sm = plan(
        ("bcp", [P, 4, PAIRS * GCH], f32), ("xpad", [P, 3 + SEQ], f32), ("cacc", [P, SEQ], f32),
        ("xcf", [P, SEQ], f32), ("ptmp", [P, 4, 256], f32), ("sm", [P, 40, PAIRS], f32), start=tail)
    s5x_at = tail + 4096 + 2112 + 4096 + 4096 + 2560
    q_re, q_im = plan(("q_re", [P, SUP, PAIRS], f32), ("q_im", [P, SUP, PAIRS], f32),
                      start=s5x_at)
    keep_at = s5x_at + 1024
    acol, = plan(("acol", [P, SB, HEADS], f32), start=keep_at)
    qk2, aj2 = plan(("qk2", [P, 2 * PAIRS, SUP], f32), ("aj2", [P, 2 * PAIRS, SUP], f32), start=ssum_at)
    st1 = at("st1", [P, 2 * PAIRS, SUP], xn_at)
    st2 = at("st2", [P, 2 * PAIRS, SUP], xn_at + 1024)
    cdiag = at("cdiag", [P, 2, PAIRS, 2, GCH], xn_at + 4 * 2048)
    XD = [P, 2, PAIRS // 2, 2, NCH]
    xdiag = [at("xdiag0", XD, base + 6 * size(F2) + 8192), at("xdiag1", XD, xn_at + 8 * 2048)]
    hsq = at("hsq", [P, SEQ], xn_at + 2048)
    dsq = at("dsq", [P, 2, SEQ], xn_at + 2 * 2048)
    g8 = at("g8", [8, SEQ], xn_at + 6 * 2048)
    lf = at("lf", [HEADS, SEQ], xn_at + 7 * 2048)
    fcum = at("fcum", [HEADS, SEQ], xn_at + 14 * 2048)
    arow = at("arow", [HEADS, SEQ], xn_at + 15 * 2048)
    nmrow = at("nmrow", [HEADS, 2, SEQ], ssum_at - 4096)
    (aq, akd, avT, vwin, bandsb, sbuf2, pbuf, ptb, obuf, st) = plan(
        ("aq", [P, 8, SEQ], f32), ("akd", [P, 2, WIN + SEQ], f32), ("avT", [P, WIN + SEQ], f32),
        ("vwin", [P, NC, P], f32), ("bandsb", [P, 8, P], f32), ("sbuf2", [P, 2, 4, KW], f32),
        ("pbuf", [P, 4, 4, KW], f32), ("ptb", [P, 2, SEQ], f32), ("obuf", [P, 8, SEQ], f32),
        ("st", [P, 4, 3, 4], f32))
    assert base + 16384 + 2 * 2304 + 2304 + 2 * 4096 + 8 * 4096 + 16384 <= h_at
    outb = at("outb", [P, KB, SEQ], base)

    bank = [ctx.enter_context(nc.psum_tensor(f"bank{b}", [P, SEQ], f32)) for b in range(8)]

    raw_in = [sem(f"raw_in{s}") for s in range(RAWS)]
    hi_done, lo_done = sem("hi_done"), sem("lo_done")
    tile_used = sem("tile_used")
    out_freed = sem("out_freed")
    params_in, bc_in, band_in = sem("params_in"), sem("bc_in"), sem("band_in")
    x_in = [sem(f"x_in{k}") for k in range(4)]
    consts_set = sem("consts_set")
    pads_set = sem("pads_set")
    sq_done, acc_done = sem("sq_done"), sem("acc_done")
    mean_done, rstd_done, rms_done = sem("mean_done"), sem("rstd_done"), sem("rms_done")
    xhi_done, xlo_done = sem("xhi_done"), sem("xlo_done")
    dve_step, act_step, pool_step = sem("dve_step"), sem("act_step"), sem("pool_step")
    conv_done, silu_done, a_done, ahi_done, alo_done = (sem(n) for n in (
        "conv_done", "silu_done", "a_done", "ahi_done", "alo_done"))
    u_saved, u_back = sem("u_saved"), sem("u_back")
    s5_recip, prep_done = sem("s5_recip"), sem("prep_done")
    ybhi_done, oahi_done, oalo_done = sem("ybhi_done"), sem("oahi_done"), sem("oalo_done")
    yahi_done = sem("yahi_done")
    mconv_done, xcf_done, xchi_done, xclo_done = (sem(n) for n in ("mconv_done", "xcf_done", "xchi_done", "xclo_done"))
    o_scaled, sigo_done = sem("o_scaled"), sem("sigo_done")
    dt_done, g_built, lam_sq = sem("dt_done"), sem("g_built"), sem("lam_sq")
    k_ready, k_copied, k_final, toep_clear, toep_built = (sem(n) for n in (
        "k_ready", "k_copied", "k_final", "toep_clear", "toep_built"))
    m1_ready, m1_copied = sem("m1_ready"), sem("m1_copied")
    s5in_ready, s5in_copied, scan_done = sem("s5in_ready"), sem("s5in_copied"), sem("scan_done")
    qk_ready, gates_ready, gates_copied, fsel_ready = (sem(n) for n in (
        "qk_ready", "gates_ready", "gates_copied", "fsel_ready"))
    absf_done, expf_done, lnf_done, rows_done, sum_rows, emrow_done = (sem(n) for n in (
        "absf_done", "expf_done", "lnf_done", "rows_done", "sum_rows", "emrow_done"))
    acol_ready, acol_copied, vtok_ready, vtok_copied = (sem(n) for n in (
        "acol_ready", "acol_copied", "vtok_ready", "vtok_copied"))
    nmb_ready, emb_ready, e_done, sc_ready, w_done, w_used = (sem(n) for n in (
        "nmb_ready", "emb_ready", "e_done", "sc_ready", "w_done", "w_used"))
    hsq_done, dsq_done, num_gated, floor_done, hms_ready, hms_added, hfac_done, yb_done = (sem(n) for n in (
        "hsq_done", "dsq_done", "num_gated", "floor_done", "hms_ready", "hms_added", "hfac_done", "yb_done"))
    y_ready, y_copied, y_saved, y_back, gelu_done = (sem(n) for n in (
        "y_ready", "y_copied", "y_saved", "y_back", "gelu_done"))
    gahi_done, galo_done, glu_ready, glusig_done, ya_done = (sem(n) for n in (
        "gahi_done", "galo_done", "glu_ready", "glusig_done", "ya_done"))
    x_back, cdiag_set, xdiag_zero, xdiag_set = (sem(n) for n in (
        "x_back", "cdiag_set", "xdiag_zero", "xdiag_set"))
    kdup_in = sem("kdup_in")
    qkv_done, vwin_ready, vwin_copied = sem("qkv_done"), sem("vwin_ready"), sem("vwin_copied")
    asc_ready, asc_read, asc_done, aexp_done, anorm_done, apt_ready, apt_copied, ao_ready, ao_copied = (sem(n) for n in (
        "asc_ready", "asc_read", "asc_done", "aexp_done", "anorm_done", "apt_ready", "apt_copied", "ao_ready", "ao_copied"))
    asum_inv = sem("asum_inv")
    out_done, out_saved = sem("out_done"), sem("out_saved")

    block = ctx.enter_context(nc.Block())

    def wait_tile_used(eng, t):
        if isinstance(t, tuple):
            eng.wait_ge(tile_used, t[1] * t[2] + used_count(t[0]))
        elif t == T_QK:
            eng.wait_ge(qk_ready, 8)
        elif t in (T_GLU, T_GLU + 1):
            eng.wait_ge(glu_ready, 2 * (t - T_GLU + 1))
        else:
            eng.wait_ge(tile_used, used_count(t))

    @block.sync
    def _(sp):
        pairs_of = wstream[0:T_END - 1].rearrange("(r s) p f -> r s p f", s=RAWS)
        sp.dma_start(con[:, :, :], consts).then_inc(params_in, 16)
        sp.dma_start(prm[:, 0:NCOL], params).then_inc(params_in, 16)
        for k in range(4):
            sp.dma_start(xin[:, 2 * k:2 * k + 2, :], xT[:, 2 * k:2 * k + 2, :]).then_inc(x_in[k], 16)
            if k in (0, 1):
                sp.dma_start(raw[:, k, :], wstream[k]).then_inc(raw_in[k], 16)
        sp.dma_start(bcp[:, :, :], bc).then_inc(bc_in, 16)

        def load(t, s, need):
            sp.wait_ge(lo_done, need)
            sp.dma_start(raw[:, s, :], wstream[t]).then_inc(raw_in[s], 16)

        def loads(t0, t1):
            with sp.Fori(t0 // 2, t1 // 2) as r:
                need0, need1 = sp.snap(r * 2 - 1), sp.snap(r * 2)
                sp.wait_ge(lo_done, need0)
                sp.dma_start(raw[:, 0, :], pairs_of[r, 0]).then_inc(raw_in[0], 16)
                sp.wait_ge(lo_done, need1)
                sp.dma_start(raw[:, 1, :], pairs_of[r, 1]).then_inc(raw_in[1], 16)

        loads(2, 10)
        sp.wait_ge(out_freed, 4)
        sp.dma_start(u_scratch.rearrange("m p s c -> p m (s c)"), uperm[:, :, :]).then_inc(u_saved, 16)
        sp.wait_ge(u_saved, 16)
        for s in range(CH):
            src = u_scratch.rearrange("m (g i) s c -> i (m g) s c", i=GCH)[:, :, CH - 1 - s, :]
            sp.dma_start(uc[s * GCH:(s + 1) * GCH, :, :], src).then_inc(u_back, 16)
        loads(10, T_QK)
        load(T_QK, 0, T_QK - 1)
        for t in range(T_QK + 1, T_YA + 1):
            load(t, t % RAWS, t - 1)
        sp.wait_ge(k_final, 1)
        sp.wait_ge(toep_clear, 1)
        for t in range(CH):
            sp.dma_start(toep[(CH - 1 - t) * GCH:P, t, :, :],
                         ksb[0:(t + 1) * GCH, :, :]).then_inc(toep_built, 16)
        load(T_YA + 1, 0, T_YA)
        for half in range(2):
            sp.wait_ge(y_copied, 2 * half + 2)
            for s in range(CH):
                sp.dma_start(y_scratch.rearrange("g i s c -> s i g c")[s, :, 16 * half:16 * half + 16, :],
                             ysb[s * GCH:(s + 1) * GCH, 16 * half:16 * half + 16, :]).then_inc(y_saved, 16)
            sp.wait_ge(y_saved, 16 * CH * (half + 1))
            for m in (2 * half, 2 * half + 1):
                sp.dma_start(uperm[:, m, :], y_scratch.rearrange("(m g) i s c -> m (g i) (s c)", g=8)[m]
                             ).then_inc(y_back, 16)
        sp.wait_ge(yb_done, HEADS)
        sp.wait_ge(galo_done, 4)
        sp.dma_start(h[:, :, :], xT).then_inc(x_back, 16)
        load(T_OUT, 1, T_OUT - 1)
        loads(T_OUT + 1, T_QKV + 5)
        sp.wait_ge(tile_used, used_count(T_DN[0] + 3 * KB - 1))
        sp.dma_start(bandsb[:, :, :], band).then_inc(band_in, 16)
        loads(T_QKV + 5, T_QKV + 7)
        sp.wait_ge(qkv_done, 1)
        sp.dma_start(akd[AHD:P, 0, WIN:], akd[0:AHD, 0, WIN:]).then_inc(kdup_in, 16)
        sp.dma_start(akd[0:AHD, 1, WIN:], akd[AHD:P, 1, WIN:]).then_inc(kdup_in, 16)
        loads(T_QKV + 7, T_END - 1)
        load(T_END - 1, 0, T_END - 2)
        for m in range(KB):
            sp.wait_ge(out_done, m + 1)
            sp.dma_start(outT[:, m, :], outb[:, m, :]).then_inc(out_saved, 16)
        sp.wait_ge(out_saved, 16 * KB)

    @block.gpsimd
    def _(pool):
        steps = Steps(pool_step)
        G = nc.gpsimd

        def do(ins):
            steps.up(ins)

        def settle():
            pool.wait_ge(pool_step, steps.value())

        G.memset(ones[:, :], 1.0)
        G.memset(prm[:, NCOL:NCOL + 1], EPS)
        G.memset(mean_w[:, :], 1.0 / DM).then_inc(consts_set, 1)
        G.memset(xpad[:, 0:3], 0.0)
        G.memset(xs[:, :, :, 0:1], 0.0).then_inc(pads_set, 1)

        def sum_squares(first):
            for m in range(KB):
                add_square(KB * first + m, m)

        def add_square(n, m):
            pool.wait_ge(sq_done, n + 1)
            if m == 0:
                pool.wait_ge(mean_done, n // KB)
                G.tensor_copy(ssum[:, :], sq[:, m % 2, :]).then_inc(acc_done, 1)
            else:
                pool.wait_ge(acc_done, n)
                G.tensor_tensor(ssum[:, :], ssum[:, :], sq[:, m % 2, :], ALU.add).then_inc(acc_done, 1)

        pool.wait_ge(params_in, 32)
        pool.wait_ge(bc_in, 16)
        S = [sm[:, j, :] for j in range(40)]
        lr, zr, zi, wr, wi, pr, pi, mr, mi, den, cr, ci = S[:12]
        T = S[12:16]
        li = cols("aim")

        def tt(o, a, b, op):
            do(G.tensor_tensor(o, a, b, op))

        def ts(o, a, s1, op0, s2=None, op1=ALU.bypass):
            if s2 is None:
                do(G.tensor_scalar(o, a, s1, None, op0))
            else:
                do(G.tensor_scalar(o, a, s1, s2, op0, op1))

        def cmul(orr, oi, ar, ai, br, bi, t):
            tt(t[0], ar, br, ALU.mult)
            tt(t[1], ai, bi, ALU.mult)
            tt(t[2], ar, bi, ALU.mult)
            tt(t[3], ai, br, ALU.mult)
            settle()
            tt(orr, t[0], t[1], ALU.subtract)
            tt(oi, t[2], t[3], ALU.add)
            settle()

        ts(lr, cols("are"), -1e-4, ALU.min)
        pool.wait_ge(dt_done, 1)
        settle()
        dt = S[39]
        tt(zr, lr, dt, ALU.mult)
        tt(zi, li, dt, ALU.mult)
        settle()
        ts(wr, zr, 2.0 ** -EXPM_LOG, ALU.mult)
        ts(wi, zi, 2.0 ** -EXPM_LOG, ALU.mult)
        settle()
        ts(pr, wr, 1.0 / 6, ALU.mult, 1.0, ALU.add)
        ts(pi, wi, 1.0 / 6, ALU.mult)
        settle()
        for n in (5, 4, 3, 2):
            cmul(cr, ci, wr, wi, pr, pi, T)
            ts(pr, cr, 1.0 / n, ALU.mult, 1.0, ALU.add)
            ts(pi, ci, 1.0 / n, ALU.mult)
            settle()
        cmul(mr, mi, wr, wi, pr, pi, T)
        for _ in range(EXPM_LOG):
            ts(cr, mr, 2.0, ALU.add)
            settle()
            cmul(pr, pi, mr, mi, cr, mi, T)
            ts(mr, pr, 1.0, ALU.mult)
            ts(mi, pi, 1.0, ALU.mult)
            settle()
        tt(T[0], lr, lr, ALU.mult)
        tt(T[1], li, li, ALU.mult)
        ts(wi, li, -1.0, ALU.mult)
        settle()
        G.tensor_tensor(den, T[0], T[1], ALU.add).then_inc(lam_sq, 1)
        pool.wait_ge(lam_sq, 1)
        cmul(cr, ci, mr, mi, lr, wi, T)
        pool.wait_ge(s5_recip, 1)
        tt(pr, cr, den, ALU.mult)
        tt(pi, ci, den, ALU.mult)
        ts(q_re[:, 0, :], mr, 1.0, ALU.add)
        ts(q_im[:, 0, :], mi, 1.0, ALU.mult)
        settle()

        def bro(ap, n):
            return ap.unsqueeze(1).to_broadcast([P, n, PAIRS])

        Tp = [ptmp[:, j, 0:4 * PAIRS].rearrange("p (a b) -> p a b", b=PAIRS) for j in range(4)]
        for n in (1, 2, 4):
            cmul(q_re[:, n:2 * n, :], q_im[:, n:2 * n, :], q_re[:, 0:n, :], q_im[:, 0:n, :],
                 bro(q_re[:, n - 1, :], n), bro(q_im[:, n - 1, :], n), [t[:, 0:n, :] for t in Tp])

        T3 = [ptmp[:, j, :].rearrange("p (a b) -> p a b", b=GCH) for j in range(4)]
        B = [bcp[:, j, :].rearrange("p (a b) -> p a b", b=GCH) for j in range(4)]

        def wide(ap):
            return ap.unsqueeze(2).to_broadcast([P, PAIRS, GCH])

        def step_view(tensor, s):
            return tensor[:, :, s * GCH:(s + 1) * GCH]

        cmul(step_view(gre, 0), step_view(gim, 0), B[0], B[1], wide(pr), wide(pi), T3)
        for s in range(1, CH):
            cmul(step_view(gre, s), step_view(gim, s), step_view(gre, 0), step_view(gim, 0),
                 wide(q_re[:, s - 1, :]), wide(q_im[:, s - 1, :]), T3)
        tt(T3[0], B[3], B[3], ALU.add)
        settle()
        G.tensor_tensor(B[3], B[3], T3[0], ALU.subtract).then_inc(g_built, 1)
        pool.wait_ge(g_built, 1)
        pool.wait_ge(mean_done, 1)
        r2 = qk2[:, :, :].rearrange("p (r j) k -> p r j k", r=2)
        i2 = aj2[:, :, :].rearrange("p (r j) k -> p r j k", r=2)
        Ts = [ptmp[:, j, 0:4 * PAIRS].rearrange("p (b a) -> p b a", b=PAIRS) for j in range(4)]
        ts(r2[:, 0, :, 0], q_re[:, 7, :], 1.0, ALU.mult)
        ts(i2[:, 1, :, 0], q_im[:, 7, :], 1.0, ALU.mult)
        settle()
        for n in (1, 2, 4):
            bb = [x.to_broadcast([P, PAIRS, n]) for x in (r2[:, 0, :, n - 1:n], i2[:, 1, :, n - 1:n])]
            cmul(r2[:, 0, :, n:2 * n], i2[:, 1, :, n:2 * n], r2[:, 0, :, 0:n], i2[:, 1, :, 0:n],
                 bb[0], bb[1], [t[:, :, 0:n] for t in Ts])
        ts(r2[:, 1, :, :], r2[:, 0, :, :], 1.0, ALU.mult)
        G.tensor_scalar(i2[:, 0, :, :], i2[:, 1, :, :], -1.0, None, ALU.mult).then_inc(prep_done, 1)
        pool.wait_ge(prep_done, 1)
        settle()
        pool.wait_ge(s5in_copied, 2)
        X = [xs[:, r, :, 1:NCH + 1].rearrange("p j (s i) -> p j s i", i=SUP) for r in range(2)]
        XX = xs[:, :, :, 1:NCH + 1].rearrange("p r j (s i) -> p (r j) s i", i=SUP)

        def axpy(dst, co, prev, a, b, shape):
            tt(a, co[0].to_broadcast(shape), prev[0], ALU.mult)
            half = [shape[0], PAIRS] + list(shape[2:])
            tt(b[:, 0:PAIRS], co[1][:, 0:PAIRS].to_broadcast(half), prev[1][1], ALU.mult)
            tt(b[:, PAIRS:], co[1][:, PAIRS:].to_broadcast(half), prev[1][0], ALU.mult)
            settle()
            tt(a, a, b, ALU.add)
            settle()
            tt(dst, dst, a, ALU.add)
            settle()

        a8, b8 = st1[:, :, 0:SUP], st2[:, :, 0:SUP]
        for i in range(1, SUP):
            axpy(XX[:, :, :, i], (qk2[:, :, 0:1], aj2[:, :, 0:1]),
                 (XX[:, :, :, i - 1], (X[0][:, :, :, i - 1], X[1][:, :, :, i - 1])), a8, b8,
                 [P, 2 * PAIRS, SUP])
        G.memset(xdiag[1][:, :, :, :, :], 0.0)
        pool.wait_ge(vtok_ready, HEADS)
        pool.wait_ge(gates_ready, 1)
        G.memset(xdiag[0][:, :, :, :, :], 0.0).then_inc(xdiag_zero, 1)
        a1, b1 = st1[:, :, 0:1], st2[:, :, 0:1]
        for s in range(1, SUP):
            axpy(XX[:, :, s, SUP - 1:SUP], (qk2[:, :, SUP - 1:SUP], aj2[:, :, SUP - 1:SUP]),
                 (XX[:, :, s - 1, SUP - 1:SUP], (X[0][:, :, s - 1, SUP - 1:SUP], X[1][:, :, s - 1, SUP - 1:SUP])),
                 a1, b1, [P, 2 * PAIRS, 1])
        a7, b7 = st1[:, :, 0:SUP - 1], st2[:, :, 0:SUP - 1]
        for i in range(SUP - 1):
            axpy(XX[:, :, 1:, i], (qk2[:, :, i:i + 1], aj2[:, :, i:i + 1]),
                 (XX[:, :, 0:SUP - 1, SUP - 1], (X[0][:, :, 0:SUP - 1, SUP - 1], X[1][:, :, 0:SUP - 1, SUP - 1])),
                 a7, b7, [P, 2 * PAIRS, SUP - 1])
        G.memset(xs[:, 0, :, 0:1], 0.0).then_inc(scan_done, 1)

        sum_squares(1)
        sum_squares(2)
        for w in range(2 * NC):
            p4 = pbuf[:, w % 4, :, 0:KW - 1]
            pool.wait_ge(asum_inv, w + 1)
            G.tensor_tensor(p4, p4, st[:, w % 4, 2, :].unsqueeze(2).to_broadcast([P, 4, P]),
                            ALU.mult).then_inc(anorm_done, 1)
        sum_squares(3)
        sum_squares(4)

    @block.scalar
    def _(act):
        steps = Steps(act_step)
        A = nc.scalar.activation

        def split_hi(t, i=0, per=0):
            act.wait_ge(raw_in[t % RAWS], i * (8 * per) + 16 * (t // RAWS + 1))
            if t >= RING:
                wait_tile_used(act, (t - RING, i, per) if per else t - RING)
            A(whi[:, t % RING, :], raw[:, t % RAWS, :], ACT.Copy).then_inc(hi_done, 1)

        def square(src, n, slot, i=0, per=0):
            if n >= 2:
                act.wait_ge(acc_done, i * per + n - 1)
            A(sq[:, slot, :], src, ACT.Square).then_inc(sq_done, 1)

        def root_mean_square(n):
            A(warm[:, :], prm[:, NCOL:NCOL + 1], ACT.Sqrt)
            act.wait_ge(mean_done, n + 1)
            if n:
                act.wait_ge(out_freed, (0, O_IN + 16, O_DN[0], O_WO, O_DN[1])[n])
            A(rstd[:, :], bank[7][:, :], ACT.Sqrt, bias=prm[:, NCOL:NCOL + 1]).then_inc(rms_done, 1)

        def operand_hi(src, g):
            for m in range(KB):
                A(xhi[:, m, :], src[:, m, :], ACT.Copy, scale=col(g, m)).then_inc(xhi_done, 1)

        act.wait_ge(params_in, 32)
        act.wait_ge(consts_set, 1)
        for m in range(KB):
            act.wait_ge(x_in[m // 2], 16)
            A(xhi[:, m, :], xin[:, m, :], ACT.Copy, scale=col("g_mix0", m)).then_inc(xhi_done, 1)
            if m == 1:
                split_hi(0)
        for t in range(1, RING):
            split_hi(t)
        A(sm[:, 39, :], cols("ldt"), ACT.Exp).then_inc(dt_done, 1)
        for m in range(KB):
            square(xin[:, m, :], m, m % 2)
        root_mean_square(0)

        for t in range(16):
            split_hi(t + RING)
            if 4 <= t < 8:
                m = t - 4
                act.wait_ge(mconv_done, m + 1)
                if m:
                    act.wait_ge(xclo_done, m)
                A(xcf[:, :], cacc[:, :], ACT.Silu).then_inc(xcf_done, 1)
                act.wait_ge(xcf_done, m + 1)
                A(xchi[:, m, :], xcf[:, :], ACT.Copy).then_inc(xchi_done, 1)
            if t >= 12:
                m = t - 12
                act.wait_ge(out_freed, t + 1)
                A(sigo[:, m, :], sigo[:, m, :], ACT.Sigmoid).then_inc(sigo_done, 1)
        for b in range(8):
            act.wait_ge(m1_ready, b + 1)
            dst = (m1re if b < 4 else m1im)[:, 4 * (b % 4):4 * (b % 4) + 4, :]
            A(dst, bank[5 + b % 2][:, :].rearrange("p (j q) -> p j q", q=P), ACT.Copy).then_inc(m1_copied, 1)
        for r in range(2):
            act.wait_ge(s5in_ready, r + 1)
            for k in range(2):
                ins = A(xs[:, r, 8 * k:8 * k + 8, 1:NCH + 1],
                        bank[4 + 2 * r + k][:, :].rearrange("p (j c) -> p j c", c=NCH), ACT.Copy)
            ins.then_inc(s5in_copied, 1)
        split_hi(T_QK + RING)
        for hd in range(HEADS):
            act.wait_ge(vtok_ready, hd + 1)
            A(vtok[:, hd, :, :], bank[6 + hd % 2][:, :].rearrange("p (s v) -> p s v", v=P),
              ACT.Copy).then_inc(vtok_copied, 1)
        act.wait_ge(fsel_ready, 1)
        A(lf[:, :], bank[5][0:HEADS, :], ACT.Abs).then_inc(absf_done, 1)
        act.wait_ge(absf_done, 1)
        A(lf[:, :], lf[:, :], ACT.Exp, scale=-1.0).then_inc(expf_done, 1)
        act.wait_ge(expf_done, 1)
        A(lf[:, :], lf[:, :], ACT.Ln, bias=1.0).then_inc(lnf_done, 1)
        act.wait_ge(sum_rows, 1)
        A(nmrow[:, 1, :], nmrow[:, 1, :], ACT.Exp, scale=-2.0).then_inc(emrow_done, 1)
        act.wait_ge(prep_done, 1)
        act.wait_ge(k_final, 1)

        def decay(hd, s):
            act.wait_ge(nmb_ready, hd + 1)
            if hd:
                act.wait_ge(w_done, SB * (hd - 1) + s + 1)
            A(ebuf[:, s, P * s:], bank[2][:, P * s:], ACT.Exp, bias=acol[:, s, hd:hd + 1]).then_inc(e_done, 1)

        def head_squares(hd):
            act.wait_ge(w_used, SB * (hd + 1))
            if hd:
                act.wait_ge(hms_ready, hd)
            A(hsq[:, :], bank[NUM_BANK[hd]][:, :], ACT.Square).then_inc(hsq_done, 1)
            if hd >= 2:
                act.wait_ge(yb_done, hd - 1)
            A(dsq[:, hd % 2, :], bank[NUM_BANK[hd] + 1][:, :], ACT.Square, scale=DEN_SCALE ** 0.5).then_inc(dsq_done, 1)

        def head_factor(hd):
            act.wait_ge(hms_added, hd + 1)
            steps.up(A(dsq[:, hd % 2, :], dsq[:, hd % 2, :], ACT.Ln, scale=float(DM // P)))
            act.wait_ge(act_step, steps.value())
            A(dsq[:, hd % 2, :], dsq[:, hd % 2, :], ACT.Exp, scale=-0.5).then_inc(hfac_done, 1)

        def head_hi(hd):
            act.wait_ge(o_scaled, hd + 1)
            A(xhi[:, 4 + hd, :], hb[:, hd % 2, :], ACT.Copy).then_inc(ybhi_done, 1)

        def s5_output(q):
            act.wait_ge(y_ready, q + 1)
            A(ysb[:, 8 * q:8 * q + 8, :],
              bank[q % 2][:, :].rearrange("p (g c) -> p g c", c=NCH), ACT.Copy).then_inc(y_copied, 1)

        def s5_states():
            act.wait_ge(scan_done, 1)
            act.wait_ge(xdiag_zero, 1)
            for half in range(2):
                for r in range(2):
                    A(xdiag[half][0:STATE, r, :, 0, :], xs[0:STATE, r, 8 * half:8 * half + 8, 0:NCH],
                      ACT.Copy).then_inc(xdiag_set, 1)

        act.wait_ge(acol_copied, 1)
        for s in range(SB):
            decay(0, s)
        for hd in range(HEADS):
            if hd + 1 < HEADS:
                decay(hd + 1, 0)
                decay(hd + 1, 1)
            head_squares(hd)
            if hd == 1:
                s5_states()
            if hd + 1 < HEADS:
                for q in Y_AFTER[hd]:
                    s5_output(q)
                decay(hd + 1, 2)
                decay(hd + 1, 3)
                head_factor(hd)
                head_hi(hd)
        s5_output(2)
        head_factor(HEADS - 1)
        head_hi(HEADS - 1)
        s5_output(3)
        for half in range(2):
            act.wait_ge(y_back, 16 * 2 * (half + 1))
            for m in (2 * half, 2 * half + 1):
                A(uperm[:, m, :], uperm[:, m, :], ACT.Gelu_apprx_tanh).then_inc(gelu_done, 1)
            for m in (2 * half, 2 * half + 1):
                act.wait_ge(gelu_done, m + 1)
                A(xhi[:, m, :], uperm[:, m, :], ACT.Copy).then_inc(gahi_done, 1)
        for half in range(2):
            split_hi(T_YA + half)

        def gate(m):
            act.wait_ge(glu_ready, m + 1)
            A(gsig[:, m, :], bank[4 + m][:, :], ACT.Sigmoid).then_inc(glusig_done, 1)

        def gated_hi(m):
            act.wait_ge(out_freed, O_GLU + m + 1)
            A(xhi[:, m, :], yaf[:, m, :], ACT.Copy).then_inc(yahi_done, 1)

        for m in range(3):
            gate(m)
        act.wait_ge(glu_ready, 4)
        for m in range(3):
            gated_hi(m)
        gate(3)
        gated_hi(3)
        for t in (T_GLU, T_GLU + 1):
            split_hi(t + RING)

        def residual_squares(splits, o0, n, g):
            for m in range(KB):
                if m < KB - 1 and splits[m]:
                    split_hi(splits[m])
                act.wait_ge(out_freed, o0 + m + 1)
                if m == KB - 1:
                    operand_hi(h, g)
                square(h[:, m, :], KB * n + m, m % 2)
            split_hi(splits[-1])

        def mlp(l):
            t0, d0 = T_UP[l], T_DN[l]
            with act.Fori(0, FJ // 2) as i:
                for jj in range(2):
                    j = FJ * l + jj
                    split_hi(t0 + 2 * jj + RING, i, 4)
                    split_hi(t0 + 2 * jj + 1 + RING, i, 4)
                    act.wait_ge(conv_done, i * 2 + (j + 1))
                    A(sbuf[:, :], cbuf[:, :], ACT.Silu).then_inc(silu_done, 1)
                    act.wait_ge(a_done, i * 2 + (j + 1))
                    A(ahi[:, i * 2 + jj, :], abuf[:, :], ACT.Copy).then_inc(ahi_done, 1)
            n = 1 + 2 * l + 1

            def down(i, last):
                for s in range(12):
                    if not (last and s >= 8):
                        split_hi(d0 + s + RING, i, 12)
                    if s % 3 == 2:
                        m = s // 3
                        act.wait_ge(out_freed, i * 4 + (O_DN[l] + m + 1))
                        square(h[:, i * 4 + s // 3, :], KB * n + s // 3, (s // 3) % 2, i, 4)
                        if l == 0:
                            o = COLS["g_mix1"][0] + m
                            A(xhi[:, i * 4 + m, :], h[:, i * 4 + m, :], ACT.Copy,
                              scale=prm[:, bass.ds(i * 4 + o, 1)]).then_inc(xhi_done, 1)

            if l == 0:
                with act.Fori(0, 2) as i:
                    down(i, False)
            else:
                down(0, False)
                down(1, True)

        residual_squares(OUT_SPLITS, O_OUT, 1, "g_ffn0")
        root_mean_square(1)
        mlp(0)
        root_mean_square(2)
        for m in range(NQKV):
            split_hi(T_QKV + m + RING)
        for b in range(2):
            act.wait_ge(vwin_ready, b + 1)
            A(vwin[:, 4 * b:4 * b + 4, :], bank[4 + b][:, :].rearrange("p (c v) -> p c v", v=P),
              ACT.Copy).then_inc(vwin_copied, 1)
        for w in range(2 * NC + 3):
            if w < 2 * NC:
                act.wait_ge(asc_done, w + 1)
                if w >= 4:
                    act.wait_ge(apt_ready, w - 3)
                for j in range(4):
                    ins = A(pbuf[:, w % 4, j, :], sbuf2[:, w % 2, j, :], ACT.Exp, bias=st[:, w % 4, 0, j:j + 1],
                            accum_out=st[:, w % 4, 1, j:j + 1])
                ins.then_inc(aexp_done, 1)
            if 2 <= w <= 2 * NC + 1:
                v = w - 2
                act.wait_ge(apt_ready, v + 1)
                if v >= 2:
                    act.wait_ge(ao_ready, v - 1)
                A(ptb[:, v % 2, :], bank[(6, 0)[v % 2]][:, :], ACT.Copy).then_inc(apt_copied, 1)
            if w >= 3:
                v = w - 3
                c, kv = v // 2, v % 2
                if v == 2 * NC - 1:
                    act.wait_ge(ao_copied, v)
                    for m in range(4):
                        A(xhi[:, m, :], obuf[:, m, :], ACT.Copy).then_inc(oahi_done, 1)
                act.wait_ge(ao_ready, v + 1)
                A(obuf[:, 4 * kv:4 * kv + 4, WIN * c:WIN * (c + 1)],
                  bank[(7, 1)[v % 2]][:, 0:4 * WIN].rearrange("p (j q) -> p j q", q=WIN),
                  ACT.Copy).then_inc(ao_copied, 1)
        act.wait_ge(ao_copied, 2 * NC)
        for m in range(4, KB):
            A(xhi[:, m, :], obuf[:, m, :], ACT.Copy).then_inc(oahi_done, 1)
        residual_squares(WO_SPLITS, O_WO, 3, "g_ffn1")
        root_mean_square(3)
        mlp(1)
        root_mean_square(4)

    @block.vector
    def _(dve):
        steps = Steps(dve_step)
        V = nc.vector

        def settle():
            dve.wait_ge(dve_step, steps.value())

        def split_lo(t, i=0, per=0):
            dve.wait_ge(hi_done, i * per + (t + 1))
            V.tensor_tensor(wlo[:, t % RING, :], raw[:, t % RAWS, :], whi[:, t % RING, :].bitcast(f32),
                            ALU.subtract).then_inc(lo_done, 1)

        def operand_lo(src, g, k):
            for m in range(KB):
                dve.wait_ge(xhi_done, KB * k + m + 1)
                V.scalar_tensor_tensor(out=xlo[:, m, :], in0=src[:, m, :], scalar=col(g, m),
                                       in1=xhi[:, m, :].bitcast(f32), op0=ALU.mult,
                                       op1=ALU.subtract).then_inc(xlo_done, 1)

        def row_factor(n):
            dve.wait_ge(rms_done, n + 1)
            V.reciprocal(rstd[:, :], rstd[:, :]).then_inc(rstd_done, 1)
            dve.wait_ge(rstd_done, n + 1)

        dve.wait_ge(params_in, 32)
        for m in range(KB):
            dve.wait_ge(x_in[m // 2], 16)
            dve.wait_ge(xhi_done, m + 1)
            V.scalar_tensor_tensor(out=xlo[:, m, :], in0=xin[:, m, :], scalar=col("g_mix0", m),
                                   in1=xhi[:, m, :].bitcast(f32), op0=ALU.mult,
                                   op1=ALU.subtract).then_inc(xlo_done, 1)
            if m == 1:
                split_lo(0)
        for t in range(1, RING):
            split_lo(t)
        for m in range(KB):
            dve.wait_ge(sq_done, m + 1)
            if m:
                dve.wait_ge(acc_done, m)
                V.tensor_tensor(ssum[:, :], ssum[:, :], sq[:, m % 2, :], ALU.add).then_inc(acc_done, 1)
            else:
                V.tensor_copy(ssum[:, :], sq[:, 0, :]).then_inc(acc_done, 1)
        row_factor(0)
        dve.wait_ge(pads_set, 1)
        for t in range(16):
            wait_tile_used(dve, t)
            split_lo(t + RING)
            src = bank[t % 4]
            m = t % 4
            if t < 4:
                V.tensor_tensor(uperm[:, m, :].rearrange("p (s c) -> p c s", s=CH),
                                src[:, :].rearrange("p (c s) -> p c s", s=CH),
                                rstd[:, :].rearrange("p (c s) -> p c s", s=CH), ALU.mult).then_inc(out_freed, 1)
            elif t < 8:
                V.tensor_tensor(xpad[:, 3:], src[:, :], rstd[:, :], ALU.mult).then_inc(out_freed, 1)
                dve.wait_ge(out_freed, t + 1)
                if m:
                    dve.wait_ge(xcf_done, m)
                steps.up(V.tensor_scalar(cacc[:, :], xpad[:, 3:], col("mlw", 4 * m + 3), col("mlb", m),
                                         ALU.mult, ALU.add))
                for w in (2, 1, 0):
                    settle()
                    ins = V.scalar_tensor_tensor(out=cacc[:, :], in0=xpad[:, w:w + SEQ],
                                                 scalar=col("mlw", 4 * m + w), in1=cacc[:, :],
                                                 op0=ALU.mult, op1=ALU.add)
                    if w:
                        steps.up(ins)
                ins.then_inc(mconv_done, 1)
                dve.wait_ge(xchi_done, m + 1)
                V.tensor_tensor(xclo[:, m, :], xcf[:, :], xchi[:, m, :].bitcast(f32),
                                ALU.subtract).then_inc(xclo_done, 1)
            elif t < 12:
                if m == 0:
                    dve.wait_ge(u_saved, 16)
                V.tensor_tensor(vT[:, m, :], src[:, :], rstd[:, :], ALU.mult).then_inc(out_freed, 1)
            else:
                V.tensor_tensor(sigo[:, m, :], src[:, :], rstd[:, :], ALU.mult).then_inc(out_freed, 1)
            if t == 5:
                dve.wait_ge(lam_sq, 1)
                V.reciprocal(sm[:, 9, :], sm[:, 9, :]).then_inc(s5_recip, 1)
        steps.up(V.memset(cdiag[:, :, :, :, :], 0.0))
        dve.wait_ge(g_built, 1)
        settle()
        for f in range(2):
            r = slice(STATE * f, STATE * f + STATE)
            V.tensor_copy(cdiag[r, :, :, f, :], bcp[r, 2:4, :].rearrange("p r (j i) -> p r j i", i=GCH)
                          ).then_inc(cdiag_set, 1)
        c_re, c_im = (bcp[:, k, :].rearrange("p (j i) -> p j i", i=GCH) for k in (2, 3))
        T4 = [t[:, k:k + 256].rearrange("p (j i) -> p j i", i=GCH) for t in (cacc, xcf) for k in (0, 256)]

        def read_out(s):
            pw, pv = (q[:, s, :].unsqueeze(2).to_broadcast([P, PAIRS, GCH]) for q in (q_re, q_im))
            for o, a, b in zip(T4, (c_re, c_im, c_im, c_re), (pw, pv, pw, pv)):
                steps.up(V.tensor_tensor(o, a, b, ALU.mult))
            settle()
            steps.up(V.tensor_tensor(fre[:, :, s * GCH:(s + 1) * GCH], T4[0], T4[1], ALU.add))
            steps.up(V.tensor_tensor(fim[:, :, s * GCH:(s + 1) * GCH], T4[2], T4[3], ALU.subtract))
            settle()

        for s in range(3):
            read_out(s)
        for b in range(8):
            dve.wait_ge(qk_ready, b + 1)
            V.tensor_copy((qT if b < 4 else kT)[:, b % 4, :], bank[b % 4][:, :]).then_inc(out_freed, 1)
        split_lo(T_QK + RING)
        for s in range(3, CH):
            read_out(s)
        dve.wait_ge(gates_ready, 1)
        V.tensor_scalar(g8[:, :], bank[4][0:8, :], col("bgate", 0, 8), None, ALU.add).then_inc(gates_copied, 1)
        dve.wait_ge(lnf_done, 1)
        steps.up(V.scalar_tensor_tensor(out=lf[:, :], in0=bank[5][0:HEADS, :], scalar=0.0, in1=lf[:, :],
                                        op0=ALU.min, op1=ALU.subtract))
        settle()
        steps.up(V.tensor_tensor_scan(fcum[:, :], ones[0:HEADS, 0:1].to_broadcast([HEADS, SEQ]), lf[:, :], 0.0,
                                      ALU.mult, ALU.add))
        settle()
        steps.up(V.tensor_tensor(arow[:, :], g8[0:HEADS, :], fcum[:, :], ALU.subtract))
        settle()
        steps.up(V.tensor_tensor_scan(lf[:, :], arow[:, :], arow[:, :], 0.0, ALU.max, ALU.max))
        settle()
        V.tensor_tensor(nmrow[:, 1, :], lf[:, :], fcum[:, :], ALU.add).then_inc(sum_rows, 1)
        V.tensor_scalar(nmrow[:, 0, :], lf[:, :], -1.0, None, ALU.mult).then_inc(rows_done, 1)
        dve.wait_ge(acol_ready, 1)
        V.tensor_copy(acol[:, :, :], bank[4][:, 0:SB * HEADS].rearrange("p (s h) -> p s h", h=HEADS)
                      ).then_inc(acol_copied, 1)
        dve.wait_ge(k_ready, 1)
        V.tensor_copy(ksb[:, :, :], bank[6][:, :].rearrange("p (g i) -> p i g", i=GCH)).then_inc(k_copied, 1)
        skip = cacc[0:GCH, :].rearrange("p (i g) -> p i g", i=GCH)
        steps.up(V.tensor_tensor(skip, ident[0:GCH, 0:GCH].unsqueeze(2).to_broadcast([GCH, GCH, GROUPS]),
                                 cols("ddiag", GCH).unsqueeze(1).to_broadcast([GCH, GCH, GROUPS]), ALU.mult))
        dve.wait_ge(k_copied, 1)
        settle()
        V.tensor_tensor(ksb[0:GCH, :, :], ksb[0:GCH, :, :], skip, ALU.add).then_inc(k_final, 1)

        def weights(k):
            hd, s = k // SB, k % SB
            dve.wait_ge(e_done, k + 1)
            diag = ebuf[:, s, P * s:P * (s + 1)]
            steps.up(V.scalar_tensor_tensor(out=diag, in0=diag, scalar=1.0, in1=tri, op0=ALU.min, op1=ALU.mult))
            settle()
            dve.wait_ge(sc_ready, k + 1)
            if k >= 2:
                dve.wait_ge(w_used, k - 1)
            V.scalar_tensor_tensor(out=wbuf[:, k % 2, 0:SEQ - P * s], in0=bank[4 + k % 2][:, 0:SEQ - P * s],
                                   scalar=float(P) ** -0.5, in1=ebuf[:, s, P * s:],
                                   op0=ALU.mult, op1=ALU.mult).then_inc(w_done, 1)

        def head_gate(hd):
            dve.wait_ge(hsq_done, hd + 1)
            V.tensor_tensor(hb[:, hd % 2, :], bank[NUM_BANK[hd]][:, :], sigo[:, hd, :], ALU.mult).then_inc(num_gated, 1)
            dve.wait_ge(emb_ready, hd + 1)
            dve.wait_ge(dsq_done, hd + 1)
            V.scalar_tensor_tensor(out=dsq[:, hd % 2, :], in0=bank[3][:, :], scalar=DEN_SCALE,
                                   in1=dsq[:, hd % 2, :], op0=ALU.mult, op1=ALU.max).then_inc(floor_done, 1)

        def head_sum(hd):
            dve.wait_ge(hms_ready, hd + 1)
            dve.wait_ge(floor_done, hd + 1)
            V.tensor_tensor(dsq[:, hd % 2, :], dsq[:, hd % 2, :], bank[3][:, :], ALU.add).then_inc(hms_added, 1)

        def head_scale(hd):
            dve.wait_ge(num_gated, hd + 1)
            dve.wait_ge(hfac_done, hd + 1)
            V.tensor_tensor(hb[:, hd % 2, :], hb[:, hd % 2, :], dsq[:, hd % 2, :], ALU.mult).then_inc(o_scaled, 1)

        def head_lo(hd):
            dve.wait_ge(ybhi_done, hd + 1)
            V.tensor_tensor(xlo[:, 4 + hd, :], hb[:, hd % 2, :], xhi[:, 4 + hd, :].bitcast(f32),
                            ALU.subtract).then_inc(yb_done, 1)

        for m in range(HEADS):
            dve.wait_ge(sigo_done, m + 1)
            steps.up(V.tensor_scalar(sigo[:, m, :], sigo[:, m, :], col("mlg", m), None, ALU.mult))
        settle()
        weights(0)
        for hd in range(HEADS):
            weights(SB * hd + 1)
            if hd == 0:
                V.memset(toep[:, :, :, :], 0.0).then_inc(toep_clear, 1)
            weights(SB * hd + 2)
            if hd:
                head_sum(hd - 1)
            weights(SB * hd + 3)
            if hd:
                head_scale(hd - 1)
            if hd == 2:
                dve.wait_ge(scan_done, 1)
                dve.wait_ge(xdiag_zero, 1)
                for half in range(2):
                    for r in range(2):
                        V.tensor_copy(xdiag[half][STATE:P, r, :, 1, :],
                                      xs[STATE:P, r, 8 * half:8 * half + 8, 0:NCH]).then_inc(xdiag_set, 1)
            if hd + 1 < HEADS:
                weights(SB * (hd + 1))
            if hd:
                head_lo(hd - 1)
            head_gate(hd)
        head_sum(HEADS - 1)
        head_scale(HEADS - 1)
        head_lo(HEADS - 1)
        for m in range(4):
            dve.wait_ge(gahi_done, m + 1)
            V.tensor_tensor(xlo[:, m, :], uperm[:, m, :], xhi[:, m, :].bitcast(f32),
                            ALU.subtract).then_inc(galo_done, 1)
        for half in range(2):
            wait_tile_used(dve, T_YB + half)
            split_lo(T_YA + half)

        def gated_lo(m):
            dve.wait_ge(yahi_done, m + 1)
            V.tensor_tensor(xlo[:, m, :], yaf[:, m, :], xhi[:, m, :].bitcast(f32),
                            ALU.subtract).then_inc(ya_done, 1)

        def gated(m):
            dve.wait_ge(glusig_done, m + 1)
            V.tensor_tensor(yaf[:, m, :].rearrange("p (c s) -> p c s", s=CH),
                            uperm[:, m, :].rearrange("p (s c) -> p c s", s=CH),
                            gsig[:, m, :].rearrange("p (s c) -> p c s", s=CH), ALU.mult).then_inc(out_freed, 1)

        for m in range(3):
            gated(m)
        gated_lo(0)
        gated_lo(1)
        gated(3)
        gated_lo(2)
        gated_lo(3)
        split_lo(T_GLU + RING)
        split_lo(T_GLU + 1 + RING)

        def residual(tiles, splits, o0, g, n):
            for m in range(KB):
                wait_tile_used(dve, tiles[m])
                if m < KB - 1 and splits[m]:
                    split_lo(splits[m])
                V.tensor_tensor(h[:, m, :], h[:, m, :], bank[(o0 + m) % 4][:, :], ALU.add).then_inc(out_freed, 1)
            dve.wait_ge(out_freed, o0 + KB)
            operand_lo(h, g, n)
            split_lo(splits[-1])
            row_factor(n)

        def mlp(l):
            t0, d0, fw = T_UP[l], T_DN[l], "fw%d" % l
            V.memset(gpad[:, 0:2], 0.0)
            with dve.Fori(0, FJ // 2) as i:
                steps.enter(i, 4)
                for jj in range(2):
                    j = FJ * l + jj

                    def tap(k):
                        o = COLS[fw][0] + FJ * k + jj
                        return prm[:, bass.ds(i * 2 + o, 1)]

                    wait_tile_used(dve, (t0 + 2 * jj, i, 4))
                    split_lo(t0 + 2 * jj + RING, i, 4)
                    V.tensor_tensor(gpad[:, 2:], bank[(O_UP[l] + 2 * jj) % 4][:, :], rstd[:, :],
                                    ALU.mult).then_inc(out_freed, 1)
                    dve.wait_ge(out_freed, i * 4 + (O_UP[l] + 2 * jj + 1))
                    if j:
                        dve.wait_ge(silu_done, i * 2 + j)
                    steps.up(V.tensor_scalar(cbuf[:, :], gpad[:, 2:], tap(2), tap(3), ALU.mult, ALU.add))
                    settle()
                    steps.up(V.scalar_tensor_tensor(out=cbuf[:, :], in0=gpad[:, 1:1 + SEQ], scalar=tap(1),
                                                    in1=cbuf[:, :], op0=ALU.mult, op1=ALU.add))
                    settle()
                    V.scalar_tensor_tensor(out=cbuf[:, :], in0=gpad[:, 0:SEQ], scalar=tap(0),
                                           in1=cbuf[:, :], op0=ALU.mult, op1=ALU.add).then_inc(conv_done, 1)
                    wait_tile_used(dve, (t0 + 2 * jj + 1, i, 4))
                    split_lo(t0 + 2 * jj + 1 + RING, i, 4)
                    V.tensor_tensor(vbuf[:, :], bank[(O_UP[l] + 2 * jj + 1) % 4][:, :], rstd[:, :],
                                    ALU.mult).then_inc(out_freed, 1)
                    dve.wait_ge(out_freed, i * 4 + (O_UP[l] + 2 * jj + 2))
                    dve.wait_ge(silu_done, i * 2 + (j + 1))
                    V.tensor_tensor(abuf[:, :], vbuf[:, :], sbuf[:, :], ALU.mult).then_inc(a_done, 1)
                    dve.wait_ge(ahi_done, i * 2 + (j + 1))
                    V.tensor_tensor(alo[:, i * 2 + jj, :], abuf[:, :], ahi[:, i * 2 + jj, :].bitcast(f32),
                                    ALU.subtract).then_inc(alo_done, 1)
            steps.leave(FJ // 2)

            def down(i, last):
                for s in range(12):
                    wait_tile_used(dve, (d0 + s, i, 12))
                    if not (last and s >= 8):
                        split_lo(d0 + s + RING, i, 12)
                    if s % 3 == 2:
                        m = s // 3
                        V.tensor_tensor(h[:, i * 4 + m, :], h[:, i * 4 + m, :], bank[(O_DN[l] + m) % 4][:, :],
                                        ALU.add).then_inc(out_freed, 1)
                        if l == 0:
                            o = COLS["g_mix1"][0] + m
                            dve.wait_ge(out_freed, i * 4 + (O_DN[0] + m + 1))
                            dve.wait_ge(xhi_done, i * 4 + (2 * KB + m + 1))
                            V.scalar_tensor_tensor(
                                out=xlo[:, i * 4 + m, :], in0=h[:, i * 4 + m, :],
                                scalar=prm[:, bass.ds(i * 4 + o, 1)], in1=xhi[:, i * 4 + m, :].bitcast(f32),
                                op0=ALU.mult, op1=ALU.subtract).then_inc(xlo_done, 1)

            if l == 0:
                with dve.Fori(0, 2) as i:
                    down(i, False)
            else:
                down(0, False)
                down(1, True)
            dve.wait_ge(out_freed, O_DN[l] + KB)

        dve.wait_ge(x_back, 16)
        residual(OUT_TILES, OUT_SPLITS, O_OUT, "g_ffn0", 1)
        mlp(0)
        row_factor(2)
        V.memset(akd[:, :, 0:WIN], 0.0)
        steps.up(V.memset(avT[:, 0:WIN], 0.0))
        for m in range(NQKV):
            wait_tile_used(dve, T_QKV + m)
            split_lo(T_QKV + m + RING)
            src = bank[(O_QKV + m) % 4]
            if m == 0:
                for f in range(2):
                    r = slice(AHD * f, AHD * f + AHD)
                    ins = V.tensor_tensor(akd[r, f, WIN:], src[r, :], rstd[r, :], ALU.mult)
                    if f == 0:
                        steps.up(ins)
                ins.then_inc(out_freed, 1)
                settle()
                dve.wait_ge(out_freed, O_QKV + 1)
                for f in range(2):
                    r = slice(AHD * f, AHD * f + AHD)
                    ins = V.tensor_scalar(akd[r, f, WIN:], akd[r, f, WIN:], col("bqkv")[r, :], None, ALU.add)
                ins.then_inc(qkv_done, 1)
                continue
            dst = avT[:, WIN:] if m == 1 else aq[:, m - 2, :]
            V.tensor_tensor(dst, src[:, :], rstd[:, :], ALU.mult).then_inc(out_freed, 1)
            dve.wait_ge(out_freed, O_QKV + m + 1)
            V.tensor_scalar(dst, dst, col("bqkv", m), None, ALU.add).then_inc(qkv_done, 1)
        dve.wait_ge(band_in, 16)
        for kv in range(2):
            steps.up(V.tensor_copy(sbuf2[:, kv, :, KW - 1], cols("sink")[:, 4 * kv:4 * kv + 4]))

        def scores(w):
            c, kv = w // 2, w % 2
            s4 = sbuf2[:, w % 2, :, 0:KW - 1]
            nmx = st[:, w % 4, 0, :]
            dve.wait_ge(asc_ready, w + 1)
            if w >= 2:
                dve.wait_ge(aexp_done, w - 1)
            V.scalar_tensor_tensor(
                out=s4, in0=bank[4 + w % 2][:, :].rearrange("p (j k) -> p j k", k=P), scalar=float(AHD) ** -0.5,
                in1=bandsb[:, 4 * kv:4 * kv + 4, :], op0=ALU.mult, op1=ALU.add).then_inc(asc_read, 1)
            dve.wait_ge(asc_read, w + 1)
            if c == 0:
                steps.up(V.memset(s4[:, :, 0:WIN], -1e30))
                settle()
            if w == 0:
                settle()
            steps.up(V.tensor_reduce(nmx, sbuf2[:, w % 2, :, :], AX.X, ALU.max))
            settle()
            V.tensor_scalar(nmx, nmx, -1.0, None, ALU.mult).then_inc(asc_done, 1)

        def invert(w):
            dve.wait_ge(aexp_done, w + 1)
            V.reciprocal(st[:, w % 4, 2, :], st[:, w % 4, 1, :]).then_inc(asum_inv, 1)

        for w in range(2 * NC + 1):
            if w < 2 * NC:
                scores(w)
            if w:
                invert(w - 1)
        for m in range(KB):
            dve.wait_ge(oahi_done, m + 1)
            V.tensor_tensor(xlo[:, m, :], obuf[:, m, :], xhi[:, m, :].bitcast(f32),
                            ALU.subtract).then_inc(oalo_done, 1)
        residual(WO_TILES, WO_SPLITS, O_WO, "g_ffn1", 3)
        mlp(1)
        row_factor(4)
        for m in range(KB):
            V.scalar_tensor_tensor(out=outb[:, m, :], in0=h[:, m, :], scalar=col("g_fin", m), in1=rstd[:, :],
                                   op0=ALU.mult, op1=ALU.mult).then_inc(out_done, 1)

    @block.tensor
    def _(pe):
        MM = nc.tensor.matmul

        def block3(dst, slot, b, rhi, rlo, start, stop):
            wh, wl = whi[:, slot, b * P:(b + 1) * P], wlo[:, slot, b * P:(b + 1) * P]
            MM(dst, wh, rhi, start=start, stop=False)
            MM(dst, wh, rlo, start=False, stop=False)
            return MM(dst, wl, rhi, start=False, stop=stop)

        def product(t, o, i=0, per=0, fresh=None):
            pe.wait_ge(lo_done, i * per + (t + 1))
            if o >= 4:
                pe.wait_ge(out_freed, i * per + (o - 3))
            for b in range(KB):
                if fresh is not None:
                    pe.wait_ge(fresh[0], fresh[1] + b + 1)
                ins = block3(bank[o % 4][:, :], t % RING, b, xhi[:, b, :], xlo[:, b, :], b == 0, b == KB - 1)
            ins.then_inc(tile_used, 1)

        def mean(n):
            pe.wait_ge(acc_done, KB * (n + 1))
            MM(bank[7][:, :], mean_w[:, :], ssum[:, :], start=True, stop=True).then_inc(mean_done, 1)

        def transpose(dst, src, k):
            return nc.tensor.transpose(dst, src, ident[0:k, 0:k])

        pe.wait_ge(params_in, 32)
        pe.wait_ge(consts_set, 1)
        for t in range(16):
            product(t, t, fresh=(xlo_done, 0) if t == 0 else None)
            if t == 2:
                mean(0)
        pe.wait_ge(g_built, 1)
        for b in range(8):
            if b >= 2:
                pe.wait_ge(m1_copied, b - 1)
            for k in range(4):
                ins = transpose(bank[5 + b % 2][:, k * P:(k + 1) * P],
                                (gre if b < 4 else gim)[:, 4 * (b % 4) + k, :], P)
            ins.then_inc(m1_ready, 1)
        pe.wait_ge(m1_copied, 8)
        pe.wait_ge(u_back, 16 * CH)
        pe.wait_ge(rstd_done, 1)
        for r, m1 in enumerate((m1re, m1im)):
            for g in list(range(0, GROUPS, 2)) + list(range(1, GROUPS, 2)):
                p0, j = STATE * (g % 2), g // 2
                ins = MM(bank[4 + 2 * r + j // 8][p0:p0 + STATE, (j % 8) * NCH:(j % 8 + 1) * NCH],
                         m1[:, j, p0:p0 + STATE], uc[:, g, :], start=True, stop=True)
            ins.then_inc(s5in_ready, 1)
        pe.wait_ge(lo_done, T_QK + 1)
        pe.wait_ge(xclo_done, HEADS)
        for b in range(8):
            pe.wait_ge(out_freed, O_QK + b - 3)
            block3(bank[b % 4][:, :], T_QK % RING, b, xchi[:, b % 4, :], xclo[:, b % 4, :], True,
                   True).then_inc(qk_ready, 1)
        pe.wait_ge(s5in_copied, 2)
        for hd in range(HEADS):
            if hd >= 2:
                pe.wait_ge(vtok_copied, hd - 1)
            for s in range(SB):
                ins = transpose(bank[6 + hd % 2][:, s * P:(s + 1) * P], vT[:, hd, s * P:(s + 1) * P], P)
            ins.then_inc(vtok_ready, 1)
        pe.wait_ge(out_freed, O_QK + 8)
        for k in range(12):
            ins = MM(bank[4][0:8, :], cols("wg")[:, 8 * k:8 * k + 8], (qT, kT, vT)[k % 3][:, k // 3, :],
                     start=k == 0, stop=k == 11)
        ins.then_inc(gates_ready, 1)
        pe.wait_ge(gates_copied, 1)
        MM(bank[5][0:HEADS, :], ident[0:8, HEADS:8], g8[:, :], start=True, stop=True).then_inc(fsel_ready, 1)
        pe.wait_ge(vtok_copied, HEADS)
        pe.wait_ge(cdiag_set, 2)
        for j in range(PAIRS):
            dst = bank[6][:, 2 * j * GCH:2 * (j + 1) * GCH]
            for r, g in enumerate((gre, gim)):
                ins = MM(dst, g[:, j, :], cdiag[:, r, j, :, :].rearrange("p f i -> p (f i)"),
                         start=r == 0, stop=r == 1)
        ins.then_inc(k_ready, 1)
        pe.wait_ge(rows_done, 1)
        for s in range(SB):
            ins = transpose(bank[4][:, s * HEADS:(s + 1) * HEADS], arow[:, s * P:(s + 1) * P], HEADS)
        ins.then_inc(acol_ready, 1)

        def broadcast_row(hd, row):
            pick = ident[0:HEADS, hd:hd + 1].to_broadcast([HEADS, P])
            if row == 0:
                pe.wait_ge(e_done, SB * hd) if hd else None
            else:
                pe.wait_ge(hms_added, hd) if hd else None
            MM(bank[2 + row][:, :], pick, nmrow[:, row, :], start=True, stop=True).then_inc(
                (nmb_ready, emb_ready)[row], 1)

        def head_scores(k):
            hd, s = k // SB, k % SB
            if k >= 2:
                pe.wait_ge(w_done, k - 1)
            MM(bank[4 + k % 2][:, 0:SEQ - P * s], kT[:, hd, s * P:(s + 1) * P], qT[:, hd, s * P:],
               start=True, stop=True).then_inc(sc_ready, 1)

        def mean_square(hd):
            pe.wait_ge(hsq_done, hd + 1)
            pe.wait_ge(floor_done, hd + 1)
            MM(bank[3][:, :], mean_w[:, :], hsq[:, :], start=True, stop=True).then_inc(hms_ready, 1)

        def s5_output(q):
            pe.wait_ge(toep_built, 16 * CH)
            if q >= 2:
                pe.wait_ge(y_copied, q - 1)
            for g in range(8 * q, 8 * q + 8):
                MM(bank[q % 2][:, (g % 8) * NCH:(g % 8 + 1) * NCH], toep[:, :, :, g].rearrange("p s i -> p (s i)"),
                   uc[:, g, :], start=g == 8 * q, stop=False)
            pe.wait_ge(xdiag_set, 8)
            for j in range(4 * q, 4 * q + 4):
                for r, f in enumerate((fre, fim)):
                    ins = MM(bank[q % 2][:, (j % 4) * 2 * NCH:(j % 4 + 1) * 2 * NCH], f[:, j, :],
                             xdiag[q // 2][:, r, j % 8, :, :].rearrange("p f c -> p (f c)"),
                             start=False, stop=j == 4 * q + 3 and r == 1)
            ins.then_inc(y_ready, 1)

        broadcast_row(0, 0)
        pe.wait_ge(k_copied, 1)
        head_scores(0)
        head_scores(1)
        pe.wait_ge(emrow_done, 1)
        for hd in range(HEADS):
            for s in range(SB):
                k = SB * hd + s
                before = (0, 0, 1, 3)[hd]
                if s == 0 and before:
                    pe.wait_ge(num_gated, before)
                    pe.wait_ge(dsq_done, before)
                pe.wait_ge(w_done, k + 1)
                w = wbuf[:, k % 2, 0:SEQ - P * s]
                MM(bank[NUM_BANK[hd]][:, P * s:], vtok[:, hd, s, :], w, start=s == 0, stop=s == SB - 1)
                MM(bank[NUM_BANK[hd] + 1][:, P * s:], ones[:, :], w, start=s == 0, stop=s == SB - 1).then_inc(w_used, 1)
                if k + 2 < SB * HEADS:
                    head_scores(k + 2)
                if s == 0 and hd:
                    mean_square(hd - 1)
                if s == 2:
                    if hd + 1 < HEADS:
                        broadcast_row(hd + 1, 0)
                    broadcast_row(hd, 1)
            for q in Y_AFTER[hd]:
                s5_output(q)
                if q == 2:
                    mean_square(HEADS - 1)
        pe.wait_ge(y_copied, 4)
        pe.wait_ge(e_done, SB * HEADS)
        pe.wait_ge(hms_added, HEADS)
        pe.wait_ge(lo_done, T_YB + 2)
        for b in range(4, KB):
            pe.wait_ge(yb_done, b - 3)
            for m in range(4):
                ins = block3(bank[m][:, :], (T_YB + m // 2) % RING, 4 * (m % 2) + b - 4, xhi[:, b, :],
                             xlo[:, b, :], b == 4, False)
                if b == KB - 1 and m % 2:
                    ins.then_inc(tile_used, 1)
        pe.wait_ge(lo_done, T_GLU + 2)
        for half in range(2):
            pe.wait_ge(galo_done, 2 * (half + 1))
            for m in range(4):
                for b in (2 * half, 2 * half + 1):
                    ins = block3(bank[4 + m][:, :], (T_GLU + m // 2) % RING, 4 * (m % 2) + b, xhi[:, b, :],
                                 xlo[:, b, :], b == 0, b == 3)
                if half:
                    ins.then_inc(glu_ready, 1)
        for m in range(4):
            t = T_YA + m // 2
            pe.wait_ge(lo_done, t + 1)
            for b in range(4):
                if m == 0:
                    pe.wait_ge(ya_done, b + 1)
                ins = block3(bank[m][:, :], t % RING, 4 * (m % 2) + b, xhi[:, b, :], xlo[:, b, :], False, b == 3)
            if m % 2:
                ins.then_inc(tile_used, 1)
        for m in range(4):
            product(T_OUT + m, O_OUT + 4 + m)

        def mlp(l):
            for s in range(4):
                product(T_UP[l] + s, O_UP[l] + s, fresh=(xlo_done, KB * (1 + 2 * l)) if s == 0 else None)
                if s == 0:
                    mean(1 + 2 * l)
            with pe.Fori(1, FJ // 2) as i:
                for s in range(4):
                    product(T_UP[l] + s, O_UP[l] + s, i, 4)
            with pe.Fori(0, 2) as i:
                for m in range(4):
                    pe.wait_ge(out_freed, i * 4 + (O_DN[l] + m - 3))
                    for part in range(3):
                        t = T_DN[l] + 3 * m + part
                        pe.wait_ge(lo_done, i * 12 + (t + 1))
                        ks = (range(0, 8), range(8, 15), range(15, FJ))[part]
                        for k in ks:
                            if k == 0 or k == FJ - 2:
                                pe.wait_ge(alo_done, FJ * (l + 1) - (2 if k == 0 else 0))
                            ins = block3(bank[(O_DN[l] + m) % 4][:, :], t % RING, k - ks[0], ahi[:, k, :],
                                         alo[:, k, :], k == 0, k == FJ - 1)
                        ins.then_inc(tile_used, 1)

        mlp(0)
        for m in range(NQKV):
            product(T_QKV + m, O_QKV + m, fresh=(xlo_done, 2 * KB) if m == 0 else None)
            if m == 0:
                mean(2)
        pe.wait_ge(qkv_done, 2)
        for b in range(2):
            for k in range(4):
                c = 4 * b + k
                ins = transpose(bank[4 + b][:, k * P:(k + 1) * P], avT[:, c * WIN:c * WIN + P], P)
            ins.then_inc(vwin_ready, 1)
        pe.wait_ge(vwin_copied, 2)
        for w in range(2 * NC + 3):
            if w < 2 * NC:
                c, kv = w // 2, w % 2
                if w < 2:
                    pe.wait_ge(qkv_done, 2 + 4 * (w + 1))
                    pe.wait_ge(kdup_in, 32)
                else:
                    pe.wait_ge(asc_read, w - 1)
                for hf in range(2):
                    for j in range(4):
                        r = slice(AHD * hf, AHD * hf + AHD)
                        ins = MM(bank[4 + w % 2][r, j * P:(j + 1) * P],
                                 aq[r, 4 * kv + j, WIN * c:WIN * (c + 1)], akd[r, kv, WIN * c:WIN * c + P],
                                 start=True, stop=True)
                ins.then_inc(asc_ready, 1)
            if 2 <= w <= 2 * NC + 1:
                v = w - 2
                pe.wait_ge(anorm_done, v + 1)
                if v >= 2:
                    pe.wait_ge(apt_copied, v - 1)
                for j in range(4):
                    ins = transpose(bank[(6, 0)[v % 2]][:, j * P:(j + 1) * P], pbuf[:, v % 4, j, 0:P], P)
                ins.then_inc(apt_ready, 1)
            if w >= 3:
                v = w - 3
                c, kv = v // 2, v % 2
                pe.wait_ge(apt_copied, v + 1)
                if v >= 2:
                    pe.wait_ge(ao_copied, v - 1)
                p4 = ptb[:, v % 2, :].rearrange("p (j f q) -> p j f q", f=2, q=WIN)
                for hf in range(2):
                    ins = MM(bank[(7, 1)[v % 2]][AHD * hf:AHD * hf + AHD, 0:4 * WIN],
                             vwin[:, c, AHD * kv:AHD * kv + AHD], p4[:, :, hf, :], start=True, stop=True)
                ins.then_inc(ao_ready, 1)
        for m in range(KB):
            product(T_WO + m, O_WO + m, fresh=(oalo_done, 0) if m == 0 else None)
        mlp(1)
        mean(4)

    ctx.close()


def _tile(w):
    k = w.shape[0] // P
    return w.reshape(k, P, P).transpose(1, 0, 2).reshape(P, k * P)


def _tiles(w):
    return [_tile(w[:, c:c + P]) for c in range(0, w.shape[1], P)]


def _columns(v):
    return v.reshape(-1, P).T


def _bucket():
    rel = (np.arange(2 * WIN)[None, :] - WIN) - np.arange(WIN)[:, None]
    n = np.abs(rel)
    scaled = np.log(np.maximum(n, 1) / 8) / np.log(128 / 8) * 8
    large = np.minimum(8 + scaled.astype(np.int32), 15)
    return (rel > 0).astype(np.int32) * 16 + np.where(n < 8, n, large)


def kernel(**inputs):
    import concourse.bacc as bacc
    from concourse.bass_utils import run_bass_kernel_spmd

    a = {k: np.asarray(v) for k, v in inputs.items()}
    f32 = np.float32
    stream = _tiles(a["ab_w_in"][0])
    blocks = [a["ml_w_q"][0][h] for h in range(HEADS)] + [a["ml_w_k"][0][h] for h in range(HEADS)]
    stream.append(np.concatenate(blocks, axis=1))
    glu = _tiles(a["s5_w_glu"][0])
    out = _tiles(a["ab_w_out"][0])
    half = 4 * P
    stream += [np.concatenate([w[:, half:] for w in out[2 * k:2 * k + 2]], axis=1) for k in range(2)]
    stream += [np.concatenate(glu[2 * k:2 * k + 2], axis=1) for k in range(2)]
    stream += [np.concatenate([w[:, :half] for w in out[2 * k:2 * k + 2]], axis=1) for k in range(2)]
    stream += out[4:]

    def mlp(l):
        up = _tiles(a["ffn_w_up"][l])
        out = []
        for j in range(FJ):
            out += [up[j], up[FJ + j]]
        for w in _tiles(a["ffn_w_down"][l]):
            for k0, k1 in ((0, 8), (8, 15), (15, FJ)):
                part = w[:, k0 * P:k1 * P]
                out.append(np.concatenate([part, np.zeros((P, (8 - k1 + k0) * P), f32)], axis=1))
        return out

    stream += mlp(0)
    wqkv = a["swa_w_qkv"][0]
    bqkv = a["swa_b_qkv"][0]
    nq = QH * AHD
    order = np.concatenate([np.arange(nq, nq + 4 * AHD), np.arange(nq)])
    stream += _tiles(wqkv[:, order])
    stream += _tiles(a["swa_w_o"][0])
    stream += mlp(1)
    assert len(stream) == T_END
    wstream = np.ascontiguousarray(np.stack(stream))

    def pairs(v):
        v = v.reshape((PAIRS, P) + v.shape[2:])
        return np.moveaxis(v, 0, 1)

    prm = np.zeros((P, NCOL), f32)

    def put(name, v):
        o, n = COLS[name]
        assert v.shape[1] == n, name
        prm[:v.shape[0], o:o + n] = v

    put("g_mix0", _columns(a["norm_mix_g"][0]))
    put("g_mix1", _columns(a["norm_mix_g"][1]))
    put("g_ffn0", _columns(a["norm_ffn_g"][0]))
    put("g_ffn1", _columns(a["norm_ffn_g"][1]))
    put("g_fin", _columns(a["norm_final_g"]))
    for l in range(2):
        put("fw%d" % l, np.concatenate([_columns(a["ffn_conv_w"][l][k]) for k in range(3)]
                                       + [_columns(a["ffn_conv_b"][l])], axis=1))
    put("mlw", np.stack([_columns(a["ml_conv_w"][0][k]) for k in range(4)], axis=2).reshape(P, 4 * HEADS))
    put("mlb", _columns(a["ml_conv_b"][0]))
    put("mlg", _columns(a["ml_norm_g"][0]))
    put("bqkv", _columns(bqkv[order]))
    put("sink", np.repeat(a["swa_sinks"][0].reshape(QH // 2, 2).T, WIN, axis=0))
    put("bgate", a["ml_b_gates"][0].reshape(8, 1))
    put("ddiag", a["s5_d"][0].reshape(GROUPS, GCH).T)
    put("ldt", pairs(np.repeat(a["s5_log_dt"][0][:, None], STATE, axis=1)))
    put("are", pairs(a["s5_a_re"][0]))
    put("aim", pairs(a["s5_a_im"][0]))
    put("wg", a["ml_w_gates"][0].reshape(12, P, 8).transpose(1, 0, 2).reshape(P, 96))
    bc = np.stack([pairs(a["s5_b_re"][0]), pairs(a["s5_b_im"][0]),
                   pairs(a["s5_c_re"][0].transpose(0, 2, 1)), pairs(a["s5_c_im"][0].transpose(0, 2, 1))], axis=1)
    bc = np.ascontiguousarray(bc.reshape(P, 4, PAIRS * GCH))
    consts = np.stack([np.eye(P, dtype=f32), np.triu(np.ones((P, P), f32))], axis=1)
    band = a["rel_bias"][_bucket()]
    band = band.transpose(2, 0, 1).reshape(QH // 2, 2 * WIN, 2 * WIN).transpose(1, 0, 2)
    xT = a["x"][0].T.reshape(KB, P, SEQ).transpose(1, 0, 2)

    nc = bacc.Bacc("TRN2", target_bir_lowering=False, num_devices=1)
    dt = mybir.dt.float32
    arrays = {"wstream": wstream, "xT": xT, "params": prm, "bc": bc, "consts": consts, "band": band}
    arrays = {k: np.ascontiguousarray(v) for k, v in arrays.items()}
    aps = {k: nc.dram_tensor(k, v.shape, dt, kind="ExternalInput").ap() for k, v in arrays.items()}
    outT = nc.dram_tensor("outT", (P, KB, SEQ), dt, kind="ExternalOutput").ap()
    u_scratch = nc.dram_tensor("u_scratch", (4, P, CH, NCH), dt, kind="Internal").ap()
    y_scratch = nc.dram_tensor("y_scratch", (GROUPS, GCH, CH, NCH), dt, kind="Internal").ap()
    build(nc, **aps, outT=outT, u_scratch=u_scratch, y_scratch=y_scratch)
    r = run_bass_kernel_spmd(nc, [arrays], core_ids=[0])
    out = r.results[0]["outT"]
    return np.ascontiguousarray(out.transpose(2, 1, 0).reshape(1, SEQ, DM))
```
